# Optimizing a Trainium2 kernel written in Bass

```python
import math, functools
import jax, jax.numpy as jnp
from jax import lax
import numpy as np

D_MODEL = 1024
BATCH = 1
SEQ = 1024
DEPTH = 1
DEC_BATCH = 8
DEC_SEQ = 1
PAST_LEN = 256
PAGE_SIZE = 128

N_HEADS = 8
HEAD_DIM = 64
V_DIM = 2 * HEAD_DIM
QK_WIDTH = N_HEADS * 2 * HEAD_DIM
ATTN_WIDTH = N_HEADS * V_DIM
ROPE_THETA = 10000.0
Q_BLOCK = 128
POOL_WINDOWS = (2, 4, 8, 16)
POOL_GROUPS = len(POOL_WINDOWS)
POOL_GROUP_DIM = 128
POOL_WIDTH = POOL_GROUPS * POOL_GROUP_DIM
POOL_OUT_DIM = D_MODEL // POOL_GROUPS
POOL_BUF = max(POOL_WINDOWS) - 1
N_BRANCHES = 2
IN_COLS = 2 * QK_WIDTH + ATTN_WIDTH + POOL_WIDTH + N_BRANCHES * D_MODEL
N_GROUPS = 4
EXPERTS_PER_GROUP = 4
N_EXPERTS = N_GROUPS * EXPERTS_PER_GROUP
TOP_K_IN_GROUP = 2
EXPERT_FF = D_MODEL // 4
LN_EPS = 1e-5
SUBLN_EPS = 1e-5
N_MOD = 6

kernel_name = "hybrid_pool_diffattn_hmoe_decode_step"

def layer_norm(x, g, b):
    xf = x.astype(jnp.float32)
    mu = jnp.mean(xf, axis=-1, keepdims=True)
    var = jnp.mean(jnp.square(xf - mu), axis=-1, keepdims=True)
    return ((xf - mu) * lax.rsqrt(var + LN_EPS) * g.astype(jnp.float32) + b.astype(jnp.float32)).astype(x.dtype)

def head_rmsnorm(o, g):
    of = o.astype(jnp.float32)
    y = of * lax.rsqrt(jnp.mean(jnp.square(of), axis=-1, keepdims=True) + SUBLN_EPS) * g.astype(jnp.float32)
    return y.astype(o.dtype)

def rope(x, pos):
    half = HEAD_DIM // 2
    inv = ROPE_THETA ** (-jnp.arange(half, dtype=jnp.float32) / half)
    ang = pos.astype(jnp.float32)[:, None] * inv[None, :]
    cos = jnp.cos(ang)[:, None, None, :]
    sin = jnp.sin(ang)[:, None, None, :]
    xf = x.astype(jnp.float32)
    x1, x2 = xf[..., :half], xf[..., half:]
    return jnp.concatenate([x1 * cos - x2 * sin, x2 * cos + x1 * sin], axis=-1).astype(x.dtype)

def diff_weights(scores, lam):
    p = jax.nn.softmax(scores, axis=-1)
    return p[:, :, 0] - lam * p[:, :, 1]

def attend_prompt(q, k, v, lam):
    b, s = q.shape[0], q.shape[1]
    nb = s // Q_BLOCK
    qb = q.reshape(b, nb, Q_BLOCK, N_HEADS, 2, HEAD_DIM).transpose(1, 0, 2, 3, 4, 5)
    k_pos = jnp.arange(s)
    scale = HEAD_DIM ** -0.5

    def one_block(args):
        i, q_i = args
        sc = jnp.einsum('bqhmd,bkhmd->bhmqk', q_i, k, preferred_element_type=jnp.float32) * scale
        q_pos = i * Q_BLOCK + jnp.arange(Q_BLOCK)
        mask = k_pos[None, :] <= q_pos[:, None]
        sc = jnp.where(mask, sc, -jnp.inf)
        w = diff_weights(sc, lam)
        return jnp.einsum('bhqk,bkhv->bqhv', w.astype(v.dtype), v)

    out = lax.map(one_block, (jnp.arange(nb), qb))
    return out.transpose(1, 0, 2, 3, 4).reshape(b, s, N_HEADS, V_DIM)

def attend_sample(q, k_new, v_new, lam, k_past, v_past):
    s1 = q.shape[1]
    p = k_past.shape[1]
    scale = HEAD_DIM ** -0.5
    sc_past = jnp.einsum('bqhmd,bkhmd->bhmqk', q, k_past, preferred_element_type=jnp.float32) * scale
    sc_new = jnp.einsum('bqhmd,bkhmd->bhmqk', q, k_new, preferred_element_type=jnp.float32) * scale
    causal = jnp.arange(s1)[None, :] <= jnp.arange(s1)[:, None]
    sc_new = jnp.where(causal, sc_new, -jnp.inf)
    w = diff_weights(jnp.concatenate([sc_past, sc_new], axis=-1), lam).astype(v_new.dtype)
    return (jnp.einsum('bhqk,bkhv->bqhv', w[..., :p], v_past)
            + jnp.einsum('bhqk,bkhv->bqhv', w[..., p:], v_new))

def pool_mixer(u_buf, u_new, start_pos, w_pool, pool_scale):
    bt, s = u_new.shape[0], u_new.shape[1]
    u_ext = jnp.concatenate([u_buf, u_new], axis=1)
    uf = u_ext.astype(jnp.float32)
    cs = jnp.concatenate([jnp.zeros((bt, 1, POOL_WIDTH), jnp.float32), jnp.cumsum(uf, axis=1)], axis=1)
    pos = start_pos + jnp.arange(s)
    outs = []
    for g, win in enumerate(POOL_WINDOWS):
        sl = slice(g * POOL_GROUP_DIM, (g + 1) * POOL_GROUP_DIM)
        top = cs[:, POOL_BUF + 1:POOL_BUF + 1 + s, sl]
        bot = cs[:, POOL_BUF + 1 - win:POOL_BUF + 1 - win + s, sl]
        cnt = jnp.minimum(win, pos + 1).astype(jnp.float32)[None, :, None]
        outs.append((top - bot) / cnt - uf[:, POOL_BUF:, sl])
    pooled = jnp.concatenate(outs, axis=-1).reshape(bt, s, POOL_GROUPS, POOL_GROUP_DIM).astype(u_new.dtype)
    mixed = jnp.einsum('bsgc,gcd->bsgd', pooled, w_pool).reshape(bt, s, D_MODEL) * pool_scale
    return mixed, u_ext[:, -POOL_BUF:]

def hier_moe(h, w_group, b_group, w_router, b_router, w_e_gate, w_e_up, w_e_down):
    bt, s, d = h.shape
    t = h.reshape(bt * s, d)
    n_tok = t.shape[0]
    g_logits = (t @ w_group + b_group).astype(jnp.float32)
    g_prob = jax.nn.softmax(g_logits, axis=-1)
    g_idx = jnp.argmax(g_logits, axis=-1)
    p_g = jnp.take_along_axis(g_prob, g_idx[:, None], axis=-1)
    e_logits = (t @ w_router + b_router).astype(jnp.float32).reshape(n_tok, N_GROUPS, EXPERTS_PER_GROUP)
    e_sel = jnp.take_along_axis(e_logits, g_idx[:, None, None], axis=1)[:, 0]
    top_v, top_i = lax.top_k(e_sel, TOP_K_IN_GROUP)
    top_w = jax.nn.softmax(top_v, axis=-1) * p_g
    within = jnp.sum(jax.nn.one_hot(top_i, EXPERTS_PER_GROUP, dtype=jnp.float32) * top_w[..., None], axis=1)
    combine = (jax.nn.one_hot(g_idx, N_GROUPS, dtype=jnp.float32)[:, :, None] * within[:, None, :])
    combine = combine.reshape(n_tok, N_EXPERTS).astype(h.dtype)
    hg = jnp.einsum('td,edf->tef', t, w_e_gate)
    hu = jnp.einsum('td,edf->tef', t, w_e_up)
    act = jax.nn.silu(hg) * hu * combine[:, :, None]
    return jnp.einsum('tef,efd->td', act, w_e_down).reshape(bt, s, d)

def decoder_layer(x, c, start_pos, attend, pool_buf, lam_init, alpha,
                  w_ada, b_ada, w_in, lambda_q1, lambda_k1, lambda_q2, lambda_k2, subln_g,
                  w_pool, pool_scale, w_out, ln1_g, ln1_b,
                  w_group, b_group, w_router, b_router, w_e_gate, w_e_up, w_e_down, ln2_g, ln2_b):
    bt, s = x.shape[0], x.shape[1]
    mod = (jax.nn.silu(c) @ w_ada + b_ada)[:, None, :]
    sh1, sc1, g1, sh2, sc2, g2 = jnp.split(mod, N_MOD, axis=-1)
    h = x * (1 + sc1) + sh1
    proj = h @ w_in
    q, k, v, u, gates = jnp.split(
        proj, [QK_WIDTH, 2 * QK_WIDTH, 2 * QK_WIDTH + ATTN_WIDTH, 2 * QK_WIDTH + ATTN_WIDTH + POOL_WIDTH], axis=-1)
    pos = start_pos + jnp.arange(s)
    q = rope(q.reshape(bt, s, N_HEADS, 2, HEAD_DIM), pos)
    k = rope(k.reshape(bt, s, N_HEADS, 2, HEAD_DIM), pos)
    v = v.reshape(bt, s, N_HEADS, V_DIM)
    lam = (jnp.exp(jnp.sum(lambda_q1.astype(jnp.float32) * lambda_k1.astype(jnp.float32)))
           - jnp.exp(jnp.sum(lambda_q2.astype(jnp.float32) * lambda_k2.astype(jnp.float32))) + lam_init)
    o = attend(q, k, v, lam)
    attn_out = (head_rmsnorm(o, subln_g) * (1.0 - lam_init)).reshape(bt, s, ATTN_WIDTH)
    pool_out, new_pool = pool_mixer(pool_buf, u, start_pos, w_pool, pool_scale)
    g_pool, g_attn = jnp.split(jax.nn.sigmoid(gates), N_BRANCHES, axis=-1)
    merged = g_pool * pool_out + g_attn * attn_out
    x = layer_norm(alpha * x + (1 + g1) * (merged @ w_out), ln1_g, ln1_b)
    h2 = x * (1 + sc2) + sh2
    x = layer_norm(alpha * x + (1 + g2) * hier_moe(h2, w_group, b_group, w_router, b_router,
                                                     w_e_gate, w_e_up, w_e_down), ln2_g, ln2_b)
    return x, k, v, new_pool

def setup_inputs(seed: int = 0) -> dict:
    key = jax.random.key(seed)
    ks = jax.random.split(key, 32)
    n_pages = PAST_LEN // PAGE_SIZE
    n_used = DEC_BATCH * n_pages
    n_phys = (n_used * 5) // 4
    beta = (8.0 * DEPTH) ** -0.25
    f32 = jnp.float32
    nrm = lambda k, shp, s: jax.random.normal(k, shp, f32) * s
    page_table = jax.random.permutation(ks[0], n_phys)[:n_used].reshape(DEC_BATCH, n_pages).astype(jnp.int32)
    return {
        "x_prompt": nrm(ks[1], (BATCH, SEQ, D_MODEL), 1.0),
        "x_sample": nrm(ks[2], (DEC_BATCH, DEC_SEQ, D_MODEL), 1.0),
        "cache_k": nrm(ks[3], (DEPTH, n_phys, PAGE_SIZE, N_HEADS, 2, HEAD_DIM), 1.0),
        "cache_v": nrm(ks[4], (DEPTH, n_phys, PAGE_SIZE, N_HEADS, V_DIM), 1.0),
        "state_pool": nrm(ks[5], (DEPTH, DEC_BATCH, POOL_BUF, POOL_WIDTH), 1.0),
        "page_table": page_table,
        "c_prompt": nrm(ks[6], (BATCH, D_MODEL), 1.0),
        "c_sample": nrm(ks[7], (DEC_BATCH, D_MODEL), 1.0),
        "w_ada": nrm(ks[8], (DEPTH, D_MODEL, N_MOD * D_MODEL), 0.25 * D_MODEL ** -0.5),
        "b_ada": nrm(ks[9], (DEPTH, N_MOD * D_MODEL), 0.01),
        "w_in": nrm(ks[10], (DEPTH, D_MODEL, IN_COLS), D_MODEL ** -0.5),
        "lambda_q1": nrm(ks[11], (DEPTH, HEAD_DIM), 0.1),
        "lambda_k1": nrm(ks[12], (DEPTH, HEAD_DIM), 0.1),
        "lambda_q2": nrm(ks[13], (DEPTH, HEAD_DIM), 0.1),
        "lambda_k2": nrm(ks[14], (DEPTH, HEAD_DIM), 0.1),
        "subln_g": 1.0 + nrm(ks[15], (DEPTH, V_DIM), 0.01),
        "w_pool": nrm(ks[16], (DEPTH, POOL_GROUPS, POOL_GROUP_DIM, POOL_OUT_DIM), POOL_GROUP_DIM ** -0.5),
        "pool_scale": 1.0 + nrm(ks[17], (DEPTH, D_MODEL), 0.01),
        "w_out": nrm(ks[18], (DEPTH, D_MODEL, D_MODEL), beta * D_MODEL ** -0.5),
        "ln1_g": 1.0 + nrm(ks[19], (DEPTH, D_MODEL), 0.01),
        "ln1_b": nrm(ks[20], (DEPTH, D_MODEL), 0.01),
        "w_group": nrm(ks[21], (DEPTH, D_MODEL, N_GROUPS), D_MODEL ** -0.5),
        "b_group": nrm(ks[22], (DEPTH, N_GROUPS), 0.01),
        "w_router": nrm(ks[23], (DEPTH, D_MODEL, N_EXPERTS), D_MODEL ** -0.5),
        "b_router": nrm(ks[24], (DEPTH, N_EXPERTS), 0.01),
        "w_e_gate": nrm(ks[25], (DEPTH, N_EXPERTS, D_MODEL, EXPERT_FF), D_MODEL ** -0.5),
        "w_e_up": nrm(ks[26], (DEPTH, N_EXPERTS, D_MODEL, EXPERT_FF), D_MODEL ** -0.5),
        "w_e_down": nrm(ks[27], (DEPTH, N_EXPERTS, EXPERT_FF, D_MODEL), beta * EXPERT_FF ** -0.5),
        "ln2_g": 1.0 + nrm(ks[28], (DEPTH, D_MODEL), 0.01),
        "ln2_b": nrm(ks[29], (DEPTH, D_MODEL), 0.01),
    }

def reference(x_prompt, x_sample, cache_k, cache_v, state_pool, page_table, c_prompt, c_sample,
              w_ada, b_ada, w_in, lambda_q1, lambda_k1, lambda_q2, lambda_k2, subln_g,
              w_pool, pool_scale, w_out, ln1_g, ln1_b,
              w_group, b_group, w_router, b_router, w_e_gate, w_e_up, w_e_down, ln2_g, ln2_b):
    alpha = (2.0 * DEPTH) ** 0.25
    db = x_sample.shape[0]
    past_len = page_table.shape[1] * PAGE_SIZE
    xp, xs = x_prompt, x_sample
    kp_rows, vp_rows, pool_p, ks_rows, vs_rows, pool_s = [], [], [], [], [], []
    for l in range(DEPTH):
        lam_init = 0.8 - 0.6 * math.exp(-0.3 * l)
        weights = (w_ada[l], b_ada[l], w_in[l], lambda_q1[l], lambda_k1[l], lambda_q2[l], lambda_k2[l], subln_g[l],
                   w_pool[l], pool_scale[l], w_out[l], ln1_g[l], ln1_b[l],
                   w_group[l], b_group[l], w_router[l], b_router[l], w_e_gate[l], w_e_up[l], w_e_down[l],
                   ln2_g[l], ln2_b[l])
        zero_buf = jnp.zeros((xp.shape[0], POOL_BUF, POOL_WIDTH), xp.dtype)
        xp, kp, vp, pp = decoder_layer(xp, c_prompt, 0, attend_prompt, zero_buf, lam_init, alpha, *weights)
        k_past = cache_k[l][page_table].reshape(db, past_len, N_HEADS, 2, HEAD_DIM)
        v_past = cache_v[l][page_table].reshape(db, past_len, N_HEADS, V_DIM)
        attend_s = functools.partial(attend_sample, k_past=k_past, v_past=v_past)
        xs, kn, vn, ps = decoder_layer(xs, c_sample, past_len, attend_s, state_pool[l], lam_init, alpha, *weights)
        kp_rows.append(kp); vp_rows.append(vp); pool_p.append(pp)
        ks_rows.append(kn); vs_rows.append(vn); pool_s.append(ps)
    return (xp, xs, jnp.stack(kp_rows), jnp.stack(vp_rows), jnp.stack(pool_p),
            jnp.stack(ks_rows), jnp.stack(vs_rows), jnp.stack(pool_s))


_drawn_inputs = setup_inputs


def setup_inputs(seed=0):
    import zlib

    import numpy as np

    out = dict(_drawn_inputs(seed))
    spreads = {}
    factors = {'b_ada': 3.198,
     'lambda_k1': 4.429,
     'lambda_q2': 4.554,
     'lambda_k2': 5.681,
     'subln_g': 49.837,
     'pool_scale': 41.386,
     'ln1_b': 4.178,
     'b_group': 5.252,
     'b_router': 22.522,
     'ln2_g': 29.679,
     'ln2_b': 32.011,
     'ln1_g': 3.95}
    for name, (base, spread) in spreads.items():
        noise = np.random.default_rng([zlib.crc32(name.encode()), seed]).standard_normal(out[name].shape)
        drawn = base * np.exp(spread * noise) if base else spread * noise
        out[name] = __import__('jax').numpy.asarray(drawn.astype(out[name].dtype))
    for name, factor in factors.items():
        out[name] = (out[name] * factor).astype(out[name].dtype)
    return out
```

```python
from contextlib import ExitStack

import numpy as np

import concourse.bass as bass
from concourse import mybir

F32 = mybir.dt.float32
F32R = mybir.dt.float32r
BF16 = mybir.dt.bfloat16
I32 = mybir.dt.int32
U32 = mybir.dt.uint32
ALU = mybir.AluOpType
ACT = mybir.ActivationFunctionType
AX = mybir.AxisListType

P = 128
D = 1024
KC = D // P
SEQ = 1024
NS = 8
T = SEQ + NS
PIECE = T // 3
NT = SEQ // P
H = 8
HD = 64
SCALE = HD ** -0.5
PAGES = 2
PAST = PAGES * P
N_PHYS = 20
WIN = (2, 4, 8, 16)
BUF = 15
NG = 4
EPG = 4
NE = NG * EPG
FF = 256
ALPHA = 2.0 ** 0.25
LAM_INIT = 0.2
EPS = 1e-5
NMOD = 6
SLOT_TILES = (2 * T + NE * (P - 1)) // P
SLOTS = SLOT_TILES * P
QC, KCOL, VC, UC, GPC, GAC = 0, 1024, 2048, 3072, 3584, 4608
BIG = 3.0e38

CONST_COLS = {}
_at = 0
for _n, _w in (("ident", 128), ("mask", 128), ("tri", 128), ("half", 2), ("delta", 64), ("coef_a", 1), ("coef_b", 1),
               ("corr", 64), ("sel", 8), ("tok", 9), ("start", SLOT_TILES), ("valid", 9), ("dec", 4), ("eps", 1), ("ones", 128)):
    CONST_COLS[_n] = (_at, _at + _w)
    _at += _w
NCONST = _at


def constants():
    c = np.zeros((P, NCONST), np.float32)
    p = np.arange(P)

    def put(name, value):
        a, b = CONST_COLS[name]
        c[:, a:b] = value

    put("ident", np.eye(P))
    put("mask", np.where(p[None, :] > p[:, None], -BIG, 0.0))
    put("tri", (p[:, None] < p[None, :]))
    put("half", np.stack([p < HD, p >= HD], 1))
    put("delta", np.tile(np.eye(NS).reshape(1, 64), (P, 1)))
    put("coef_a", (p % 2 == 0)[:, None])
    put("coef_b", (p % 2 == 1)[:, None])
    put("corr", np.concatenate([[w / min(w, t + 1) for t in range(16)] for w in WIN])[None, :])
    put("sel", (p[:, None] // 2 == np.arange(NS)[None, :]))
    put("tok", p[:, None] + P * np.arange(NT + 1)[None, :])
    put("start", P * np.arange(SLOT_TILES)[None, :])
    valid = np.ones((P, NT + 1))
    valid[NS:, NT] = 0
    put("valid", valid)
    put("dec", np.array([4, 3, 2, 1])[None, :])
    put("eps", EPS)
    put("ones", 1.0)
    half = HD // 2
    inv = (np.float32(10000.0) ** (-np.arange(half, dtype=np.float32) / half)).astype(np.float32)
    pos = np.concatenate([np.arange(SEQ), np.full(NS, PAST)]).astype(np.float32)
    ang = (pos[None, :] * inv[p % half][:, None]).astype(np.float32)
    sign = np.where(p % HD < half, -1.0, 1.0)[:, None]
    return c, np.stack([np.cos(ang), sign * np.sin(ang)], 1).astype(np.float32)


class Event:

    def __init__(self, sem, per, first=0):
        self.sem, self.per, self.first = sem, per, first

    def wait(self, eng, h, k):
        eng.wait_ge(self.sem, h * self.per + (self.first + k + 1))

    def wait_first(self, eng, k):
        eng.wait_ge(self.sem, k + 1)


class Chain:

    def __init__(self, eng, sem):
        self.eng, self.sem, self.base, self.n = eng, sem, 0, 0

    def __call__(self, ins):
        self.n += 1
        ins.then_inc(self.sem, 1)
        self.eng.wait_ge(self.sem, self.base + self.n)

    def loop(self, start, end, per):
        chain = self

        class _Loop:
            def __enter__(self):
                self.before = chain.n
                self.cm = chain.eng.Fori(start, end)
                i = self.cm.__enter__()
                chain.base = (i - start) * per if start else i * per
                return i

            def __exit__(self, *a):
                r = self.cm.__exit__(*a)
                used = chain.n - self.before
                assert used == per or a[0], ("chained instructions in a turn", used)
                chain.base, chain.n = 0, self.before + per * (end - start)
                return r
        return _Loop()


def build(nc, ins, outs):
    with ExitStack() as ctx:
        _build(nc, ctx, ins, outs)


def _build(nc, ctx, I, O):
    def sb(name, shape, dt):
        return ctx.enter_context(nc.sbuf_tensor(name, shape, dt))

    def sem(name):
        return ctx.enter_context(nc.semaphore(name))

    def dram(name, shape, dt=F32):
        return nc.dram_tensor(name, shape, dt, kind="Internal").ap()

    NR = 30848
    NF = 20700
    R = sb("R", [P, NR], F32R)
    F = sb("F", [P, NF], F32)
    cst = sb("cst", [P, NCONST], F32)
    maskb = sb("maskb", [P, P], BF16)
    identb = sb("identb", [P, P], BF16)
    sm = sb("sm", [P, 352], F32)

    class Pool_:
        def __init__(self, t, size):
            self.t, self.size, self.at = t, size, 0

        def take(self, n, *dims):
            a = self.t[:, self.at:self.at + n]
            self.at += n
            assert self.at <= self.size, (self.at, self.size)
            if len(dims) == 2:
                a = a.rearrange("p (a b) -> p a b", a=dims[0])
            if len(dims) == 3:
                a = a.rearrange("p (a b c) -> p a b c", a=dims[0], b=dims[1])
            return a

    def const(name):
        a, b = CONST_COLS[name]
        return cst[:, a:b]

    ident, ones = const("ident"), const("ones")
    S = ctx.enter_context(nc.psum_tensor("S", [P, 2048], F32))
    TB = [ctx.enter_context(nc.psum_tensor(f"T{i}", [P, 512], F32)) for i in range(2)]
    OB = ctx.enter_context(nc.psum_tensor("OB", [P, 512], F32))
    PB = ctx.enter_context(nc.psum_tensor("PB", [P, 512], F32))
    Sb = [S[:, 512 * i:512 * i + 512] for i in range(4)]

    smp = Pool_(sm, 352)
    neglam = smp.take(1)
    coef = smp.take(1)
    lamt = smp.take(4)
    sublng = smp.take(1)
    pscale = smp.take(8)
    modT = smp.take(144, 16, 9)
    nmax = smp.take(2)
    esum = smp.take(2)
    resum = smp.take(2)
    snm = smp.take(1)
    sss = smp.take(1)
    srs = smp.take(1)
    qs = smp.take(8)
    ks = smp.take(8)
    sE = smp.take(16, 8, 2)
    sT = smp.take(32, 2, 16)
    wsum = smp.take(16, 2, 8)
    dgw = smp.take(8)
    stat = smp.take(12, 2, 6)
    mv = smp.take(2)
    rstd1 = smp.take(1)
    pt = sb("pt", [1, 16], I32)

    mod_d = dram("mod_d", [9, NMOD * D])
    pool_d = dram("pool_d", [8, P, T])
    mg_d = dram("mg_d", [8, P, T])
    x1_d = dram("x1_d", [T, D])
    h2_d = dram("h2_d", [T, D])
    tok_d = dram("tok_d", [SLOTS, 1], U32)
    y_d = dram("y_d", [SLOTS, D])

    x_p = I["x_prompt"].rearrange("b s d -> (b s) d")
    x_s = I["x_sample"].rearrange("b s d -> (b s) d")
    w_in = I["w_in"][0].rearrange("(k p) n -> p k n", p=P)
    w_ada = I["w_ada"][0].rearrange("(k p) n -> p k n", p=P)
    y_p = O[0].rearrange("b s d -> (b s) d")
    y_s = O[1].rearrange("b s d -> (b s) d")
    nk_p = O[2].rearrange("l b (t p) h m d -> (l b) p t h (m d)", p=P)
    nv_p = O[3].rearrange("l b (t p) h d -> (l b) p t h d", p=P)
    nk_s = O[5].rearrange("l b s h m d -> (l s) b h (m d)")
    nv_s = O[6].rearrange("l b s h d -> (l s) b h d")
    ck = I["cache_k"][0].rearrange("n p h m d -> n p h (m d)")
    cv = I["cache_v"][0]

    stage_done = sem("stage_done")

    def stage_end(eng, n):
        eng.sem_inc(stage_done, 1)
        eng.wait_ge(stage_done, 5 * (n + 1))

    waits_apart = sem("waits_apart")

    def apart(eng):
        eng.sem_inc(waits_apart, 1)

    v_chain, a_chain = sem("vector_chain"), sem("scalar_chain")

    f = Pool_(F, NF)
    cossin = f.take(2 * T, 2, T)
    xr = f.take(9 * D, 9, D)
    crow = f.take(D)
    modrow = [f.take(256) for _ in range(2)]
    badab = [f.take(256) for _ in range(2)]
    sTc = f.take(72, 8, 9)
    AW = 256
    adaw = [f.take(KC * AW, KC, AW) for _ in range(2)]
    h32 = [f.take(512) for _ in range(2)]
    lamv = f.take(256, 4, 64)
    hs32 = f.take(64, 8, 8)
    NADA = NMOD * D // AW

    r = Pool_(R, NR)
    hT = [r.take(KC * T, KC, T) for _ in range(2)]
    whl = [[r.take(KC * P, KC, P) for _ in range(2)] for _ in range(2)]
    r_heads = r.at

    ld_c = sem("ld_c")
    ld_ada = [sem(f"ld_ada{i}") for i in range(2)]
    ld_x = sem("ld_x")
    ld_small = sem("ld_small")
    ada_done = sem("ada_done")
    ada_row = sem("ada_row")
    ada_st = [sem(f"ada_st{i}") for i in range(2)]
    cT_done, silu_done, cT_copied = sem("cT_done"), sem("silu_done"), sem("cT_copied")
    modT_done, modT_copied = sem("modT_done"), sem("modT_copied")
    xT_done, h_hi, h_lo, hs_ready = sem("xT_done"), sem("h_hi"), sem("h_lo"), sem("hs_ready")
    h_full = sem("h_full")
    lam_exp = sem("lam_exp")
    lam_sum = sem("lam_sum")

    f = Pool_(F, NF)
    f.take(2 * T)
    ubuf = f.take(16 + T)
    sA = f.take(16 + SEQ)
    sB = f.take(16 + SEQ)
    pooled = f.take(T)
    poolo = [f.take(T) for _ in range(2)]
    stt = f.take(512)
    stall = f.take(480, 4, 120)
    ssum = f.take(8)
    wp32 = f.take(256)
    upo = f.take(128)
    uso = f.take(128)
    wraw = [f.take(KC * P, KC, P) for _ in range(2)]
    r1 = Pool_(R, NR)
    r1.at = r_heads
    plr = [r1.take(T) for _ in range(2)]
    wpr = [r1.take(256) for _ in range(2)]

    w_landed = [sem(f"w_landed{i}") for i in range(2)]
    w_hi = Event(sem("w_hi"), 5, 4)
    w_lo = Event(sem("w_lo"), 5, 4)
    piece_ready = Event(sem("piece_ready"), 15, 12)
    piece_copied = Event(sem("piece_copied"), 9, 12)
    piece_rope = Event(sem("piece_rope"), 6)
    swap_done = Event(sem("swap_done"), 6)
    ld_pool = sem("ld_pool")
    stT_ready, stT_copied = sem("stT_ready"), sem("stT_copied")
    pool_split, pool_ready, pool_out = sem("pool_split"), sem("pool_ready"), sem("pool_out")
    pool_st = [sem(f"pool_st{i}") for i in range(2)]
    uT_ready, uT_copied, u_st = sem("uT_ready"), sem("uT_copied"), sem("u_st")
    state_st = sem("state_st")
    pl_hi = sem("pl_hi")
    pooled_done = sem("pooled_done")
    wp_landed = sem("wp_landed")

    f = Pool_(F, NF)
    f.take(2 * T)
    cosT, sinT = cossin[:, 0, :], cossin[:, 1, :]
    Pr = f.take(2 * SEQ, 2, SEQ)
    Wt = f.take(2 * SEQ, 2, SEQ)
    q32, k32, v32 = f.take(T), f.take(T), f.take(T)
    gate = [f.take(T) for _ in range(2)]
    poolc = f.take(T)
    O32 = f.take(T)
    kout = f.take(SEQ, 8, P)
    vt32 = f.take(SEQ, 8, P)
    KV = f.take(16 * P, 16, P)
    wraw2 = [f.take(KC * P, KC, P) for _ in range(2)]
    swp = f.take(PIECE)
    kso, vso = f.take(P), f.take(P)
    ps32 = f.take(PAST + 2)
    os32 = f.take(P)
    W8 = f.take(128, 16, 8)
    sq = Pr[:, :, :].rearrange("p a b -> p (a b)")[:, 0:T]
    rst = Wt[:, :, :].rearrange("p a b -> p (a b)")[:, 0:T]
    Bd = O32[:, 0:1024].rearrange("p (b f) -> p b f", b=8)
    r2 = Pool_(R, NR)
    r2.at = r_heads
    qhl = [r2.take(2 * SEQ, 2, SEQ) for _ in range(2)]
    khl = [r2.take(SEQ) for _ in range(2)]
    vhl = [r2.take(SEQ, 8, P) for _ in range(2)]
    wt = [[r2.take(512, 2, 256) for _ in range(2)] for _ in range(2)]

    def ev(name, per, first=0):
        return Event(sem(name), per, first)

    s_ready, smax, exp_done, comb = ev("s_ready", 8), ev("smax", 8), ev("exp_done", 8), ev("comb", 8)
    t_ready, wt_hi, wt_lo, pv_done = ev("t_ready", 10), ev("wt_hi", 10), ev("wt_lo", 10), ev("pv_done", 10)
    o_copied = ev("o_copied", 4)
    kt_ready, kt_copied = ev("kt_ready", 5), ev("kt_copied", 5)
    qk_hi, qk_lo, v_hi, v_lo = ev("qk_hi", 1), ev("qk_lo", 1), ev("v_hi", 1), ev("v_lo", 1)
    bd_done, qbc_ready, sT_done, sT_ready = ev("bd_done", 1), ev("qbc_ready", 1), ev("sT_done", 1), ev("sT_ready", 1)
    smx_done, sexp_done, pn_done = ev("smx_done", 1), ev("sexp_done", 1), ev("pn_done", 1)
    pnT_ready, w8_done, os_ready, os_copied = ev("pnT_ready", 1), ev("w8_done", 1), ev("os_ready", 1), ev("os_copied", 1)
    osT_ready, osT_copied = ev("osT_ready", 1), ev("osT_copied", 1)
    sq_done, ms_ready, ln_done, rst_done = ev("sq_done", 1), ev("ms_ready", 3), ev("ln_done", 3), ev("rst_done", 1)
    merged = ev("merged", 2)

    k_landed, v_landed = sem("kpages_landed"), sem("vpages_landed")
    poolc_landed = sem("poolc_landed")
    mg_st = sem("merged_stored")
    kout_st, vout_st, kvs_st = sem("kout_stored"), sem("vout_stored"), sem("kvs_stored")
    qzero = sem("qzero")

    f = Pool_(F, NF)
    wo32 = f.take(4096, 4, D)
    mt32 = [f.take(D, KC, P) for _ in range(2)]
    x3 = [f.take(D) for _ in range(2)]
    y3 = f.take(D)
    x1t = [f.take(D) for _ in range(2)]
    h2t = [f.take(D) for _ in range(2)]
    h2T = f.take(D, KC, P)
    g1b, sc2b, sh2b, l1g, l1b = [f.take(D) for _ in range(5)]
    r3 = Pool_(R, NR)
    wo = [r3.take(KC * D, KC, D) for _ in range(2)]
    mhl = [[r3.take(D, KC, P) for _ in range(2)] for _ in range(2)]
    wrgv = f.take(KC * 20, KC, 20)
    brg = f.take(20)
    rlv = f.take(180, 9, 20)
    wo_landed, wo_hi, wo_lo = sem("wo_landed"), sem("wo_hi"), sem("wo_lo")
    tab_landed = sem("tab_landed")
    m_landed = [sem(f"m_landed{i}") for i in range(2)]
    m_hi, m_lo = sem("m_hi"), sem("m_lo")
    wout_ready, wout_used = sem("wout_ready"), sem("wout_used")
    var_done, std_done = sem("var_done"), sem("std_done")
    h2_done = sem("h2_done")
    x1_st, h2_st = [sem(f"x1_st{i}") for i in range(2)], [sem(f"h2_st{i}") for i in range(2)]
    h2T_ready, h2T_copied, rl_ready, rl_used = sem("h2T_ready"), sem("h2T_copied"), sem("rl_ready"), sem("rl_used")
    x1_ready = sem("x1_ready")

    w1c, w2c = sb("w1c", [P, 9], F32), sb("w2c", [P, 9], F32)
    slot = [sb(f"slot{i}", [P, 9], U32) for i in range(2)]
    toku = sb("toku", [P, 9], U32)
    te = sb("te", [1, 32], I32)
    route_exp, route_exp_done = sem("route_exp"), sem("route_exp_done")
    m_mask, pos_ready, slots_done = sem("m_mask"), sem("pos_ready"), sem("slots_done")
    zero_done, zero_st, tok_st = sem("zero_done"), sem("zero_st"), sem("tok_st")
    f = Pool_(F, NF)
    M1, M2, M12, slotf = [f.take(144, 9, 16) for _ in range(4)]
    cnt = f.take(16)
    base = f.take(17)
    tef = f.take(32 * 16, 32, 16)
    te32 = f.take(32)
    pref = f.take(160, 10, 16)
    tokz = f.take(32)
    oh_g, esel, oh1, oh2 = [f.take(36, 9, 4) for _ in range(4)]
    rt36 = [f.take(36, 9, 4) for _ in range(2)]
    r9 = [f.take(9) for _ in range(4)]
    cnti = sb("cnti", [P, 16], I32)
    assert f.at <= 4096
    Mb = sb("Mb", [P, 144], BF16)
    trib = sb("trib", [P, P], BF16)
    onesb = sb("onesb", [P, P], BF16)

    f = Pool_(F, NF)
    raw_g = [f.take(KC * FF, KC, FF) for _ in range(2)]
    raw_u = [f.take(KC * FF, KC, FF) for _ in range(2)]
    raw_d = [f.take(2 * D, 2, D) for _ in range(2)]
    xg = [f.take(D) for _ in range(2)]
    yv = [f.take(D) for _ in range(2)]
    silu = f.take(FF)
    av = f.take(FF)
    r4 = Pool_(R, NR)
    gu = [[r4.take(KC * 512, KC, 512) for _ in range(2)] for _ in range(2)]
    dn = [[r4.take(2 * D, 2, D) for _ in range(2)] for _ in range(2)]
    hg = [[r4.take(D, KC, P) for _ in range(2)] for _ in range(2)]
    aT = [r4.take(FF, 2, P) for _ in range(2)]
    idx = [sb(f"idx{i}", [P, 1], U32) for i in range(2)]
    idx_landed = [sem(f"idx_landed{i}") for i in range(2)]
    xg_landed = [sem(f"xg_landed{i}") for i in range(2)]
    e_landed = [sem(f"e_landed{i}") for i in range(2)]
    d_landed = [sem(f"d_landed{i}") for i in range(2)]
    xgT_ready, hg_hi, hg_lo = sem("xgT_ready"), sem("hg_hi"), sem("hg_lo")
    g_hi, g_lo, u_lo, dn_hi, dn_lo = sem("g_hi"), sem("g_lo"), sem("u_lo"), sem("dn_hi"), sem("dn_lo")
    gu_used, dn_used = sem("gu_used"), sem("dn_used")
    silu_ok, av_done, avT_ready, avT_hi, avT_lo = sem("silu_ok"), sem("av_done"), sem("avT_ready"), sem("avT_hi"), sem("avT_lo")
    y_copied = sem("y_copied")
    y_st = [sem(f"y_st{i}") for i in range(2)]

    f = Pool_(F, NF)
    x5 = [f.take(D) for _ in range(2)]
    ya = [f.take(D) for _ in range(2)]
    yb = [f.take(D) for _ in range(2)]
    m5 = f.take(D)
    o5 = [f.take(D) for _ in range(2)]
    g2b, l2g, l2b = [f.take(D) for _ in range(3)]
    x5_landed = [sem(f"x5_landed{i}") for i in range(2)]
    y5_landed = [sem(f"y5_landed{i}") for i in range(2)]
    tab5 = sem("tab5")
    out_ready = sem("out_ready")
    out_st = [sem(f"out_st{i}") for i in range(2)]
    m5_used = sem("m5_used")

    def landed_value(h, c):
        if c % 2 == 0:
            return h * 48 + 16 * (2 + c // 2 + 1)
        return h * 32 + 16 * (2 + c // 2 + 1)

    COLS = (QC, KCOL, VC, GPC, GAC)
    block = ctx.enter_context(nc.Block())

    @block.sync
    def _(sp):
        with nc.allow_non_contiguous_dma(reason="small tables by feature"):
            sp.dma_start(cst[:, :], I["cst"]).then_inc(ld_c, 16)
            sp.dma_start(crow[0:1, :], I["c_prompt"]).then_inc(ld_c, 16)
            sp.dma_start(crow[1:9, :], I["c_sample"]).then_inc(ld_c, 16)

            def ada(n, b, i, wait):
                if wait is not None:
                    sp.wait_ge(ada_row, wait)
                sp.dma_start(adaw[b], w_ada[:, :, bass.ds(n * AW, AW)]).then_inc(ld_ada[b], 16)
                sp.dma_start(badab[b][0:9, 0:AW], I["b_ada"][:, bass.ds(n * AW, AW)].to_broadcast([9, AW])).then_inc(ld_ada[b], 16)

            for n in range(8):
                ada(n, n % 2, n, n - 1 if n >= 2 else None)
                if n == 1:
                    for t in range(NT):
                        sp.dma_start(xr[:, t, :], x_p[t * P:(t + 1) * P, :]).then_inc(ld_x, 16)
                    sp.dma_start(xr[0:NS, NT, :], x_s).then_inc(ld_x, 16)
                    sp.dma_start(cossin, I["rope"]).then_inc(ld_small, 16)
                    sp.dma_start(sublng, I["subln_g"][0].rearrange("(p o) -> p o", o=1)).then_inc(ld_small, 16)
                    sp.dma_start(pscale, I["pool_scale"][0].rearrange("(k p) -> p k", p=P)).then_inc(ld_small, 16)
                    sp.dma_start(pt[:, :], I["page_table"].rearrange("b j -> (b j)").rearrange("(o n) -> o n", o=1)).then_inc(ld_small, 16)
                    for m, name in enumerate(("lambda_q1", "lambda_k1", "lambda_q2", "lambda_k2")):
                        sp.dma_start(lamv[:, m, :], I[name].to_broadcast([P, 64])).then_inc(ld_small, 16)
            with sp.Fori(0, (NADA - 8) // 2) as i:
                for b in range(2):
                    ada(i * 2 + 8 + b, b, None, i * 2 + (8 + b - 1))
            sp.wait_ge(ld_small, 16 * 8)
            stage_end(sp, 0)

            def wchunk(col, b, landed):
                sp.dma_start(wraw[b], w_in[:, :, bass.ds(col, P)]).then_inc(w_landed[b], 16)

            sp.dma_start(stt[0:120, :], I["state_pool"][0].rearrange("b r c -> (b r) c")).then_inc(ld_pool, 16)
            for g in range(4):
                if g >= 2:
                    w_hi.wait_first(sp, g - 2)
                    w_lo.wait_first(sp, g - 2)
                wchunk(UC + g * P, g % 2, None)
                if g >= 1:
                    sp.wait_ge(pool_split, 2 * g)
                sp.dma_start(wp32, I["w_pool"][0, g]).then_inc(wp_landed, 16)
            sp.dma_start(O[7][0, :, 0:BUF - 1, :], I["state_pool"][0, :, 1:BUF, :]).then_inc(state_st, 16)
            for b in range(2):
                sp.wait_ge(pool_st[b], 16 * 4)
            sp.wait_ge(u_st, 16 * 8)
            sp.wait_ge(state_st, 16)
            stage_end(sp, 1)

            def chunk(h, c):
                before = -1 if c == 0 else c - 2 if c > 1 else -2
                w_lo.wait(sp, h, before)
                w_hi.wait(sp, h, before)
                col = h * P + COLS[c]
                sp.dma_start(wraw2[c % 2], w_in[:, :, bass.ds(col, P)]).then_inc(w_landed[c % 2], 16)

            def pages(h, table, landed):
                apart(sp)
                for n in range(16):
                    page = sp.value_load(pt[0:1, n:n + 1], min_val=0, max_val=N_PHYS - 1)
                    sp.dma_start(KV[:, n, :], table[bass.ds(page, 1), :, bass.ds(h, 1), :]
                                 .rearrange("a p h d -> (a p) (h d)")).then_inc(landed, 16)

            def step(h, nxt, first):
                if nxt:
                    chunk(h + 1, 0)
                if not first:
                    os_ready.wait(sp, h, -1)
                pages(h, ck, k_landed)
                if nxt:
                    chunk(h + 1, 1)
                if not first:
                    sp.wait_ge(mg_st, h * 16)
                sp.dma_start(poolc, pool_d[bass.ds(h, 1), :, :].rearrange("a p n -> (a p) n")).then_inc(poolc_landed, 16)
                sT_done.wait(sp, h, 0)
                pages(h, cv, v_landed)
                if nxt:
                    for c in range(2, 5):
                        chunk(h + 1, c)

            for c in range(5):
                chunk(0, c)
            step(0, True, True)
            with sp.Fori(1, H - 1) as h:
                step(h, True, False)
            step(H - 1, False, False)
            sp.wait_ge(mg_st, 16 * H)
            stage_end(sp, 2)

            wov = I["w_out"][0].rearrange("(k p) n -> p k n", p=P)
            for q in range(2):
                if q:
                    sp.wait_ge(wo_lo, 1)
                    sp.wait_ge(wo_hi, 1)
                sp.dma_start(wo32, wov[:, 4 * q:4 * q + 4, :]).then_inc(wo_landed, 16)
                if q == 0:
                    sp.dma_start(wrgv[:, :, 0:4], I["w_group"][0].rearrange("(k p) n -> p k n", p=P)).then_inc(tab_landed, 16)
                    sp.dma_start(wrgv[:, :, 4:20], I["w_router"][0].rearrange("(k p) n -> p k n", p=P)).then_inc(tab_landed, 16)
                    sp.dma_start(brg[:, 0:4], I["b_group"].to_broadcast([P, 4])).then_inc(tab_landed, 16)
                    sp.dma_start(brg[:, 4:20], I["b_router"].to_broadcast([P, 16])).then_inc(tab_landed, 16)
                    sp.dma_start(g1b, mod_d[0:1, 2 * D:3 * D].to_broadcast([P, D])).then_inc(tab_landed, 16)
                    sp.dma_start(sh2b, mod_d[0:1, 3 * D:4 * D].to_broadcast([P, D])).then_inc(tab_landed, 16)
                    sp.dma_start(sc2b, mod_d[0:1, 4 * D:5 * D].to_broadcast([P, D])).then_inc(tab_landed, 16)
                    sp.dma_start(l1g, I["ln1_g"].to_broadcast([P, D])).then_inc(tab_landed, 16)
                    sp.dma_start(l1b, I["ln1_b"].to_broadcast([P, D])).then_inc(tab_landed, 16)

            def tile3(t, i, b, rows, wait):
                if wait:
                    sp.wait_ge(h2_done, i * 2 + (b - 1))
                sp.dma_start(mt32[b][:, :, 0:rows], mg_d.rearrange("k p n -> p k n")[:, :, bass.ds(t * P, rows)]).then_inc(m_landed[b], 16)
                sp.dma_start(x3[b][0:rows, :], (x_p[bass.ds(t * P, rows), :] if rows == P else x_s)).then_inc(m_landed[b], 16)

            tile3(0, 0, 0, P, False)
            tile3(1, 0, 1, P, False)
            with sp.Fori(1, NT // 2) as i:
                for b in range(2):
                    tile3(i * 2 + b, i, b, P, True)
            tile3(NT, NT // 2, 0, NS, True)
            sp.wait_ge(h2_done, NT)
            sp.dma_start(g1b[0:NS, :], mod_d[1:9, 2 * D:3 * D]).then_inc(tab_landed, 16)
            sp.dma_start(sh2b[0:NS, :], mod_d[1:9, 3 * D:4 * D]).then_inc(tab_landed, 16)
            sp.dma_start(sc2b[0:NS, :], mod_d[1:9, 4 * D:5 * D]).then_inc(tab_landed, 16)
            for b in range(2):
                sp.wait_ge(x1_st[b], 16 * (5 if b == 0 else 4))
                sp.wait_ge(h2_st[b], 16 * (5 if b == 0 else 4))
            sp.wait_ge(tok_st, 16 * 18)
            stage_end(sp, 3)

            def experts(n, b, later):
                if later is not None:
                    sp.wait_ge(xg_landed[b], later)
                    apart(sp)
                e = sp.value_load(te[0:1, bass.ds(n, 1)], min_val=0, max_val=NE - 1)
                sp.dma_start(idx[b][:, :], tok_d[bass.ds(n * P, P), :]).then_inc(idx_landed[b], 16)
                if later is not None:
                    sp.wait_ge(g_hi, n * 4 - 4)
                    sp.wait_ge(g_lo, n * 2 - 2)
                sp.dma_start(raw_g[b], I["w_e_gate"][0, bass.ds(e, 1)].rearrange("a (k p) n -> p (a k) n", p=P)).then_inc(e_landed[b], 16)
                if later is not None:
                    sp.wait_ge(u_lo, n * 2 - 2)
                sp.dma_start(raw_u[b], I["w_e_up"][0, bass.ds(e, 1)].rearrange("a (k p) n -> p (a k) n", p=P)).then_inc(e_landed[b], 16)
                if later is not None:
                    sp.wait_ge(dn_hi, n * 2 - 2)
                    sp.wait_ge(dn_lo, n * 2 - 2)
                sp.dma_start(raw_d[b], I["w_e_down"][0, bass.ds(e, 1)].rearrange("a (k p) n -> p (a k) n", p=P)).then_inc(d_landed[b], 16)

            for b in range(2):
                experts(b, b, None)
            with sp.Fori(1, SLOT_TILES // 2) as i:
                for b in range(2):
                    experts(i * 2 + b, b, i * 16)
            for b in range(2):
                sp.wait_ge(y_st[b], 16 * (SLOT_TILES // 2 + 1))
            stage_end(sp, 4)

            sp.dma_start(g2b, mod_d[0:1, 5 * D:6 * D].to_broadcast([P, D])).then_inc(tab5, 16)
            sp.dma_start(l2g, I["ln2_g"].to_broadcast([P, D])).then_inc(tab5, 16)
            sp.dma_start(l2b, I["ln2_b"].to_broadcast([P, D])).then_inc(tab5, 16)
            for t in range(NT + 1):
                rows = P if t < NT else NS
                if t >= 2:
                    sp.wait_ge(m5_used, t - 1)
                sp.dma_start(x5[t % 2][0:rows, :], x1_d[t * P:t * P + rows, :]).then_inc(x5_landed[t % 2], 16)
            sp.wait_ge(m5_used, NT)
            sp.dma_start(g2b[0:NS, :], mod_d[1:9, 5 * D:6 * D]).then_inc(tab5, 16)
            sp.wait_ge(out_st[0], 16 * 5)
            sp.wait_ge(out_st[1], 16 * 4)

    @block.tensor
    def _(pe):
        mm, tr = nc.tensor.matmul, nc.tensor.transpose

        def mm3(out, w, m, start=True, stop=True):
            mm(out, w[0], m[1], start=start, stop=False)
            mm(out, w[1], m[0], start=False, stop=False)
            return mm(out, w[0], m[0], start=False, stop=stop)

        pe.wait_ge(ld_c, 48)
        pe.wait_ge(silu_done, 1)
        for k in range(KC):
            last = tr(TB[0][:, 9 * k:9 * k + 9], crow[0:9, k * P:(k + 1) * P], ident[0:9, 0:9])
        last.then_inc(cT_done, 1)
        pe.wait_ge(cT_copied, 1)

        def ada(b, landed, used):
            pe.wait_ge(ld_ada[b], landed)
            if used is not None:
                pe.wait_ge(ada_row, used)
            for k in range(KC):
                last = mm(Sb[b][0:9, 0:AW], sTc[:, k, :], adaw[b][:, k, :], start=(k == 0), stop=(k == KC - 1))
            last.then_inc(ada_done, 1)

        for n in range(8):
            ada(n % 2, 32 * (n // 2 + 1), n - 1 if n >= 2 else None)
            pe.wait_ge(ada_row, n + 1)
            if n >= 1:
                pe.wait_ge(modT_copied, n)
            for q in range(2):
                last = tr(TB[1][:, 9 * q:9 * q + 9], modrow[n % 2][0:9, q * P:(q + 1) * P], ident[0:9, 0:9])
            last.then_inc(modT_done, 1)
        with pe.Fori(0, (NADA - 8) // 2) as i:
            for b in range(2):
                ada(b, i * 32 + 32 * 5, i * 2 + (8 + b - 1))
        pe.wait_ge(ld_x, 16 * 9)
        pe.wait_ge(modT_copied, 8)
        for k in range(KC):
            for q in range(2):
                n = 2 * k + q
                if n >= 2:
                    pe.wait_ge(h_full, n - 1)
                for t in range(4):
                    last = tr(TB[n % 2][:, t * P:(t + 1) * P], xr[:, 4 * q + t, k * P:(k + 1) * P], ident)
                last.then_inc(xT_done, 1)
        for k in range(KC):
            last = tr(OB[:, NS * k:NS * k + NS], xr[0:NS, NT, k * P:(k + 1) * P], ident[0:NS, 0:NS])
        last.then_inc(xT_done, 1)
        stage_end(pe, 0)

        def piece(b, s):
            for k in range(KC):
                last = mm3(PB[:, 0:PIECE], [w[:, k, :] for w in whl[b]],
                           [x[:, k, s * PIECE:(s + 1) * PIECE] for x in hT], start=(k == 0), stop=(k == KC - 1))
            return last

        pe.wait_ge(ld_pool, 16)
        for g in range(4):
            last = tr(TB[0][:, 120 * g:120 * g + 120], stt[0:120, g * P:(g + 1) * P], ident[0:120, 0:120])
        last.then_inc(stT_ready, 1)
        pe.wait_ge(stT_copied, 1)
        for g in range(4):
            w_hi.wait_first(pe, g)
            w_lo.wait_first(pe, g)
            for s in range(3):
                if 3 * g + s:
                    piece_copied.wait_first(pe, 3 * g + s - 1)
                piece(g % 2, s).then_inc(piece_ready.sem, 1)
            piece_copied.wait_first(pe, 3 * g + 2)
            if g:
                pe.wait_ge(uT_copied, 2 * g)
            tr(OB[0:BUF, 0:P], ubuf[:, 16 + SEQ - BUF:16 + SEQ], ident)
            tr(OB[0:NS, P:2 * P], ubuf[:, 16 + SEQ:16 + T], ident).then_inc(uT_ready, 1)
            pe.wait_ge(pool_split, 2 * (g + 1))
            pe.wait_ge(pl_hi, 2 * (g + 1))
            for c in range(2):
                for s in range(3):
                    n = 6 * g + 3 * c + s
                    if n >= 2:
                        pe.wait_ge(pool_out, n - 1)
                    mm3(TB[n % 2][:, 0:PIECE], [w[:, c * P:(c + 1) * P] for w in wpr],
                        [x[:, s * PIECE:(s + 1) * PIECE] for x in plr]).then_inc(pool_ready, 1)
        stage_end(pe, 1)

        def proj(h, n):
            c = n // 3
            if n % 3 == 0:
                w_hi.wait(pe, h, c)
                w_lo.wait(pe, h, c)
            if n == 0:
                piece_copied.wait(pe, h, -1)
            elif n <= 6:
                piece_rope.wait(pe, h, n - 1)
            else:
                piece_copied.wait(pe, h, n - 7)
            piece(c % 2, n % 3).then_inc(piece_ready.sem, 1)

        def kv_rows(h, n):
            if n == 0:
                piece_rope.wait(pe, h, 5)
                piece_copied.wait(pe, h, 2)
            if n >= 2:
                kt_copied.wait(pe, h, n - 2)
            if n < 4:
                src = (k32, v32)[n // 2]
                for t in range(4):
                    last = tr(TB[n % 2][:, t * P:(t + 1) * P], src[:, (4 * (n % 2) + t) * P:(4 * (n % 2) + t + 1) * P], ident)
            else:
                tr(TB[0][0:NS, 0:P], k32[:, SEQ:T], ident)
                last = tr(TB[0][0:NS, P:2 * P], v32[:, SEQ:T], ident)
            last.then_inc(kt_ready.sem, 1)

        def scores(h, i):
            L = (i + 1) * P
            for m in range(2):
                for a in range(0, L, 512):
                    n = max(min(512, L - a), 256)
                    out = S[:, m * SEQ + a:m * SEQ + a + n]
                    q, k = [x[:, m, i * P:(i + 1) * P] for x in qhl], [x[:, a:a + n] for x in khl]
                    mm(out, q[0], k[1], start=True, stop=False)
                    mm(out, q[1], k[0], start=False, stop=False)
                    if a + 512 >= L:
                        mm(S[:, m * SEQ + i * P:m * SEQ + L], identb[:, :], maskb[:, :], start=False, stop=False)
                    last = mm(out, q[0], k[0], start=False, stop=True)
            last.then_inc(s_ready.sem, 1)

        def groups(h, i):
            p = i // 2
            at = p * (p + 1) // 2

            def turn(g):
                n = at + g
                if n == 0:
                    sT_done.wait(pe, h, 0)
                elif n == 1:
                    sexp_done.wait(pe, h, 0)
                elif n == 3:
                    w8_done.wait(pe, h, 0)
                elif n == 6:
                    osT_copied.wait(pe, h, 0)
                if n >= 2:
                    wt_lo.wait(pe, h, n - 2)
                for j in range(2):
                    for t in range(2):
                        last = tr(TB[n % 2][:, (2 * j + t) * P:(2 * j + t + 1) * P],
                                  Wt[:, t, (2 * g + j) * P:(2 * g + j + 1) * P], ident)
                last.then_inc(t_ready.sem, 1)

            def product(g):
                n = at + g
                wt_hi.wait(pe, h, n)
                wt_lo.wait(pe, h, n)
                if g == 0 and p > 0:
                    o_copied.wait(pe, h, p - 1)
                for j in range(2):
                    last = mm3(OB[:, 0:256], [v[:, 2 * g + j, :] for v in vhl], [w[:, j, :] for w in wt[n % 2]],
                               start=(g == 0 and j == 0), stop=(g == p and j == 1))
                last.then_inc(pv_done.sem, 1)

            comb.wait(pe, h, i)
            turn(0)
            for g in range(1, p + 1):
                turn(g)
                product(g - 1)
            product(p)

        def step(h, nxt, first):
            qk_hi.wait(pe, h, 0)
            qk_lo.wait(pe, h, 0)
            if not first:
                ln_done.wait(pe, h, -1)
            scores(h, 0)
            kt_copied.wait(pe, h, 4)
            bd_done.wait(pe, h, 0)
            for b in range(2):
                last = mm(TB[b][:, :], ones, Bd[:, 4 * b:4 * b + 4, :], start=True, stop=True)
            last.then_inc(qbc_ready.sem, 1)
            for i in range(8):
                if nxt:
                    proj(h + 1, i)
                    if i == 7:
                        proj(h + 1, 8)
                if i == 2:
                    v_hi.wait(pe, h, 0)
                    v_lo.wait(pe, h, 0)
                    if not first:
                        o_copied.wait(pe, h, -1)
                if i % 2 == 0 and i:
                    groups(h, i - 1)
                if i < 7:
                    exp_done.wait(pe, h, i)
                    scores(h, i + 1)
                if i == 2:
                    sT_done.wait(pe, h, 0)
                    for j in range(2):
                        tr(TB[1][0:16, j * P:(j + 1) * P], sT[:, j, :], ident)
                    mm(TB[1][0:16, PAST:PAST + 1], sE[:, :, :], ones[:, 0:1], start=True, stop=True).then_inc(sT_ready.sem, 1)
                if i == 4:
                    pn_done.wait(pe, h, 0)
                    wt_lo.wait(pe, h, 1)
                    apart(pe)
                    for j in range(2):
                        tr(TB[1][:, j * 16:j * 16 + 16], ps32[0:16, j * P:(j + 1) * P], ident[0:16, 0:16])
                    mm(TB[1][0:NS, 32:33], const("sel")[0:16, :], ps32[0:16, PAST:PAST + 1], start=True, stop=True)\
                        .then_inc(pnT_ready.sem, 1)
                if i == 6:
                    w8_done.wait(pe, h, 0)
                    wt_lo.wait(pe, h, 4)
                    pe.wait_ge(v_landed, (h + 1) * 256)
                    for n in range(16):
                        mm(TB[0][0:NS, 0:P], W8[:, n, :], KV[:, n, :], start=(n == 0), stop=False)
                    mm(TB[0][0:NS, 0:P], dgw[0:NS, :], vso[0:NS, :], start=False, stop=True).then_inc(os_ready.sem, 1)
            os_copied.wait(pe, h, 0)
            apart(pe)
            tr(TB[0][:, 0:NS], os32[0:NS, :], ident[0:NS, 0:NS]).then_inc(osT_ready.sem, 1)
            groups(h, 7)
            if nxt:
                wt_lo.wait(pe, h, 9)
                kv_rows(h + 1, 0)
                kv_rows(h + 1, 1)
            exp_done.wait(pe, h, 7)
            sq_done.wait(pe, h, 0)
            for s in range(3):
                mm(Sb[s][:, 0:PIECE], ones, sq[:, s * PIECE:(s + 1) * PIECE], start=True, stop=True).then_inc(ms_ready.sem, 1)
            if nxt:
                proj(h + 1, 9)
                kv_rows(h + 1, 2)
                kv_rows(h + 1, 3)
                proj(h + 1, 10)
                kv_rows(h + 1, 4)
                for n in range(11, 15):
                    proj(h + 1, n)

        for n in range(9):
            proj(0, n)
        for n in range(5):
            kv_rows(0, n)
        for n in range(9, 15):
            proj(0, n)
        step(0, True, True)
        with pe.Fori(1, H - 1) as h:
            step(h, True, False)
        step(H - 1, False, False)
        stage_end(pe, 2)

        pe.wait_ge(wo_hi, 2)
        pe.wait_ge(wo_lo, 2)
        pe.wait_ge(tab_landed, 16 * 9)

        def project(n, b, rows):
            pe.wait_ge(m_hi, n + 1)
            pe.wait_ge(m_lo, n + 1)
            if not (isinstance(n, int) and n < 2):
                pe.wait_ge(wout_used, n - 1)
            for q in range(2):
                for k in range(KC):
                    last = mm3(S[0:rows, 1024 * b + 512 * q:1024 * b + 512 * q + 512], [m[:, k, 0:rows] for m in mhl[b]],
                               [w[:, k, 512 * q:512 * q + 512] for w in wo], start=(k == 0), stop=(k == KC - 1))
            last.then_inc(wout_ready, 1)

        def router(n, b, rows):
            pe.wait_ge(h2_done, n + 1)
            if not (isinstance(n, int) and n == 0):
                pe.wait_ge(h2T_copied, n)
            for k in range(KC):
                last = tr(TB[k // 4][:, (k % 4) * P:(k % 4) * P + rows], h2t[b][0:rows, k * P:(k + 1) * P], ident[0:rows, 0:rows])
            last.then_inc(h2T_ready, 1)
            pe.wait_ge(h2T_copied, n + 1)
            if not (isinstance(n, int) and n == 0):
                pe.wait_ge(rl_used, n)
            for k in range(KC):
                last = mm(PB[0:rows, 0:20], h2T[:, k, 0:rows], wrgv[:, k, :], start=(k == 0), stop=(k == KC - 1))
            last.then_inc(rl_ready, 1)

        project(0, 0, P)
        project(1, 1, P)
        router(0, 0, P)
        with pe.Fori(1, NT // 2) as i:
            project(i * 2, 0, P)
            router(i * 2 - 1, 1, P)
            project(i * 2 + 1, 1, P)
            router(i * 2, 0, P)
        project(NT, 0, NS)
        router(NT - 1, 1, P)
        router(NT, 0, NS)
        pe.wait_ge(m_mask, 1)
        mm(TB[0][:, 0:144], trib[:, :], Mb[:, :], start=True, stop=True)
        mm(TB[1][:, 0:144], onesb[:, :], Mb[:, :], start=True, stop=True).then_inc(pos_ready, 1)
        stage_end(pe, 3)

        def turn_rows(n, b, landed, later):
            pe.wait_ge(xg_landed[b], landed)
            if later:
                pe.wait_ge(hg_lo, 2 * n)
            for k in range(KC):
                last = tr(TB[k // 4][:, (k % 4) * P:(k % 4 + 1) * P], xg[b][:, k * P:(k + 1) * P], ident)
                if k == 3:
                    last.then_inc(xgT_ready, 1)
            last.then_inc(xgT_ready, 1)

        def gate_up(n, b, later):
            pe.wait_ge(hg_hi, n * 2 + 2)
            pe.wait_ge(hg_lo, n * 2 + 2)
            if later:
                pe.wait_ge(av_done, n - 1)
            for q in range(2):
                pe.wait_ge(g_hi, n * 4 + (2 * q + 2))
                pe.wait_ge(g_lo, n * 2 + (q + 1))
                pe.wait_ge(u_lo, n * 2 + (q + 1))
                for k in range(4 * q, 4 * q + 4):
                    last = mm3(Sb[b], [x[:, k, :] for x in hg[b]], [w[:, k, :] for w in gu[b]], start=(k == 0), stop=(k == KC - 1))
            last.then_inc(gu_used, 1)

        def turn_act(n, later):
            pe.wait_ge(av_done, n + 1)
            if later:
                pe.wait_ge(avT_lo, n)
            for c in range(2):
                last = tr(PB[:, c * P:(c + 1) * P], av[:, c * P:(c + 1) * P], ident)
            last.then_inc(avT_ready, 1)

        def down(n, b, later):
            pe.wait_ge(avT_hi, n + 1)
            pe.wait_ge(avT_lo, n + 1)
            pe.wait_ge(dn_hi, n * 2 + 2)
            pe.wait_ge(dn_lo, n * 2 + 2)
            if later:
                pe.wait_ge(y_copied, n)
            for q in range(2):
                for c in range(2):
                    last = mm3(Sb[2 + q], [a[:, c, :] for a in aT], [w[:, c, 512 * q:512 * q + 512] for w in dn[b]],
                               start=(c == 0), stop=(c == 1))
            last.then_inc(dn_used, 1)

        def tile4(n, b, landed, before, more=True):
            if more:
                turn_rows(n + 1, 1 - b, landed, True)
            if before >= 1:
                turn_act(n - 1, before >= 2)
            gate_up(n, b, before >= 2)
            if before >= 1:
                down(n - 1, 1 - b, before >= 2)

        turn_rows(0, 0, 16, False)
        tile4(0, 0, 16, 0)
        tile4(1, 1, 32, 1)
        with pe.Fori(1, SLOT_TILES // 2 - 1) as i:
            for b in range(2):
                tile4(i * 2 + b, b, i * 16 + 16 * (1 + b), 2)
        tile4(SLOT_TILES - 2, 0, 16 * (SLOT_TILES // 2), 2)
        tile4(SLOT_TILES - 1, 1, None, 2, more=False)
        turn_act(SLOT_TILES - 1, True)
        down(SLOT_TILES - 1, 1, True)
        stage_end(pe, 4)

    @block.scalar
    def _(act):
        A = Chain(act, a_chain)

        def sig(ins, event, h, k):
            ins.then_inc(event.sem, 1)
            event.wait(act, h, k)

        def act_(out, in_, func=ACT.Copy, **kw):
            return nc.scalar.activation(out, in_, func, **kw)

        act.wait_ge(ld_c, 48)
        act_(crow[0:9, :], crow[0:9, :], ACT.Silu).then_inc(silu_done, 1)

        def ada_store(n, b, row):
            act.wait_ge(ada_row, row)
            act.dma_start(mod_d[:, bass.ds(n * AW, AW)], modrow[b][0:9, 0:AW]).then_inc(ada_st[b], 16)

        for n in range(8):
            ada_store(n, n % 2, n + 1)
        with act.Fori(0, (NADA - 8) // 2) as i:
            for b in range(2):
                ada_store(i * 2 + 8 + b, b, i * 2 + (8 + b + 1))
        for n in range(16):
            k, q = n // 2, n % 2
            act.wait_ge(h_full, n + 1)
            act_(hT[0][:, k, 512 * q:512 * q + 512], h32[n % 2]).then_inc(h_hi, 1)
        act.wait_ge(hs_ready, 1)
        act_(hT[0][:, :, SEQ:T], hs32).then_inc(h_hi, 1)
        act.wait_ge(lam_sum, 1)
        act_(lamt[:, 0:2], lamt[:, 2:4], ACT.Exp).then_inc(lam_exp, 1)
        act.wait_ge(h_hi, 17)
        act.wait_ge(ada_st[0], 16 * NADA // 2)
        act.wait_ge(ada_st[1], 16 * NADA // 2)
        stage_end(act, 0)

        for g in range(4):
            act.wait_ge(w_landed[g % 2], 16 * (g // 2 + 1))
            if g >= 2:
                piece_ready.wait_first(act, 3 * (g - 2) + 2)
            act_(whl[g % 2][0], wraw[g % 2]).then_inc(w_hi.sem, 1)
            act.wait_ge(wp_landed, 16 * (g + 1))
            if g:
                act.wait_ge(pool_ready, 6 * g)
            act_(wpr[0], wp32).then_inc(pl_hi, 1)
            if g:
                act.wait_ge(pl_hi, 2 * g)
                act.wait_ge(pool_split, 2 * g)
                act.wait_ge(uT_ready, g)
            for s in range(3):
                piece_ready.wait_first(act, 3 * g + s)
                act_(ubuf[:, 16 + s * PIECE:16 + (s + 1) * PIECE], PB[:, 0:PIECE]).then_inc(piece_copied.sem, 1)
            act.wait_ge(uT_ready, g + 1)
            if g:
                act.wait_ge(u_st, 32 * g)
            act_(upo[0:BUF, :], OB[0:BUF, 0:P]).then_inc(uT_copied, 1)
            act_(uso[0:NS, :], OB[0:NS, P:2 * P]).then_inc(uT_copied, 1)
            act.wait_ge(uT_copied, 2 * g + 2)
            act.dma_start(O[4][0, 0, :, g * P:(g + 1) * P], upo[0:BUF, :]).then_inc(u_st, 16)
            act.dma_start(O[7][0, :, BUF - 1, g * P:(g + 1) * P], uso[0:NS, :]).then_inc(u_st, 16)
            act.wait_ge(pooled_done, g + 1)
            act_(plr[0], pooled).then_inc(pl_hi, 1)
            for c in range(2):
                ch = 2 * g + c
                if ch >= 2:
                    act.wait_ge(pool_st[c], 16 * g)
                for s in range(3):
                    n = 3 * ch + s
                    act.wait_ge(pool_ready, n + 1)
                    act_(poolo[c][:, s * PIECE:(s + 1) * PIECE], TB[n % 2][:, 0:PIECE], ACT.Copy, scale=pscale[:, ch:ch + 1])\
                        .then_inc(pool_out, 1)
                act.wait_ge(pool_out, 3 * ch + 3)
                act.dma_start(pool_d[ch], poolo[c]).then_inc(pool_st[c], 16)
        stage_end(act, 1)

        def split(h, c):
            act.wait_ge(w_landed[c % 2], landed_value(h, c))
            if c == 0:
                piece_ready.wait(act, h, -1)
            elif c == 1:
                piece_ready.wait(act, h, -4 if not isinstance(h, int) or h else -1)
            else:
                piece_ready.wait(act, h, 3 * (c - 2) + 2)
            sig(act_(whl[c % 2][0], wraw2[c % 2]), w_hi, h, c)

        def take(h, n):
            piece_ready.wait(act, h, n)
            s = n % 3
            cols = slice(s * PIECE, (s + 1) * PIECE)
            if n < 6:
                if n:
                    piece_rope.wait(act, h, n - 1)
                for g, src in enumerate((1, 0, 3, 2)):
                    last = act_(swp[32 * g:32 * g + 32, :], PB[32 * src:32 * src + 32, 0:PIECE])
                    if g == 3:
                        sig(last, swap_done, h, n)
                    else:
                        A(last)
            elif n < 9:
                sig(act_(v32[:, cols], PB[:, 0:PIECE]), piece_copied, h, n - 6)
            else:
                sig(act_(gate[(n - 9) // 3][:, cols], PB[:, 0:PIECE], ACT.Sigmoid), piece_copied, h, n - 6)

        def rows(h, n, first=False):
            kt_ready.wait(act, h, n)
            if n == 0 and not first:
                act.wait_ge(kout_st, h * 16)
                act.wait_ge(vout_st, h * 16)
                act.wait_ge(kvs_st, h * 32)
            if n < 4:
                dst = (kout, vt32)[n // 2]
                sig(act_(dst[:, 4 * (n % 2):4 * (n % 2) + 4, :], TB[n % 2][:, :].rearrange("p (a b) -> p a b", a=4)), kt_copied, h, n)
            if n == 1:
                act.dma_start(nk_p[0, :, :, bass.ds(h, 1), :].rearrange("p t a d -> p t (a d)"), kout).then_inc(kout_st, 16)
            if n == 3:
                act.dma_start(nv_p[0, :, :, bass.ds(h, 1), :].rearrange("p t a d -> p t (a d)"), vt32).then_inc(vout_st, 16)
            if n == 4:
                A(act_(kso[0:NS, :], TB[0][0:NS, 0:P]))
                sig(act_(vso[0:NS, :], TB[0][0:NS, P:2 * P]), kt_copied, h, 4)
                act.dma_start(nk_s[0, :, bass.ds(h, 1), :].rearrange("b a d -> b (a d)"), kso[0:NS, :]).then_inc(kvs_st, 16)
                act.dma_start(nv_s[0, :, bass.ds(h, 1), :].rearrange("b a d -> b (a d)"), vso[0:NS, :]).then_inc(kvs_st, 16)

        def operands_qk(h, first):
            if not first:
                s_ready.wait(act, h, -1)
            piece_rope.wait(act, h, 5)
            A(act_(qhl[0][0:HD, 0, :], q32[0:HD, 0:SEQ]))
            A(act_(qhl[0][HD:P, 1, :], q32[HD:P, 0:SEQ]))
            sig(act_(khl[0], k32[:, 0:SEQ]), qk_hi, h, 0)

        def operands_v(h, first):
            if not first:
                pv_done.wait(act, h, -1)
            sig(act_(vhl[0], vt32), v_hi, h, 0)

        def exps(h, i):
            L = (i + 1) * P
            smax.wait(act, h, i)
            A(act_(Pr[:, 0, 0:L], S[:, 0:L], ACT.Exp, scale=SCALE, bias=nmax[:, 0:1], accum_out=esum[:, 0:1]))
            sig(act_(Pr[:, 1, 0:L], S[:, SEQ:SEQ + L], ACT.Exp, scale=SCALE, bias=nmax[:, 1:2], accum_out=esum[:, 1:2]), exp_done, h, i)

        def groups(h, i):
            p = i // 2
            at = p * (p + 1) // 2
            for g in range(p + 1):
                n = at + g
                t_ready.wait(act, h, n)
                if n >= 2:
                    pv_done.wait(act, h, n - 2)
                sig(act_(wt[n % 2][0], TB[n % 2][:, :].rearrange("p (a b) -> p a b", a=2)), wt_hi, h, n)
            pv_done.wait(act, h, at + p)
            sig(act_(O32[:, 256 * p:256 * p + 256], OB[:, 0:256]), o_copied, h, p)

        def step(h, nxt, first):
            exps(h, 0)
            if nxt:
                split(h + 1, 0)
            for i in range(8):
                if nxt:
                    if i == 1:
                        split(h + 1, 1)
                    if i == 6:
                        split(h + 1, 3)
                    take(h + 1, i)
                    if i == 7:
                        take(h + 1, 8)
                if i == 2:
                    qbc_ready.wait(act, h, 0)
                if i % 2 == 0 and i:
                    groups(h, i - 1)
                if i < 7:
                    exps(h, i + 1)
                if i == 2:
                    smx_done.wait(act, h, 0)
                    sT_ready.wait(act, h, 0)
                    sig(act_(ps32[0:16, 0:PAST + 1], TB[1][0:16, 0:PAST + 1], ACT.Exp, scale=SCALE, bias=snm[0:16, :], accum_out=sss[0:16, :]), sexp_done, h, 0)
                if i == 3 and nxt:
                    split(h + 1, 2)
                if i == 6:
                    os_ready.wait(act, h, 0)
                    sig(act_(os32[0:NS, :], TB[0][0:NS, 0:P]), os_copied, h, 0)
            osT_ready.wait(act, h, 0)
            sig(act_(O32[:, SEQ:T], TB[0][:, 0:NS]), osT_copied, h, 0)
            if nxt:
                operands_qk(h + 1, False)
            groups(h, 7)
            comb.wait(act, h, 7)
            sig(act_(sq, O32, ACT.Square), sq_done, h, 0)
            if nxt:
                rows(h + 1, 0)
                rows(h + 1, 1)
            for s in range(3):
                ms_ready.wait(act, h, s)
                t_ready.wait(act, h, 9)
                sig(act_(rst[:, s * PIECE:(s + 1) * PIECE], Sb[s][:, 0:PIECE], ACT.Ln, scale=1.0 / P, bias=const("eps")), ln_done, h, s)
            sig(act_(rst, rst, ACT.Exp, scale=-0.5), rst_done, h, 0)
            if nxt:
                merged.wait(act, h, 0)
                take(h + 1, 9)
                rows(h + 1, 2)
                rows(h + 1, 3)
                split(h + 1, 4)
                take(h + 1, 10)
                rows(h + 1, 4)
                operands_v(h + 1, False)
                take(h + 1, 11)
            merged.wait(act, h, 1)
            act.dma_start(mg_d[bass.ds(h, 1), :, :].rearrange("a p n -> (a p) n"), poolc).then_inc(mg_st, 16)
            if nxt:
                for n in range(12, 15):
                    take(h + 1, n)

        for n in range(9):
            if n % 3 == 0:
                split(0, n // 3)
            take(0, n)
        split(0, 3)
        for n in range(5):
            rows(0, n, True)
        act.wait_ge(qzero, 4)
        operands_qk(0, True)
        operands_v(0, True)
        for n in range(9, 15):
            if n == 10:
                split(0, 4)
            take(0, n)
        n_a = A.n
        step(0, True, True)
        with A.loop(1, H - 1, A.n - n_a) as h:
            step(h, True, False)
        step(H - 1, False, False)
        act.wait_ge(kout_st, 16 * H)
        act.wait_ge(vout_st, 16 * H)
        act.wait_ge(kvs_st, 32 * H)
        stage_end(act, 2)

        for q in range(2):
            act.wait_ge(wo_landed, 16 * (q + 1))
            act_(wo[0][:, 4 * q:4 * q + 4, :], wo32).then_inc(wo_hi, 1)

        def tile3(n, b, rows, landed, i):
            act.wait_ge(m_landed[b], landed)
            if i:
                act.wait_ge(wout_ready, n - 1)
            act_(mhl[b][0][:, :, 0:rows], mt32[b][:, :, 0:rows]).then_inc(m_hi, 1)

        def norm3(n, b, rows):
            act.wait_ge(var_done, n + 1)
            act_(rstd1[0:rows, :], mv[0:rows, 1:2], ACT.Sqrt, bias=const("eps")[0:rows, :]).then_inc(std_done, 1)
            act.wait_ge(x1_ready, n + 1)
            act.dma_start(x1_d[bass.ds(n * P, rows), :], x1t[b][0:rows, :]).then_inc(x1_st[b], 16)
            act.wait_ge(h2_done, n + 1)
            act.dma_start(h2_d[bass.ds(n * P, rows), :], h2t[b][0:rows, :]).then_inc(h2_st[b], 16)
            act.wait_ge(h2T_ready, n + 1)
            if not (isinstance(n, int) and n == 0):
                act.wait_ge(rl_ready, n)
            A(act_(h2T[:, 0:4, 0:rows], TB[0][:, :].rearrange("p (a b) -> p a b", a=4)[:, :, 0:rows]))
            act_(h2T[:, 4:8, 0:rows], TB[1][:, :].rearrange("p (a b) -> p a b", a=4)[:, :, 0:rows]).then_inc(h2T_copied, 1)

        tile3(0, 0, P, 32, False)
        tile3(1, 1, P, 32, False)
        norm3(0, 0, P)
        with A.loop(1, NT // 2, 2) as i:
            tile3(i * 2, 0, P, i * 32 + 32, True)
            norm3(i * 2 - 1, 1, P)
            tile3(i * 2 + 1, 1, P, i * 32 + 32, True)
            norm3(i * 2, 0, P)
        tile3(NT, 0, NS, 32 * 5, True)
        norm3(NT - 1, 1, P)
        norm3(NT, 0, NS)
        act.wait_ge(route_exp, 1)
        act_(rt36[0], rt36[1], ACT.Exp).then_inc(route_exp_done, 1)
        act.wait_ge(route_exp, 2)
        act_(r9[2], r9[3], ACT.Exp).then_inc(route_exp_done, 1)
        act.wait_ge(route_exp_done, 2)
        act.wait_ge(h2T_copied, 9)
        stage_end(act, 3)

        def gate_up_hi(n, b, landed):
            act.wait_ge(e_landed[b], landed)
            for q in range(2):
                k = slice(4 * q, 4 * q + 4)
                act_(gu[b][0][:, k, 0:FF], raw_g[b][:, k, :]).then_inc(g_hi, 1)
                act_(gu[b][0][:, k, FF:2 * FF], raw_u[b][:, k, :]).then_inc(g_hi, 1)

        def silu4(n, b, later):
            act.wait_ge(gu_used, n + 1)
            if later:
                act.wait_ge(av_done, n)
            act_(silu, Sb[b][:, 0:FF], ACT.Silu).then_inc(silu_ok, 1)

        def rows_out(n, b, st):
            act.wait_ge(dn_used, n + 1)
            if st is not None:
                act.wait_ge(y_st[b], st)
            act_(yv[b], S[:, 1024:2048]).then_inc(y_copied, 1)
            act.wait_ge(y_copied, n + 1)
            act.dma_start(y_d[bass.ds(n * P, P), :], yv[b]).then_inc(y_st[b], 16)

        def act_hi(n, later):
            act.wait_ge(avT_ready, n + 1)
            if later:
                act.wait_ge(dn_used, n)
            act_(aT[0], PB[:, 0:FF].rearrange("p (a b) -> p a b", a=2)).then_inc(avT_hi, 1)

        def rows_hi(n, b):
            for q in range(2):
                act.wait_ge(xgT_ready, n * 2 + (q + 1))
                act_(hg[b][0][:, 4 * q:4 * q + 4, :], TB[q][:, :].rearrange("p (a b) -> p a b", a=4)).then_inc(hg_hi, 1)

        def down_hi(n, b, landed, later):
            act.wait_ge(d_landed[b], landed)
            if later:
                act.wait_ge(dn_used, n - 1)
            for c in range(2):
                act_(dn[b][0][:, c, :], raw_d[b][:, c, :]).then_inc(dn_hi, 1)

        def tile4(n, b, i, before, more=True):
            if more:
                rows_hi(n + 1, 1 - b)
            if before >= 1:
                act_hi(n - 1, before >= 2)
            if before >= 2:
                rows_out(n - 2, b, i * 16)
            if more:
                gate_up_hi(n + 1, 1 - b, i * 32 + 32 * (1 + b))
            silu4(n, b, before >= 1)
            down_hi(n, b, i * 16 + 16, before >= 2)

        for b in range(2):
            act.sem_inc(y_st[b], 16)
        gate_up_hi(0, 0, 32)
        rows_hi(0, 0)
        tile4(0, 0, 0, 0)
        tile4(1, 1, 0, 1)
        with act.Fori(1, SLOT_TILES // 2 - 1) as i:
            for b in range(2):
                tile4(i * 2 + b, b, i, 2)
        tile4(SLOT_TILES - 2, 0, SLOT_TILES // 2 - 1, 2)
        tile4(SLOT_TILES - 1, 1, SLOT_TILES // 2 - 1, 2, more=False)
        act_hi(SLOT_TILES - 1, True)
        rows_out(SLOT_TILES - 2, 0, 16 * (SLOT_TILES // 2))
        rows_out(SLOT_TILES - 1, 1, 16 * (SLOT_TILES // 2))
        stage_end(act, 4)

        for t in range(NT + 1):
            rows = P if t < NT else NS
            act.wait_ge(var_done, NT + 1 + t + 1)
            act_(rstd1[0:rows, :], mv[0:rows, 1:2], ACT.Sqrt, bias=const("eps")[0:rows, :]).then_inc(std_done, 1)
            act.wait_ge(out_ready, t + 1)
            act.dma_start(y_p[t * P:(t + 1) * P, :] if t < NT else y_s, o5[t % 2][0:rows, :]).then_inc(out_st[t % 2], 16)

    @block.vector
    def _(dve):
        V = Chain(dve, v_chain)
        TT, TS, STT = nc.vector.tensor_tensor, nc.vector.tensor_scalar, nc.vector.scalar_tensor_tensor

        def sig(ins, event, h, k):
            ins.then_inc(event.sem, 1)
            event.wait(dve, h, k)

        def mark(ins, semaphore, value):
            ins.then_inc(semaphore, 1)
            dve.wait_ge(semaphore, value)

        def rsum(out, in_):
            return nc.vector.tensor_reduce(out, in_, AX.X, ALU.add)

        def rmax(out, in_):
            return nc.vector.tensor_reduce(out, in_, AX.X, ALU.max)

        dve.wait_ge(ld_c, 48)
        V(nc.vector.tensor_copy(maskb[:, :], const("mask")))
        V(nc.vector.tensor_copy(identb[:, :], ident))
        V(nc.vector.tensor_copy(trib[:, :], const("tri")))
        V(nc.vector.tensor_copy(onesb[:, :], ones))
        dve.wait_ge(cT_done, 1)
        nc.vector.tensor_copy(sTc, TB[0][:, 0:72].rearrange("p (a b) -> p a b", a=8)).then_inc(cT_copied, 1)

        def ada_rows(n, b, st):
            dve.wait_ge(ada_done, n + 1)
            if st is not None:
                dve.wait_ge(ada_st[b], st)
            mark(TT(modrow[b][0:9, 0:AW], Sb[b][0:9, 0:AW], badab[b][0:9, 0:AW], ALU.add), ada_row, n + 1)

        for n in range(8):
            ada_rows(n, n % 2, 16 * (n // 2) if n >= 2 else None)
            dve.wait_ge(modT_done, n + 1)
            mark(nc.vector.tensor_copy(modT[:, 2 * n:2 * n + 2, :], TB[1][:, 0:18].rearrange("p (a b) -> p a b", a=2)),
                 modT_copied, n + 1)
        mark(TS(modT[:, 8:16, :], modT[:, 8:16, :], 1.0, None, ALU.add), modT_copied, 9)
        with dve.Fori(0, (NADA - 8) // 2) as i:
            for b in range(2):
                ada_rows(i * 2 + (8 + b), b, i * 16 + 64)
        def h_rest(n):
            k, q = n // 2, n % 2
            cols = slice(512 * q, 512 * q + 512)
            dve.wait_ge(h_hi, n + 1)
            mark(TT(hT[1][:, k, cols], h32[n % 2], hT[0][:, k, cols].bitcast(F32), ALU.subtract), h_lo, n + 1)

        for n in range(16):
            k = n // 2
            dve.wait_ge(xT_done, n + 1)
            mark(TS(h32[n % 2], TB[n % 2][:, :], modT[:, 8 + k, 0:1], modT[:, k, 0:1], ALU.mult, ALU.add), h_full, n + 1)
            if n:
                h_rest(n - 1)
        h_rest(15)
        dve.wait_ge(xT_done, 17)
        V(TT(hs32, OB[:, 0:64].rearrange("p (k b) -> p k b", k=8), modT[:, 8:16, 1:9], ALU.mult))
        mark(TT(hs32, hs32, modT[:, 0:8, 1:9], ALU.add), hs_ready, 1)
        dve.wait_ge(h_hi, 17)
        V(TT(hT[1][:, :, SEQ:T], hs32, hT[0][:, :, SEQ:T].bitcast(F32), ALU.subtract))
        dve.wait_ge(ld_small, 16 * 8)
        V(TT(lamv[:, 0, :], lamv[:, 0, :], lamv[:, 1, :], ALU.mult))
        V(TT(lamv[:, 1, :], lamv[:, 2, :], lamv[:, 3, :], ALU.mult))
        mark(rsum(lamt[:, 2:4], lamv[:, 0:2, :]), lam_sum, 1)
        dve.wait_ge(lam_exp, 1)
        V(TT(neglam, lamt[:, 1:2], lamt[:, 0:1], ALU.subtract))
        V(TS(neglam, neglam, LAM_INIT, None, ALU.subtract))
        V(TT(coef, const("coef_b"), neglam, ALU.mult))
        V(TT(coef, coef, const("coef_a"), ALU.add))
        V(TS(sublng, sublng, 1.0 - LAM_INIT, None, ALU.mult))
        stage_end(dve, 0)

        V(nc.vector.memset(ubuf[:, 0:16], 0.0))
        V(nc.vector.memset(sA[:, 0:16], 0.0))
        V(nc.vector.memset(sB[:, 0:16], 0.0))
        dve.wait_ge(stT_ready, 1)
        mark(nc.vector.tensor_copy(stall, TB[0][:, 0:480].rearrange("p (g n) -> p g n", g=4)), stT_copied, 1)
        for g, win in enumerate(WIN):
            dve.wait_ge(w_landed[g % 2], 16 * (g // 2 + 1))
            w_hi.wait_first(dve, g)
            TT(whl[g % 2][1], wraw[g % 2], whl[g % 2][0].bitcast(F32), ALU.subtract).then_inc(w_lo.sem, 1)
            w_lo.wait_first(dve, g)
            dve.wait_ge(pl_hi, 2 * g + 1)
            mark(TT(wpr[1], wp32, wpr[0].bitcast(F32), ALU.subtract), pool_split, 2 * g + 1)
            piece_copied.wait_first(dve, 3 * g + 2)
            cur = ubuf
            for l in range(g + 1):
                w, dst = 1 << l, (sA, sB)[l % 2]
                V(TT(dst[:, 16:16 + SEQ], cur[:, 16:16 + SEQ], cur[:, 16 - w:16 - w + SEQ], ALU.add))
                cur = dst
            V(TT(cur[:, 16:32], cur[:, 16:32], const("corr")[:, 16 * g:16 * g + 16], ALU.mult))
            V(STT(out=pooled[:, 0:SEQ], in0=cur[:, 16:16 + SEQ], scalar=1.0 / win, in1=ubuf[:, 16:16 + SEQ], op0=ALU.mult, op1=ALU.subtract))
            V(rsum(ssum, stall[:, g, :].rearrange("p (b r) -> p b r", b=NS)[:, :, 16 - win:BUF]))
            us = ubuf[:, 16 + SEQ:16 + T]
            V(TT(ssum, ssum, us, ALU.add))
            mark(STT(out=pooled[:, SEQ:T], in0=ssum, scalar=1.0 / win, in1=us, op0=ALU.mult, op1=ALU.subtract), pooled_done, g + 1)
            dve.wait_ge(pl_hi, 2 * g + 2)
            mark(TT(plr[1], pooled, plr[0].bitcast(F32), ALU.subtract), pool_split, 2 * g + 2)
        stage_end(dve, 1)

        def split(h, c):
            dve.wait_ge(w_landed[c % 2], landed_value(h, c))
            w_hi.wait(dve, h, c)
            sig(TT(whl[c % 2][1], wraw2[c % 2], whl[c % 2][0].bitcast(F32), ALU.subtract), w_lo, h, c)

        def rope(h, n, first):
            if not first:
                if n == 0:
                    qk_hi.wait(dve, h, -1)
                if n == 3:
                    kt_ready.wait(dve, h, -1)
            cols = slice((n % 3) * PIECE, (n % 3 + 1) * PIECE)
            dst = (q32, k32)[n // 3][:, cols]
            swap_done.wait(dve, h, n)
            V(TT(dst, PB[:, 0:PIECE], cosT[:, cols], ALU.mult))
            V(TT(swp, swp, sinT[:, cols], ALU.mult))
            sig(TT(dst, dst, swp, ALU.add), piece_rope, h, n)

        def operands_qk(h):
            qk_hi.wait(dve, h, 0)
            V(TT(qhl[1][0:HD, 0, :], q32[0:HD, 0:SEQ], qhl[0][0:HD, 0, :].bitcast(F32), ALU.subtract))
            V(TT(qhl[1][HD:P, 1, :], q32[HD:P, 0:SEQ], qhl[0][HD:P, 1, :].bitcast(F32), ALU.subtract))
            sig(TT(khl[1], k32[:, 0:SEQ], khl[0].bitcast(F32), ALU.subtract), qk_lo, h, 0)
            V(nc.vector.tensor_copy(qs, q32[:, SEQ:T]))
            V(nc.vector.tensor_copy(ks, k32[:, SEQ:T]))

        def operands_v(h):
            v_hi.wait(dve, h, 0)
            sig(TT(vhl[1], vt32, vhl[0].bitcast(F32), ALU.subtract), v_lo, h, 0)

        def sample_queries(h):
            sig(TT(Bd, ident.rearrange("p (o f) -> p o f", o=1).to_broadcast([P, 8, P]),
                   qs.rearrange("p (b o) -> p b o", o=1).to_broadcast([P, 8, P]), ALU.mult), bd_done, h, 0)

        def maxima(h, i):
            L = (i + 1) * P
            s_ready.wait(dve, h, i)
            V(rmax(nmax, S[:, :].rearrange("p (m n) -> p m n", m=2)[:, :, 0:L]))
            sig(TS(nmax, nmax, -SCALE, None, ALU.mult), smax, h, i)

        def combine(h, i):
            L = (i + 1) * P
            exp_done.wait(dve, h, i)
            V(nc.vector.reciprocal(resum, esum))
            V(TT(resum[:, 1:2], resum[:, 1:2], neglam, ALU.mult))
            if i % 2 == 0:
                p = i // 2
                if p:
                    t_ready.wait(dve, h, p * (p + 1) // 2 - 1)
                V(nc.vector.memset(Wt[:, 0, L:L + P], 0.0))
            w = Wt[:, i % 2, 0:L]
            V(TS(w, Pr[:, 0, 0:L], resum[:, 0:1], None, ALU.mult))
            sig(STT(out=w, in0=Pr[:, 1, 0:L], scalar=resum[:, 1:2], in1=w, op0=ALU.mult, op1=ALU.add), comb, h, i)

        def groups(h, i):
            p = i // 2
            at = p * (p + 1) // 2
            for g in range(p + 1):
                n = at + g
                wt_hi.wait(dve, h, n)
                sig(TT(wt[n % 2][1], TB[n % 2][:, :].rearrange("p (a b) -> p a b", a=2), wt[n % 2][0].bitcast(F32), ALU.subtract), wt_lo, h, n)

        def page_scores(h):
            qbc_ready.wait(dve, h, 0)
            dve.wait_ge(k_landed, (h + 1) * 256)
            for q in range(2):
                kv = KV[:, 8 * q:8 * q + 8, :].rearrange("p (b j) f -> p b j f", j=2)
                qb = TB[q][:, :].rearrange("p (b o f) -> p b o f", b=4, o=1).to_broadcast([P, 4, 2, P])
                V(TT(kv, kv, qb, ALU.mult))
            for j in range(PAGES):
                V(rsum(sT[:, j, :].rearrange("p (b m) -> p b m", m=2),
                       KV.rearrange("p (b j) (m d) -> p b j m d", j=2, m=2)[:, :, j]))
            V(TT(qs, qs, ks, ALU.mult))
            sig(TT(sE, qs.rearrange("p (b o) -> p b o", o=1).to_broadcast([P, 8, 2]),
                   const("half").rearrange("p (o m) -> p o m", o=1).to_broadcast([P, 8, 2]), ALU.mult), sT_done, h, 0)

        def page_max(h):
            sT_ready.wait(dve, h, 0)
            V(rmax(snm[0:16, :], TB[1][0:16, 0:PAST + 1]))
            sig(TS(snm[0:16, :], snm[0:16, :], -SCALE, None, ALU.mult), smx_done, h, 0)

        def page_weights(h):
            sexp_done.wait(dve, h, 0)
            V(nc.vector.reciprocal(srs[0:16, :], sss[0:16, :]))
            V(TT(srs[0:16, :], srs[0:16, :], coef[0:16, :], ALU.mult))
            sig(TS(ps32[0:16, 0:PAST + 1], ps32[0:16, 0:PAST + 1], srs[0:16, :], None, ALU.mult), pn_done, h, 0)

        def page_columns(h):
            pnT_ready.wait(dve, h, 0)
            V(rsum(wsum.rearrange("p j b -> p (j b)"), TB[1][:, 0:32].rearrange("p (n m) -> p n m", m=2)))
            V(TT(W8.rearrange("p (b j) c -> p b j c", j=2),
                 const("delta").rearrange("p (b o c) -> p b o c", b=8, o=1).to_broadcast([P, 8, 2, 8]),
                 wsum.rearrange("p j (b o) -> p b j o", o=1).to_broadcast([P, 8, 2, 8]), ALU.mult))
            sig(TS(dgw[0:NS, :], ident[0:NS, 0:NS], TB[1][0:NS, 32:33], None, ALU.mult), w8_done, h, 0)

        def merge_gates(h):
            sq_done.wait(dve, h, 0)
            osT_copied.wait(dve, h, 0)
            piece_copied.wait(dve, h, 8)
            dve.wait_ge(poolc_landed, (h + 1) * 16)
            V(STT(out=O32, in0=O32, scalar=sublng, in1=gate[1], op0=ALU.mult, op1=ALU.mult))
            sig(TT(poolc, poolc, gate[0], ALU.mult), merged, h, 0)

        def merge(h):
            rst_done.wait(dve, h, 0)
            V(TT(O32, O32, rst, ALU.mult))
            sig(TT(poolc, poolc, O32, ALU.add), merged, h, 1)

        def step(h, nxt):
            maxima(h, 0)
            if nxt:
                split(h + 1, 0)
            for i in range(8):
                if nxt:
                    if i == 1:
                        split(h + 1, 1)
                    if i == 6:
                        split(h + 1, 3)
                if i % 2 == 0 and i:
                    groups(h, i - 1)
                combine(h, i)
                if i < 6 and nxt:
                    rope(h + 1, i, False)
                if i < 7:
                    maxima(h, i + 1)
                if i == 0:
                    page_scores(h)
                if i == 2:
                    page_max(h)
                if i == 3:
                    page_weights(h)
                    if nxt:
                        split(h + 1, 2)
                if i == 4:
                    page_columns(h)
            if nxt:
                operands_qk(h + 1)
            groups(h, 7)
            merge_gates(h)
            merge(h)
            if nxt:
                split(h + 1, 4)
                operands_v(h + 1)
                sample_queries(h + 1)

        for q in range(2):
            nc.vector.memset(qhl[q][HD:P, 0, :].bitcast(F32), 0.0).then_inc(qzero, 1)
            nc.vector.memset(qhl[q][0:HD, 1, :].bitcast(F32), 0.0).then_inc(qzero, 1)
        dve.wait_ge(qzero, 4)
        split(0, 0)
        for n in range(6):
            if n == 3:
                split(0, 1)
            rope(0, n, True)
        split(0, 2)
        split(0, 3)
        operands_qk(0)
        operands_v(0)
        split(0, 4)
        sample_queries(0)
        n_v = V.n
        step(0, True)
        with V.loop(1, H - 1, V.n - n_v) as h:
            step(h, True)
        step(H - 1, False)
        stage_end(dve, 2)

        for q in range(2):
            dve.wait_ge(wo_hi, q + 1)
            mark(TT(wo[1][:, 4 * q:4 * q + 4, :], wo32, wo[0][:, 4 * q:4 * q + 4, :].bitcast(F32), ALU.subtract), wo_lo, q + 1)
        dve.wait_ge(tab_landed, 16 * 9)
        V(TS(g1b, g1b, 1.0, None, ALU.add))
        V(TS(sc2b, sc2b, 1.0, None, ALU.add))
        V(nc.vector.memset(rlv, 0.0))

        def m_rest(n, b, rows, later):
            dve.wait_ge(m_hi, n + 1)
            if later:
                dve.wait_ge(wout_ready, n - 1)
            mark(TT(mhl[b][1][:, :, 0:rows], mt32[b][:, :, 0:rows], mhl[b][0][:, :, 0:rows].bitcast(F32), ALU.subtract), m_lo, n + 1)

        def layer_norm(y, rows, var, std, n, gain, bias, out):
            for q in range(2):
                V(nc.vector.bn_stats(stat[0:rows, q, :], y[0:rows, 512 * q:512 * q + 512]))
            apart(dve)
            mark(nc.vector.bn_aggr(mv[0:rows, :], stat[0:rows, :, :].rearrange("p a b -> p (a b)")), var, n + 1)
            dve.wait_ge(std, n + 1)
            V(nc.vector.reciprocal(rstd1[0:rows, :], rstd1[0:rows, :]))
            V(TS(y[0:rows, :], y[0:rows, :], mv[0:rows, 0:1], rstd1[0:rows, :], ALU.subtract, ALU.mult))
            V(TT(y[0:rows, :], y[0:rows, :], gain[0:rows, :], ALU.mult))
            return TT(out[0:rows, :], y[0:rows, :], bias[0:rows, :], ALU.add)

        def norm3(n, b, rows, before):
            dve.wait_ge(wout_ready, n + 1)
            mark(TT(y3[0:rows, :], S[0:rows, 1024 * b:1024 * b + 1024], g1b[0:rows, :], ALU.mult), wout_used, n + 1)
            V(STT(out=y3[0:rows, :], in0=x3[b][0:rows, :], scalar=ALPHA, in1=y3[0:rows, :], op0=ALU.mult, op1=ALU.add))
            if before is not None:
                dve.wait_ge(x1_st[b], before * 16)
                dve.wait_ge(h2_st[b], before * 16)
                dve.wait_ge(h2T_ready, n - 1)
            mark(layer_norm(y3, rows, var_done, std_done, n, l1g, l1b, x1t[b]), x1_ready, n + 1)
            V(TT(h2t[b][0:rows, :], x1t[b][0:rows, :], sc2b[0:rows, :], ALU.mult))
            mark(TT(h2t[b][0:rows, :], h2t[b][0:rows, :], sh2b[0:rows, :], ALU.add), h2_done, n + 1)

        def logits(n, rows):
            dve.wait_ge(rl_ready, n + 1)
            mark(TT(rlv[0:rows, bass.ds(n, 1), :].rearrange("p a n -> p (a n)"), PB[0:rows, 0:20], brg[0:rows, :], ALU.add), rl_used, n + 1)

        m_rest(0, 0, P, False)
        m_rest(1, 1, P, False)
        norm3(0, 0, P, None)
        m_rest(2, 0, P, True)
        norm3(1, 1, P, None)
        logits(0, P)
        m_rest(3, 1, P, True)
        norm3(2, 0, P, 1)
        logits(1, P)
        n_v = V.n
        def turn3(i):
            m_rest(i * 2, 0, P, True)
            norm3(i * 2 - 1, 1, P, i - 1)
            logits(i * 2 - 2, P)
            m_rest(i * 2 + 1, 1, P, True)
            norm3(i * 2, 0, P, i)
            logits(i * 2 - 1, P)
        with V.loop(2, NT // 2, 2 * 7) as i:
            turn3(i)
        m_rest(NT, 0, NS, True)
        norm3(NT - 1, 1, P, 3)
        logits(NT - 2, P)
        dve.wait_ge(tab_landed, 16 * 12)
        V(TS(g1b[0:NS, :], g1b[0:NS, :], 1.0, None, ALU.add))
        V(TS(sc2b[0:NS, :], sc2b[0:NS, :], 1.0, None, ALU.add))
        norm3(NT, 0, NS, 4)
        logits(NT - 1, P)
        logits(NT, NS)

        def bc(a, n):
            return a.rearrange("p (t o) -> p t o", o=1).to_broadcast([P, 9, n])

        dec = const("dec").rearrange("p (o n) -> p o n", o=1).to_broadcast([P, 9, 4])

        def first_max(values, m, scratch, hot):
            V(rmax(m, values))
            V(TT(scratch, values, bc(m, 4), ALU.is_equal))
            V(TT(scratch, scratch, dec, ALU.mult))
            V(rmax(r9[1], scratch))
            V(TT(hot, scratch, bc(r9[1], 4), ALU.is_equal))

        gl = rlv[:, :, 0:4]
        first_max(gl, r9[0], rt36[0], oh_g)
        mark(TT(rt36[1], gl, bc(r9[0], 4), ALU.subtract), route_exp, 1)
        hg44 = oh_g.rearrange("p t (g o) -> p t g o", o=1).to_broadcast([P, 9, 4, 4])
        M14 = M1.rearrange("p t (g e) -> p t g e", g=4)
        M24 = M2.rearrange("p t (g e) -> p t g e", g=4)
        for t in range(9):
            V(TT(M14[:, t], rlv[:, t, 4:20].rearrange("p (g e) -> p g e", g=4), hg44[:, t], ALU.mult))
        V(rsum(esel, M1.rearrange("p t (g e) -> p t e g", g=4)))
        first_max(esel, r9[2], oh2, oh1)
        V(STT(out=esel, in0=oh1, scalar=-BIG, in1=esel, op0=ALU.mult, op1=ALU.add))
        first_max(esel, r9[3], slotf[:, :, 0:4], oh2)
        mark(TT(r9[3], r9[3], r9[2], ALU.subtract), route_exp, 2)
        for t in range(9):
            V(TT(M14[:, t], hg44[:, t], oh1[:, t, :].rearrange("p (o e) -> p o e", o=1).to_broadcast([P, 4, 4]), ALU.mult))
            V(TT(M24[:, t], hg44[:, t], oh2[:, t, :].rearrange("p (o e) -> p o e", o=1).to_broadcast([P, 4, 4]), ALU.mult))
        V(TT(M12, M1, M2, ALU.add))
        mark(TT(Mb[:, :].rearrange("p (t e) -> p t e", t=9), M12, bc(const("valid"), 16), ALU.mult), m_mask, 1)
        dve.wait_ge(route_exp_done, 2)
        V(rsum(r9[0], rt36[0]))
        V(TS(r9[3], r9[2], 1.0, None, ALU.add))
        V(TT(r9[0], r9[0], r9[3], ALU.mult))
        V(nc.vector.reciprocal(w1c[:, :], r9[0]))
        V(TT(w2c[:, :], w1c[:, :], r9[2], ALU.mult))
        V(nc.vector.memset(pref[:, 0, :], 0.0))
        V(nc.vector.memset(base[:, 0:1], 0.0))
        dve.wait_ge(pos_ready, 1)
        for t in range(9):
            V(TT(pref[:, t + 1, :], pref[:, t, :], TB[1][:, 16 * t:16 * t + 16], ALU.add))
        V(TS(cnti[:, :], pref[:, 9, :], float(P - 1), None, ALU.add))
        V(TS(cnti[:, :], cnti[:, :], 7, 7, ALU.arith_shift_right, ALU.logical_shift_left))
        V(nc.vector.tensor_copy(cnt, cnti[:, :]))
        for e in range(NE):
            V(TT(base[:, e + 1:e + 2], base[:, e:e + 1], cnt[:, e:e + 1], ALU.add))
        V(TT(slotf, TB[0][:, 0:144].rearrange("p (t e) -> p t e", t=9), pref[:, 0:9, :], ALU.add))
        V(TT(slotf, slotf, base[:, 0:16].rearrange("p (o e) -> p o e", o=1).to_broadcast([P, 9, 16]), ALU.add))
        V(TT(M1, M1, slotf, ALU.mult))
        V(TT(M2, M2, slotf, ALU.mult))
        V(rsum(r9[0], M1))
        V(rsum(r9[1], M2))
        V(nc.vector.tensor_copy(slot[0][:, :], r9[0]))
        V(nc.vector.tensor_copy(slot[1][:, :], r9[1]))
        mark(nc.vector.tensor_copy(toku[:, :], const("tok")), slots_done, 1)
        V(TT(tef, base[:, 1:17].rearrange("p (o e) -> p o e", o=1).to_broadcast([P, 32, 16]),
             const("start").rearrange("p (j o) -> p j o", o=1).to_broadcast([P, 32, 16]), ALU.is_le))
        V(rsum(te32, tef))
        V(TS(te[:, :], te32[0:1, :], float(NE - 1), None, ALU.min))
        stage_end(dve, 3)

        def gate_lo(n, b):
            for q in range(2):
                k = slice(4 * q, 4 * q + 4)
                dve.wait_ge(g_hi, n * 4 + (2 * q + 1))
                TT(gu[b][1][:, k, 0:FF], raw_g[b][:, k, :], gu[b][0][:, k, 0:FF].bitcast(F32), ALU.subtract).then_inc(g_lo, 1)

        def gated(n, b, later):
            dve.wait_ge(silu_ok, n + 1)
            if later:
                dve.wait_ge(avT_ready, n)
            TT(av, silu, Sb[b][:, FF:2 * FF], ALU.mult).then_inc(av_done, 1)

        def act_lo(n):
            dve.wait_ge(avT_hi, n + 1)
            TT(aT[1], PB[:, 0:FF].rearrange("p (a b) -> p a b", a=2), aT[0].bitcast(F32), ALU.subtract).then_inc(avT_lo, 1)

        def rows_lo(n, b):
            for q in range(2):
                dve.wait_ge(hg_hi, n * 2 + (q + 1))
                TT(hg[b][1][:, 4 * q:4 * q + 4, :], TB[q][:, :].rearrange("p (a b) -> p a b", a=4),
                   hg[b][0][:, 4 * q:4 * q + 4, :].bitcast(F32), ALU.subtract).then_inc(hg_lo, 1)

        def down_lo(n, b):
            for c in range(2):
                dve.wait_ge(dn_hi, n * 2 + (c + 1))
                TT(dn[b][1][:, c, :], raw_d[b][:, c, :], dn[b][0][:, c, :].bitcast(F32), ALU.subtract).then_inc(dn_lo, 1)

        def tile4(n, b, before, more=True):
            if more:
                rows_lo(n + 1, 1 - b)
            if before >= 1:
                act_lo(n - 1)
            if more:
                gate_lo(n + 1, 1 - b)
            gated(n, b, before >= 1)
            down_lo(n, b)

        gate_lo(0, 0)
        rows_lo(0, 0)
        tile4(0, 0, 0)
        tile4(1, 1, 1)
        with dve.Fori(1, SLOT_TILES // 2 - 1) as i:
            for b in range(2):
                tile4(i * 2 + b, b, 2)
        tile4(SLOT_TILES - 2, 0, 2)
        tile4(SLOT_TILES - 1, 1, 2, more=False)
        act_lo(SLOT_TILES - 1)
        stage_end(dve, 4)

        dve.wait_ge(tab5, 48)
        V(TS(g2b, g2b, 1.0, None, ALU.add))
        for t in range(NT + 1):
            b, rows = t % 2, P if t < NT else NS
            if t == NT:
                dve.wait_ge(tab5, 64)
                V(TS(g2b[0:NS, :], g2b[0:NS, :], 1.0, None, ALU.add))
            dve.wait_ge(y5_landed[b], 32 * (t // 2 + 1))
            V(TS(m5[0:rows, :], ya[b][0:rows, :], w1c[0:rows, t:t + 1], None, ALU.mult))
            V(STT(out=m5[0:rows, :], in0=yb[b][0:rows, :], scalar=w2c[0:rows, t:t + 1], in1=m5[0:rows, :], op0=ALU.mult, op1=ALU.add))
            V(TT(m5[0:rows, :], m5[0:rows, :], g2b[0:rows, :], ALU.mult))
            dve.wait_ge(x5_landed[b], 16 * (t // 2 + 1))
            mark(STT(out=m5[0:rows, :], in0=x5[b][0:rows, :], scalar=ALPHA, in1=m5[0:rows, :], op0=ALU.mult, op1=ALU.add), m5_used, t + 1)
            if t >= 2:
                dve.wait_ge(out_st[b], 16 * (t // 2))
            mark(layer_norm(m5, rows, var_done, std_done, NT + 1 + t, l2g, l2b, o5[b]), out_ready, t + 1)

    @block.gpsimd
    def _(pool):
        stage_end(pool, 0)
        stage_end(pool, 1)
        stage_end(pool, 2)
        pool.wait_ge(wo_lo, 2)
        nc.gpsimd.memset(tokz, 0.0).then_inc(zero_done, 1)
        pool.wait_ge(zero_done, 1)
        pool.dma_start(tok_d.rearrange("(p n) o -> p (n o)", p=P), tokz.bitcast(U32)).then_inc(zero_st, 16)
        pool.wait_ge(zero_st, 16)
        pool.wait_ge(slots_done, 1)
        for t in range(NT + 1):
            rows = P if t < NT else NS
            for c in range(2):
                nc.gpsimd.indirect_dma_start(
                    out=tok_d, out_offset=bass.IndirectOffsetOnAxis(ap=slot[c][0:rows, t:t + 1], axis=0),
                    in_=toku[0:rows, t:t + 1], in_offset=None).then_inc(tok_st, 16)
        stage_end(pool, 3)

        def gather(n, b, landed, later):
            pool.wait_ge(idx_landed[b], landed)
            if later:
                pool.wait_ge(xgT_ready, n * 2 - 2)
                apart(pool)
            nc.gpsimd.indirect_dma_start(
                out=xg[b], out_offset=None, in_=h2_d,
                in_offset=bass.IndirectOffsetOnAxis(ap=idx[b][:, 0:1], axis=0)).then_inc(xg_landed[b], 16)

        def up_lo(n, b):
            for q in range(2):
                k = slice(4 * q, 4 * q + 4)
                pool.wait_ge(g_hi, n * 4 + (2 * q + 2))
                nc.gpsimd.tensor_tensor(gu[b][1][:, k, FF:2 * FF], raw_u[b][:, k, :], gu[b][0][:, k, FF:2 * FF].bitcast(F32), ALU.subtract)\
                    .then_inc(u_lo, 1)

        gather(0, 0, 16, False)
        gather(1, 1, 16, False)
        up_lo(0, 0)
        gather(2, 0, 32, True)
        up_lo(1, 1)
        with pool.Fori(1, SLOT_TILES // 2 - 1) as i:
            for b in range(2):
                gather(i * 2 + (b + 1), 1 - b, i * 16 + 16 * (b + 1), True)
                up_lo(i * 2 + b, b)
        gather(SLOT_TILES - 1, 1, 16 * (SLOT_TILES // 2), True)
        up_lo(SLOT_TILES - 2, 0)
        up_lo(SLOT_TILES - 1, 1)
        stage_end(pool, 4)

        for t in range(NT + 1):
            b, rows = t % 2, P if t < NT else NS
            if t >= 2:
                pool.wait_ge(m5_used, t - 1)
            for c, dst in enumerate((ya, yb)):
                nc.gpsimd.indirect_dma_start(
                    out=dst[b][0:rows, :], out_offset=None, in_=y_d,
                    in_offset=bass.IndirectOffsetOnAxis(ap=slot[c][0:rows, t:t + 1], axis=0)).then_inc(y5_landed[b], 16)


INS = ["x_prompt", "x_sample", "cache_k", "cache_v", "state_pool", "page_table", "c_prompt", "c_sample",
       "w_ada", "b_ada", "w_in", "lambda_q1", "lambda_k1", "lambda_q2", "lambda_k2", "subln_g",
       "w_pool", "pool_scale", "w_out", "ln1_g", "ln1_b",
       "w_group", "b_group", "w_router", "b_router", "w_e_gate", "w_e_up", "w_e_down", "ln2_g", "ln2_b"]
OUTS = [(1, SEQ, D), (NS, 1, D), (1, 1, SEQ, H, 2, HD), (1, 1, SEQ, H, P), (1, 1, BUF, 512),
        (1, NS, 1, H, 2, HD), (1, NS, 1, H, P), (1, NS, BUF, 512)]


def kernel(**inputs):
    import concourse.bacc as bacc
    from concourse.bass_utils import run_bass_kernel_spmd as run

    nc = bacc.Bacc("TRN2", target_bir_lowering=False, num_devices=1)
    arrays, ins = {}, {}
    cst, rope = constants()
    for name in INS + ["cst", "rope"]:
        a = np.ascontiguousarray(cst if name == "cst" else rope if name == "rope" else inputs[name])
        arrays[f"in_{name}"] = a
        ins[name] = nc.dram_tensor(f"in_{name}", a.shape, mybir.dt.from_np(a.dtype), kind="ExternalInput").ap()
    outs = [nc.dram_tensor(f"out_{i}", shape, F32, kind="ExternalOutput").ap() for i, shape in enumerate(OUTS)]
    build(nc, ins, outs)
    r = run(nc, [arrays], core_ids=[0])
    return tuple(r.results[0][f"out_{i}"] for i in range(len(OUTS)))
```

```python
from contextlib import ExitStack

import numpy as np

import concourse.bass as bass
from concourse import mybir

F32 = mybir.dt.float32
F32R = mybir.dt.float32r
BF16 = mybir.dt.bfloat16
I32 = mybir.dt.int32
U32 = mybir.dt.uint32
ALU = mybir.AluOpType
ACT = mybir.ActivationFunctionType
AX = mybir.AxisListType

P = 128
D = 1024
KC = D // P
SEQ = 1024
NS = 8
T = SEQ + NS
PIECE = T // 3
NT = SEQ // P
H = 8
HD = 64
SCALE = HD ** -0.5
PAGES = 2
PAST = PAGES * P
N_PHYS = 20
WIN = (2, 4, 8, 16)
BUF = 15
NG = 4
EPG = 4
NE = NG * EPG
FF = 256
ALPHA = 2.0 ** 0.25
LAM_INIT = 0.2
EPS = 1e-5
NMOD = 6
SLOT_TILES = (2 * T + NE * (P - 1)) // P
SLOTS = SLOT_TILES * P
HALF = SLOT_TILES // 2
QC, KCOL, VC, UC, GPC, GAC = 0, 1024, 2048, 3072, 3584, 4608
BIG = 3.0e38

CONST_COLS = {}
_at = 0
for _n, _w in (("ident", 128), ("mask", 128), ("tri", 128), ("half", 2), ("delta", 64), ("coef_a", 1), ("coef_b", 1),
               ("corr", 64), ("sel", 8), ("tok", 9), ("start", SLOT_TILES), ("valid", 9), ("dec", 4), ("eps", 1), ("ones", 128)):
    CONST_COLS[_n] = (_at, _at + _w)
    _at += _w
NCONST = _at


def constants():
    c = np.zeros((P, NCONST), np.float32)
    p = np.arange(P)

    def put(name, value):
        a, b = CONST_COLS[name]
        c[:, a:b] = value

    put("ident", np.eye(P))
    put("mask", np.where(p[None, :] > p[:, None], -BIG, 0.0))
    put("tri", (p[:, None] < p[None, :]))
    put("half", np.stack([p < HD, p >= HD], 1))
    put("delta", np.tile(np.eye(NS).reshape(1, 64), (P, 1)))
    put("coef_a", (p % 2 == 0)[:, None])
    put("coef_b", (p % 2 == 1)[:, None])
    put("corr", np.concatenate([[w / min(w, t + 1) for t in range(16)] for w in WIN])[None, :])
    put("sel", (p[:, None] // 2 == np.arange(NS)[None, :]))
    put("tok", p[:, None] + P * np.arange(NT + 1)[None, :])
    put("start", P * np.arange(SLOT_TILES)[None, :])
    valid = np.ones((P, NT + 1))
    valid[NS:, NT] = 0
    put("valid", valid)
    put("dec", np.array([4, 3, 2, 1])[None, :])
    put("eps", EPS)
    put("ones", 1.0)
    half = HD // 2
    inv = (np.float32(10000.0) ** (-np.arange(half, dtype=np.float32) / half)).astype(np.float32)
    pos = np.concatenate([np.arange(SEQ), np.full(NS, PAST)]).astype(np.float32)
    ang = (pos[None, :] * inv[p % half][:, None]).astype(np.float32)
    sign = np.where(p % HD < half, -1.0, 1.0)[:, None]
    return c, np.stack([np.cos(ang), sign * np.sin(ang)], 1).astype(np.float32)


class Event:

    def __init__(self, sem, per, first=0):
        self.sem, self.per, self.first = sem, per, first

    def wait(self, eng, h, k):
        eng.wait_ge(self.sem, h * self.per + (self.first + k + 1))

    def wait_first(self, eng, k):
        eng.wait_ge(self.sem, k + 1)


class Chain:

    def __init__(self, eng, sem):
        self.eng, self.sem, self.base, self.n = eng, sem, 0, 0

    def __call__(self, ins):
        self.n += 1
        ins.then_inc(self.sem, 1)
        self.eng.wait_ge(self.sem, self.base + self.n)

    def loop(self, start, end, per):
        chain = self

        class _Loop:
            def __enter__(self):
                self.before = chain.n
                self.cm = chain.eng.Fori(start, end)
                i = self.cm.__enter__()
                chain.base = (i - start) * per if start else i * per
                return i

            def __exit__(self, *a):
                r = self.cm.__exit__(*a)
                used = chain.n - self.before
                assert used == per or a[0], ("chained instructions in a turn", used)
                chain.base, chain.n = 0, self.before + per * (end - start)
                return r
        return _Loop()


def build(nc, ins, outs):
    with ExitStack() as ctx:
        _build(nc, ctx, ins, outs)


def _build(nc, ctx, I, O):
    def sb(name, shape, dt):
        return ctx.enter_context(nc.sbuf_tensor(name, shape, dt))

    def sem(name):
        return ctx.enter_context(nc.semaphore(name))

    def dram(name, shape, dt=F32):
        return nc.dram_tensor(name, shape, dt, kind="Internal").ap()

    NR = 30848
    NF = 20700
    R = sb("R", [P, NR], F32R)
    F = sb("F", [P, NF], F32)
    cst = sb("cst", [P, NCONST], F32)
    maskb = sb("maskb", [P, P], BF16)
    identb = sb("identb", [P, P], BF16)
    sm = sb("sm", [P, 352], F32)

    class Pool_:
        def __init__(self, t, size):
            self.t, self.size, self.at = t, size, 0

        def take(self, n, *dims):
            a = self.t[:, self.at:self.at + n]
            self.at += n
            assert self.at <= self.size, (self.at, self.size)
            if len(dims) == 2:
                a = a.rearrange("p (a b) -> p a b", a=dims[0])
            if len(dims) == 3:
                a = a.rearrange("p (a b c) -> p a b c", a=dims[0], b=dims[1])
            return a

    def const(name):
        a, b = CONST_COLS[name]
        return cst[:, a:b]

    ident, ones = const("ident"), const("ones")
    S = ctx.enter_context(nc.psum_tensor("S", [P, 2048], F32))
    TB = [ctx.enter_context(nc.psum_tensor(f"T{i}", [P, 512], F32)) for i in range(2)]
    OB = ctx.enter_context(nc.psum_tensor("OB", [P, 512], F32))
    PB = ctx.enter_context(nc.psum_tensor("PB", [P, 512], F32))
    Sb = [S[:, 512 * i:512 * i + 512] for i in range(4)]

    smp = Pool_(sm, 352)
    neglam = smp.take(1)
    coef = smp.take(1)
    lamt = smp.take(4)
    sublng = smp.take(1)
    pscale = smp.take(8)
    modT = smp.take(144, 16, 9)
    nmax = smp.take(2)
    esum = smp.take(2)
    resum = smp.take(2)
    snm = smp.take(1)
    sss = smp.take(1)
    srs = smp.take(1)
    qs = smp.take(8)
    ks = smp.take(8)
    sE = smp.take(16, 8, 2)
    sT = smp.take(32, 2, 16)
    wsum = smp.take(16, 2, 8)
    dgw = smp.take(8)
    stat = smp.take(12, 2, 6)
    mv = smp.take(2)
    rstd1 = smp.take(1)
    pt = sb("pt", [1, 16], I32)

    mod_d = dram("mod_d", [9, NMOD * D])
    pool_d = dram("pool_d", [8, P, T])
    mg_d = dram("mg_d", [8, P, T])
    x1_d = dram("x1_d", [T, D])
    h2_d = dram("h2_d", [T, D])
    tok_d = dram("tok_d", [SLOTS, 1], U32)
    y_d = dram("y_d", [SLOTS, D])

    x_p = I["x_prompt"].rearrange("b s d -> (b s) d")
    x_s = I["x_sample"].rearrange("b s d -> (b s) d")
    w_in = I["w_in"][0].rearrange("(k p) n -> p k n", p=P)
    w_ada = I["w_ada"][0].rearrange("(k p) n -> p k n", p=P)
    y_p = O[0].rearrange("b s d -> (b s) d")
    y_s = O[1].rearrange("b s d -> (b s) d")
    nk_p = O[2].rearrange("l b (t p) h m d -> (l b) p t h (m d)", p=P)
    nv_p = O[3].rearrange("l b (t p) h d -> (l b) p t h d", p=P)
    nk_s = O[5].rearrange("l b s h m d -> (l s) b h (m d)")
    nv_s = O[6].rearrange("l b s h d -> (l s) b h d")
    ck = I["cache_k"][0].rearrange("n p h m d -> n p h (m d)")
    cv = I["cache_v"][0]

    stage_done = sem("stage_done")

    def stage_end(eng, n):
        eng.sem_inc(stage_done, 1)
        eng.wait_ge(stage_done, 5 * (n + 1))

    waits_apart = sem("waits_apart")

    def apart(eng):
        eng.sem_inc(waits_apart, 1)

    v_chain, a_chain, p_chain = sem("vector_chain"), sem("scalar_chain"), sem("gpsimd_chain")

    f = Pool_(F, NF)
    cossin = f.take(2 * T, 2, T)
    xr = f.take(9 * D, 9, D)
    crow = f.take(D)
    modrow = [crow[:, 256 * b:256 * b + 256] for b in range(3)]
    badab = [f.take(256) for _ in range(3)]
    sTc = f.take(72, 8, 9)
    AW = 256
    adaw = [f.take(KC * AW, KC, AW) for _ in range(3)]
    h32 = [f.take(512) for _ in range(2)]
    lamv = f.take(256, 4, 64)
    hs32 = f.take(64, 8, 8)
    NADA = NMOD * D // AW

    r = Pool_(R, NR)
    hT = [r.take(KC * T, KC, T) for _ in range(2)]
    whl = [[r.take(KC * P, KC, P) for _ in range(2)] for _ in range(2)]
    r_heads = r.at

    ld_c = sem("ld_c")
    ld_ada = [sem(f"ld_ada{i}") for i in range(3)]
    ld_x = sem("ld_x")
    ld_small = sem("ld_small")
    ada_done = sem("ada_done")
    ada_row = sem("ada_row")
    ada_st = [sem(f"ada_st{i}") for i in range(3)]
    cT_done, silu_done, cT_copied = sem("cT_done"), sem("silu_done"), sem("cT_copied")
    modT_done, modT_copied = sem("modT_done"), sem("modT_copied")
    xT_done, h_hi, h_lo, hs_ready = sem("xT_done"), sem("h_hi"), sem("h_lo"), sem("hs_ready")
    h_full = sem("h_full")
    lam_exp = sem("lam_exp")
    lam_sum = sem("lam_sum")

    f = Pool_(F, NF)
    f.take(2 * T)
    ubuf = [f.take(16 + T) for _ in range(2)]
    sA = f.take(16 + SEQ)
    sB = f.take(16 + SEQ)
    pooled = f.take(T)
    poolo = [f.take(T) for _ in range(2)]
    stt = f.take(512)
    stall = f.take(480, 4, 120)
    ssum = f.take(8)
    wp32 = f.take(1024, 4, 256)
    upo = f.take(128)
    uso = f.take(128)
    f_pool = f.at
    r1 = Pool_(R, NR)
    r1.at = r_heads
    plr = [r1.take(T) for _ in range(2)]
    wpr = [r1.take(256) for _ in range(2)]

    w_landed = [sem(f"w_landed{i}") for i in range(2)]
    w_hi = Event(sem("w_hi"), 5, 4)
    w_lo = Event(sem("w_lo"), 5, 4)
    piece_ready = Event(sem("piece_ready"), 15, 12)
    piece_copied = Event(sem("piece_copied"), 15, 12)
    piece_rope = Event(sem("piece_rope"), 6)
    swap_done = Event(sem("swap_done"), 6)
    ld_pool = sem("ld_pool")
    stT_ready, stT_copied = sem("stT_ready"), sem("stT_copied")
    pool_split, pool_ready, pool_out = sem("pool_split"), sem("pool_ready"), sem("pool_out")
    pool_st = [sem(f"pool_st{i}") for i in range(2)]
    uT_ready, uT_copied, u_st = sem("uT_ready"), sem("uT_copied"), sem("u_st")
    state_st = sem("state_st")
    pl_hi = sem("pl_hi")
    pooled_done = sem("pooled_done")
    wp_landed = sem("wp_landed")

    f = Pool_(F, NF)
    f.take(2 * T)
    cosT, sinT = cossin[:, 0, :], cossin[:, 1, :]
    Pr = f.take(2 * SEQ, 2, SEQ)
    Wt = f.take(2 * SEQ, 2, SEQ)
    q32, k32, v32 = f.take(T), f.take(T), f.take(T)
    gate = [f.take(T) for _ in range(2)]
    poolc = f.take(T)
    O32 = f.take(T)
    kout = f.take(SEQ, 8, P)
    vt32 = f.take(SEQ, 8, P)
    KV = f.take(16 * P, 16, P)
    wraw2 = [f.take(KC * P, KC, P) for _ in range(2)]
    wraw = wraw2
    assert f_pool <= f.at - 2 * KC * P
    swp = f.take(PIECE)
    kso, vso = f.take(P), f.take(P)
    ps32 = f.take(PAST + 2)
    os32 = f.take(P)
    W8 = f.take(128, 16, 8)
    sq = Pr[:, :, :].rearrange("p a b -> p (a b)")[:, 0:T]
    rst = Wt[:, :, :].rearrange("p a b -> p (a b)")[:, 0:T]
    Bd = O32[:, 0:1024].rearrange("p (b f) -> p b f", b=8)
    r2 = Pool_(R, NR)
    r2.at = r_heads
    qhl = [r2.take(2 * SEQ, 2, SEQ) for _ in range(2)]
    khl = [r2.take(SEQ) for _ in range(2)]
    vhl = [r2.take(SEQ, 8, P) for _ in range(2)]
    wt = [[r2.take(512, 2, 256) for _ in range(2)] for _ in range(2)]

    def ev(name, per, first=0):
        return Event(sem(name), per, first)

    s_ready, smax, exp_done, comb = ev("s_ready", 8), ev("smax", 8), ev("exp_done", 8), ev("comb", 8)
    t_ready, wt_hi, wt_lo, pv_done = ev("t_ready", 10), ev("wt_hi", 10), ev("wt_lo", 10), ev("pv_done", 10)
    o_copied = ev("o_copied", 4)
    kt_ready, kt_copied = ev("kt_ready", 5), ev("kt_copied", 5)
    qk_hi, qk_lo, v_hi, v_lo = ev("qk_hi", 1), ev("qk_lo", 1), ev("v_hi", 1), ev("v_lo", 1)
    bd_done, qbc_ready, sT_done, sT_ready = ev("bd_done", 1), ev("qbc_ready", 1), ev("sT_done", 1), ev("sT_ready", 1)
    smx_done, sexp_done, pn_done = ev("smx_done", 1), ev("sexp_done", 1), ev("pn_done", 1)
    qbc_used = ev("qbc_used", 2)
    pnT_ready, w8_done, os_ready, os_copied = ev("pnT_ready", 1), ev("w8_done", 1), ev("os_ready", 1), ev("os_copied", 1)
    osT_ready, osT_copied = ev("osT_ready", 1), ev("osT_copied", 1)
    sq_done, ms_ready, ln_done, rst_done = ev("sq_done", 1), ev("ms_ready", 3), ev("ln_done", 3), ev("rst_done", 1)
    merged = ev("merged", 2)

    k_landed, v_landed = sem("kpages_landed"), sem("vpages_landed")
    poolc_landed = sem("poolc_landed")
    mg_st = sem("merged_stored")
    kout_st, vout_st, kvs_st = sem("kout_stored"), sem("vout_stored"), sem("kvs_stored")
    qzero = sem("qzero")

    f = Pool_(F, NF)
    wo32 = f.take(4096, 4, D)
    mt32 = [f.take(D, KC, P) for _ in range(2)]
    x3 = [f.take(D) for _ in range(2)]
    y3 = f.take(D)
    x1t = [f.take(D) for _ in range(2)]
    h2t = [f.take(D) for _ in range(2)]
    h2T = f.take(D, KC, P)
    g1b, sc2b, sh2b, l1g, l1b = [f.take(D) for _ in range(5)]
    r3 = Pool_(R, NR)
    wo = [r3.take(KC * D, KC, D) for _ in range(2)]
    mhl = [[r3.take(D, KC, P) for _ in range(2)] for _ in range(2)]
    wrgv = f.take(KC * 20, KC, 20)
    brg = f.take(20)
    rlv = f.take(180, 9, 20)
    wo_landed, WO = [k_landed, v_landed, poolc_landed, kvs_st], [256 * H, 256 * H, 16 * H, 32 * H]
    x3_landed, X3 = pool_st, 16 * 4
    wo_hi, wo_lo = sem("wo_hi"), sem("wo_lo")
    tab_landed = sem("tab_landed")
    m_landed = [sem(f"m_landed{i}") for i in range(2)]
    m_hi, m_lo = sem("m_hi"), sem("m_lo")
    wout_ready, wout_used = sem("wout_ready"), sem("wout_used")
    var_done, std_done = sem("var_done"), sem("std_done")
    h2_done = sem("h2_done")
    x1_st, h2_st = [sem(f"x1_st{i}") for i in range(2)], [sem(f"h2_st{i}") for i in range(2)]
    h2T_ready, h2T_copied, rl_ready, rl_used = sem("h2T_ready"), sem("h2T_copied"), sem("rl_ready"), sem("rl_used")
    x1_ready = sem("x1_ready")

    w1c, w2c = sb("w1c", [P, 9], F32), sb("w2c", [P, 9], F32)
    slot = [sb(f"slot{i}", [P, 9], U32) for i in range(2)]
    toku = sb("toku", [P, 9], U32)
    te = sb("te", [1, 32], I32)
    route_exp, route_exp_done = sem("route_exp"), sem("route_exp_done")
    m_mask, pos_ready, slots_done = sem("m_mask"), sem("pos_ready"), sem("slots_done")
    zero_st, tok_st = sem("zero_st"), sem("tok_st")
    f = Pool_(F, NF)
    M1, M2, M12, slotf = [f.take(144, 9, 16) for _ in range(4)]
    cnt = f.take(16)
    base = f.take(17)
    tef = f.take(32 * 16, 32, 16)
    te32 = f.take(32)
    pref = f.take(160, 10, 16)
    tokz = f.take(32)
    oh_g, esel, oh1, oh2 = [f.take(36, 9, 4) for _ in range(4)]
    rt36 = [f.take(36, 9, 4) for _ in range(2)]
    r9 = [f.take(9) for _ in range(4)]
    cnti = sb("cnti", [P, 16], I32)
    assert f.at <= 4096
    Mb = sb("Mb", [P, 144], BF16)
    trib = sb("trib", [P, P], BF16)
    onesb = sb("onesb", [P, P], BF16)

    f = Pool_(F, NF)
    raw_g = [f.take(KC * FF, KC, FF) for _ in range(2)]
    raw_u = [f.take(KC * FF, KC, FF) for _ in range(2)]
    raw_d = [f.take(2 * D, 2, D) for _ in range(2)]
    xg = [f.take(D) for _ in range(2)]
    yv = [f.take(D) for _ in range(2)]
    silu = f.take(FF)
    av = f.take(FF)
    r4 = Pool_(R, NR)
    gu = [[r4.take(KC * 512, KC, 512) for _ in range(2)] for _ in range(2)]
    dn = [[r4.take(2 * D, 2, D) for _ in range(2)] for _ in range(2)]
    hg = [[r4.take(D, KC, P) for _ in range(2)] for _ in range(2)]
    aT = [r4.take(FF, 2, P) for _ in range(2)]
    idx = [sb(f"idx{i}", [P, 1], U32) for i in range(2)]
    idx_landed = [sem(f"idx_landed{i}") for i in range(2)]
    xg_landed = [sem(f"xg_landed{i}") for i in range(2)]
    e_landed = [sem(f"e_landed{i}") for i in range(2)]
    d_landed = [sem(f"d_landed{i}") for i in range(2)]
    xgT_ready, hg_hi, hg_lo = sem("xgT_ready"), sem("hg_hi"), sem("hg_lo")
    g_hi, g_lo, u_lo, dn_hi, dn_lo = sem("g_hi"), sem("g_lo"), sem("u_lo"), sem("dn_hi"), sem("dn_lo")
    gu_used, dn_used = sem("gu_used"), sem("dn_used")
    silu_ok, av_done, avT_ready, avT_hi, avT_lo = sem("silu_ok"), sem("av_done"), sem("avT_ready"), sem("avT_hi"), sem("avT_lo")
    y_copied = sem("y_copied")
    y_st = [sem(f"y_st{i}") for i in range(2)]

    f = Pool_(F, NF)
    x5 = [f.take(D) for _ in range(2)]
    ya = [f.take(D) for _ in range(3)]
    yb = [f.take(D) for _ in range(3)]
    m5 = [f.take(D) for _ in range(2)]
    o5 = [f.take(D) for _ in range(2)]
    g2b, l2g, l2b = [f.take(D) for _ in range(3)]
    x5_landed, LD5 = ld_ada[0:2], 32 * (NADA // 3)
    out_st, ST5 = ada_st[0:2], 16 * (NADA // 3)
    y5_landed, Y5 = [xg_landed[0], xg_landed[1], tok_st], [16 * (SLOT_TILES // 2), 16 * (SLOT_TILES // 2), 32 * (NT + 1)]
    scaled5, SC5 = pooled_done, 4
    gained5, GA5 = pool_ready, 24
    tab5 = sem("tab5")
    out_ready = sem("out_ready")
    m5_used = sem("m5_used")

    def landed_value(h, c):
        if c % 2 == 0:
            return h * 48 + 16 * (2 + c // 2 + 1)
        return h * 32 + 16 * (2 + c // 2 + 1)

    COLS = (QC, KCOL, VC, GPC, GAC)

    def piece_bank(n, first):
        return Sb[n % 4] if first else {9: Sb[3], 11: Sb[1], 12: Sb[0], 13: Sb[3]}.get(n, PB)

    block = ctx.enter_context(nc.Block())

    @block.sync
    def _(sp):
        with nc.allow_non_contiguous_dma(reason="small tables by feature"):
            sp.dma_start(cst[:, :], I["cst"]).then_inc(ld_c, 16)
            sp.dma_start(crow[0:1, :], I["c_prompt"]).then_inc(ld_c, 16)
            sp.dma_start(crow[1:9, :], I["c_sample"]).then_inc(ld_c, 16)

            for n in range(NADA):
                b = n % 3
                if n >= 3:
                    sp.wait_ge(ada_row, n - 2)
                sp.dma_start(adaw[b], w_ada[:, :, n * AW:(n + 1) * AW]).then_inc(ld_ada[b], 16)
                sp.dma_start(badab[b][0:9, 0:AW], I["b_ada"][:, n * AW:(n + 1) * AW].to_broadcast([9, AW])).then_inc(ld_ada[b], 16)
                if n < NT:
                    sp.dma_start(xr[:, n, :], x_p[n * P:(n + 1) * P, :]).then_inc(ld_x, 16)
                if n == NT:
                    sp.dma_start(xr[0:NS, NT, :], x_s).then_inc(ld_x, 16)
                    sp.dma_start(cossin, I["rope"]).then_inc(ld_small, 16)
                    sp.dma_start(sublng, I["subln_g"][0].rearrange("(p o) -> p o", o=1)).then_inc(ld_small, 16)
                    sp.dma_start(pscale, I["pool_scale"][0].rearrange("(k p) -> p k", p=P)).then_inc(ld_small, 16)
                    sp.dma_start(pt[:, :], I["page_table"].rearrange("b j -> (b j)").rearrange("(o n) -> o n", o=1)).then_inc(ld_small, 16)
                    for m, name in enumerate(("lambda_q1", "lambda_k1", "lambda_q2", "lambda_k2")):
                        sp.dma_start(lamv[:, m, :], I[name].to_broadcast([P, 64])).then_inc(ld_small, 16)
            sp.wait_ge(ld_small, 16 * 8)
            stage_end(sp, 0)

            def chunk(h, c):
                before = -1 if c == 0 else c - 2 if c > 1 else -2
                w_lo.wait(sp, h, before)
                w_hi.wait(sp, h, before)
                col = h * P + COLS[c]
                sp.dma_start(wraw2[c % 2], w_in[:, :, bass.ds(col, P)]).then_inc(w_landed[c % 2], 16)

            def wchunk(col, b, landed):
                sp.dma_start(wraw[b], w_in[:, :, bass.ds(col, P)]).then_inc(w_landed[b], 16)

            sp.dma_start(stt[0:120, :], I["state_pool"][0].rearrange("b r c -> (b r) c")).then_inc(ld_pool, 16)
            for g in range(4):
                if g >= 2:
                    w_hi.wait_first(sp, g - 2)
                    w_lo.wait_first(sp, g - 2)
                wchunk(UC + g * P, g % 2, None)
                if g == 1:
                    sp.dma_start(wp32, I["w_pool"][0].rearrange("g p n -> p g n")).then_inc(wp_landed, 16)
            sp.dma_start(O[7][0, :, 0:BUF - 1, :], I["state_pool"][0, :, 1:BUF, :]).then_inc(state_st, 16)
            chunk(0, 0)
            chunk(0, 1)
            for b in range(2):
                sp.wait_ge(pool_st[b], 16 * 4)
            sp.wait_ge(u_st, 16 * 8)
            sp.wait_ge(state_st, 16)
            stage_end(sp, 1)

            def pages(h, table, landed):
                apart(sp)
                for n in range(16):
                    page = sp.value_load(pt[0:1, n:n + 1], min_val=0, max_val=N_PHYS - 1)
                    sp.dma_start(KV[:, n, :], table[bass.ds(page, 1), :, bass.ds(h, 1), :]
                                 .rearrange("a p h d -> (a p) (h d)")).then_inc(landed, 16)

            def step(h, nxt, first):
                if nxt:
                    chunk(h + 1, 0)
                if not first:
                    os_ready.wait(sp, h, -1)
                pages(h, ck, k_landed)
                if nxt:
                    chunk(h + 1, 1)
                    chunk(h + 1, 2)
                if not first:
                    sp.wait_ge(mg_st, h * 16)
                sp.dma_start(poolc, pool_d[bass.ds(h, 1), :, :].rearrange("a p n -> (a p) n")).then_inc(poolc_landed, 16)
                sT_done.wait(sp, h, 0)
                pages(h, cv, v_landed)
                if nxt:
                    for c in range(3, 5):
                        chunk(h + 1, c)

            for c in range(2, 5):
                chunk(0, c)
            step(0, True, True)
            with sp.Fori(1, H - 1) as h:
                step(h, True, False)
            step(H - 1, False, False)
            sp.wait_ge(mg_st, 16 * H)
            stage_end(sp, 2)

            wov = I["w_out"][0].rearrange("(k p) n -> p k n", p=P)
            def w_out_chunk(k):
                if k >= 4:
                    sp.wait_ge(wo_lo, k - 3)
                    sp.wait_ge(wo_hi, k - 3)
                sp.dma_start(wo32[:, k % 4, :], wov[:, k, :]).then_inc(wo_landed[k % 4], 16)

            def tile3(t, b, rows, wait):
                if wait:
                    sp.wait_ge(m_hi, t - 1)
                    sp.wait_ge(m_lo, t - 1)
                sp.dma_start(mt32[b][:, :, 0:rows], mg_d.rearrange("k p n -> p k n")[:, :, bass.ds(t * P, rows)]).then_inc(m_landed[b], 16)
                if wait:
                    sp.wait_ge(x1_ready, t - 1)
                sp.dma_start(x3[b][0:rows, :], (x_p[bass.ds(t * P, rows), :] if rows == P else x_s)).then_inc(x3_landed[b], 16)

            w_out_chunk(0)
            w_out_chunk(1)
            tile3(0, 0, P, False)
            w_out_chunk(2)
            w_out_chunk(3)
            tile3(1, 1, P, False)
            for k in range(4, 8):
                w_out_chunk(k)
            sp.dma_start(g1b, mod_d[0:1, 2 * D:3 * D].to_broadcast([P, D])).then_inc(tab_landed, 16)
            sp.dma_start(l1g, I["ln1_g"].to_broadcast([P, D])).then_inc(tab_landed, 16)
            sp.dma_start(l1b, I["ln1_b"].to_broadcast([P, D])).then_inc(tab_landed, 16)
            sp.dma_start(sh2b, mod_d[0:1, 3 * D:4 * D].to_broadcast([P, D])).then_inc(tab_landed, 16)
            sp.dma_start(sc2b, mod_d[0:1, 4 * D:5 * D].to_broadcast([P, D])).then_inc(tab_landed, 16)
            sp.dma_start(wrgv[:, :, 0:4], I["w_group"][0].rearrange("(k p) n -> p k n", p=P)).then_inc(tab_landed, 16)
            sp.dma_start(wrgv[:, :, 4:20], I["w_router"][0].rearrange("(k p) n -> p k n", p=P)).then_inc(tab_landed, 16)
            sp.dma_start(brg[:, 0:4], I["b_group"].to_broadcast([P, 4])).then_inc(tab_landed, 16)
            sp.dma_start(brg[:, 4:20], I["b_router"].to_broadcast([P, 16])).then_inc(tab_landed, 16)
            with sp.Fori(1, NT // 2) as i:
                for b in range(2):
                    tile3(i * 2 + b, b, P, True)
            tile3(NT, 0, NS, True)
            sp.wait_ge(h2_done, NT)
            sp.wait_ge(x1_ready, NT)
            sp.dma_start(g1b[0:NS, :], mod_d[1:9, 2 * D:3 * D]).then_inc(tab_landed, 16)
            sp.dma_start(sh2b[0:NS, :], mod_d[1:9, 3 * D:4 * D]).then_inc(tab_landed, 16)
            sp.dma_start(sc2b[0:NS, :], mod_d[1:9, 4 * D:5 * D]).then_inc(tab_landed, 16)
            for b in range(2):
                sp.wait_ge(x1_st[b], 16 * (5 if b == 0 else 4))
                sp.wait_ge(h2_st[b], 16 * (5 if b == 0 else 4))
            stage_end(sp, 3)

            def experts(n, b, i):
                tile = i + b * HALF
                e = sp.value_load(te[0:1, bass.ds(tile, 1)], min_val=0, max_val=NE - 1)
                def gate_up():
                    sp.dma_start(raw_g[b], I["w_e_gate"][0, bass.ds(e, 1)].rearrange("a (k p) n -> p (a k) n", p=P)).then_inc(e_landed[b], 16)
                    sp.dma_start(raw_u[b], I["w_e_up"][0, bass.ds(e, 1)].rearrange("a (k p) n -> p (a k) n", p=P)).then_inc(e_landed[b], 16)

                def down():
                    sp.dma_start(raw_d[b], I["w_e_down"][0, bass.ds(e, 1)].rearrange("a (k p) n -> p (a k) n", p=P)).then_inc(d_landed[b], 16)

                if isinstance(i, int) and i == 0:
                    gate_up()
                    down()
                    return
                before = sp.value_load(te[0:1, bass.ds(tile - 1, 1)], min_val=0, max_val=NE - 1)
                sp.wait_ge(g_hi, n * 4 - 4)
                sp.wait_ge(g_lo, n * 2 - 2)
                sp.wait_ge(u_lo, n * 2 - 2)
                apart(sp)
                with sp.If(e != before):
                    gate_up()
                with sp.Else():
                    sp.sem_inc(e_landed[b], 32)
                sp.wait_ge(dn_hi, n * 2 - 2)
                sp.wait_ge(dn_lo, n * 2 - 2)
                apart(sp)
                with sp.If(e != before):
                    down()
                with sp.Else():
                    sp.sem_inc(d_landed[b], 16)

            for b in range(2):
                experts(b, b, 0)
            with sp.Fori(1, HALF) as i:
                for b in range(2):
                    experts(i * 2 + b, b, i)
            for b in range(2):
                sp.wait_ge(y_st[b], 16 * (SLOT_TILES // 2 + 1))
            stage_end(sp, 4)

            sp.dma_start(g2b, mod_d[0:1, 5 * D:6 * D].to_broadcast([P, D])).then_inc(tab5, 16)
            sp.dma_start(l2g, I["ln2_g"].to_broadcast([P, D])).then_inc(tab5, 16)
            sp.dma_start(l2b, I["ln2_b"].to_broadcast([P, D])).then_inc(tab5, 16)
            for t in range(NT + 1):
                rows = P if t < NT else NS
                if t >= 2:
                    sp.wait_ge(m5_used, t - 1)
                sp.dma_start(x5[t % 2][0:rows, :], x1_d[t * P:t * P + rows, :]).then_inc(x5_landed[t % 2], 16)
            sp.wait_ge(m5_used, NT)
            sp.dma_start(g2b[0:NS, :], mod_d[1:9, 5 * D:6 * D]).then_inc(tab5, 16)
            sp.wait_ge(out_st[0], ST5 + 16 * 5)
            sp.wait_ge(out_st[1], ST5 + 16 * 4)

    @block.tensor
    def _(pe):
        mm, tr = nc.tensor.matmul, nc.tensor.transpose

        def mm3(out, w, m, start=True, stop=True):
            mm(out, w[0], m[1], start=start, stop=False)
            mm(out, w[1], m[0], start=False, stop=False)
            return mm(out, w[0], m[0], start=False, stop=stop)

        pe.wait_ge(ld_c, 48)
        pe.wait_ge(silu_done, 1)
        for k in range(KC):
            last = tr(TB[0][:, 9 * k:9 * k + 9], crow[0:9, k * P:(k + 1) * P], ident[0:9, 0:9])
        last.then_inc(cT_done, 1)
        pe.wait_ge(cT_copied, 1)

        def modulation(n):
            pe.wait_ge(ada_row, n + 1)
            if n:
                pe.wait_ge(modT_copied, n)
            for q in range(2):
                last = tr(OB[:, 9 * q:9 * q + 9], modrow[n % 3][0:9, q * P:(q + 1) * P], ident[0:9, 0:9])
            last.then_inc(modT_done, 1)

        for n in range(NADA):
            pe.wait_ge(ld_ada[n % 3], 32 * (n // 3 + 1))
            if n >= 4:
                pe.wait_ge(ada_row, n - 3)
            for k in range(KC):
                last = mm(Sb[n % 4][0:9, 0:AW], sTc[:, k, :], adaw[n % 3][:, k, :], start=(k == 0), stop=(k == KC - 1))
            last.then_inc(ada_done, 1)
            if 1 <= n <= 8:
                modulation(n - 1)
            if n >= 8:
                m = n - 8
                if m == 0:
                    pe.wait_ge(ld_x, 16 * 9)
                if m >= 2:
                    pe.wait_ge(h_full, m - 1)
                for t in range(4):
                    last = tr(TB[m % 2][:, t * P:(t + 1) * P], xr[:, 4 * (m % 2) + t, (m // 2) * P:(m // 2 + 1) * P], ident)
                last.then_inc(xT_done, 1)
        pe.wait_ge(modT_copied, 8)
        for k in range(KC):
            last = tr(OB[:, NS * k:NS * k + NS], xr[0:NS, NT, k * P:(k + 1) * P], ident[0:NS, 0:NS])
        last.then_inc(xT_done, 1)
        stage_end(pe, 0)

        def piece(b, s, bank, low):
            x = [t[:, :, s * PIECE:(s + 1) * PIECE] for t in hT]
            for k in range(KC):
                mm(bank[:, 0:PIECE], whl[b][0][:, k, :], x[1][:, k, :], start=(k == 0), stop=False)
                mm(bank[:, 0:PIECE], whl[b][0][:, k, :], x[0][:, k, :], start=False, stop=False)
            low()
            for k in range(KC):
                last = mm(bank[:, 0:PIECE], whl[b][1][:, k, :], x[0][:, k, :], start=False, stop=(k == KC - 1))
            return last

        pe.wait_ge(ld_pool, 16)
        for g in range(4):
            last = tr(TB[0][:, 120 * g:120 * g + 120], stt[0:120, g * P:(g + 1) * P], ident[0:120, 0:120])
        last.then_inc(stT_ready, 1)
        pe.wait_ge(stT_copied, 1)
        def pooling(g):
            piece_copied.wait_first(pe, 3 * g + 2)
            if g:
                pe.wait_ge(uT_copied, 2 * g)
            tr(OB[0:BUF, 0:P], ubuf[g % 2][:, 16 + SEQ - BUF:16 + SEQ], ident)
            tr(OB[0:NS, P:2 * P], ubuf[g % 2][:, 16 + SEQ:16 + T], ident).then_inc(uT_ready, 1)
            pe.wait_ge(pool_split, 2 * (g + 1))
            pe.wait_ge(pl_hi, 2 * (g + 1))
            for c in range(2):
                for s in range(3):
                    n = 6 * g + 3 * c + s
                    if n >= 2:
                        pe.wait_ge(pool_out, n - 1)
                    mm3(TB[n % 2][:, 0:PIECE], [w[:, c * P:(c + 1) * P] for w in wpr],
                        [x[:, s * PIECE:(s + 1) * PIECE] for x in plr]).then_inc(pool_ready, 1)

        for g in range(4):
            w_hi.wait_first(pe, g)
            for s in range(3):
                n = 3 * g + s
                if n >= 4:
                    piece_copied.wait_first(pe, n - 4)
                piece(g % 2, s, Sb[n % 4], lambda: w_lo.wait_first(pe, g)).then_inc(piece_ready.sem, 1)
            if g:
                pooling(g - 1)
        pooling(3)
        stage_end(pe, 1)

        def proj(h, n, first=False):
            c = n // 3
            if n % 3 == 0:
                w_hi.wait(pe, h, c)
            if first:
                piece_copied.wait(pe, h, n - 4)
            elif n in (11, 12):
                ln_done.wait(pe, h - 1, 12 - n)
            else:
                piece_copied.wait(pe, h, {9: 7, 10: 8, 13: 9, 14: 10}.get(n, n - 1))
            piece(c % 2, n % 3, piece_bank(n, first), lambda: w_lo.wait(pe, h, c) if n % 3 == 0 else None).then_inc(piece_ready.sem, 1)

        def kv_rows(h, n):
            if n == 0:
                piece_rope.wait(pe, h, 5)
                piece_copied.wait(pe, h, 8)
            if n >= 2:
                kt_copied.wait(pe, h, n - 2)
            if n < 4:
                src = (k32, v32)[n // 2]
                for t in range(4):
                    last = tr(TB[n % 2][:, t * P:(t + 1) * P], src[:, (4 * (n % 2) + t) * P:(4 * (n % 2) + t + 1) * P], ident)
            else:
                tr(TB[0][0:NS, 0:P], k32[:, SEQ:T], ident)
                last = tr(TB[0][0:NS, P:2 * P], v32[:, SEQ:T], ident)
            last.then_inc(kt_ready.sem, 1)

        def scores(h, i):
            L = (i + 1) * P
            for m in range(2):
                for a in range(0, L, 512):
                    n = max(min(512, L - a), 256)
                    out = S[:, m * SEQ + a:m * SEQ + a + n]
                    q, k = [x[:, m, i * P:(i + 1) * P] for x in qhl], [x[:, a:a + n] for x in khl]
                    mm(out, q[0], k[1], start=True, stop=False)
                    mm(out, q[1], k[0], start=False, stop=False)
                    if a + 512 >= L:
                        mm(S[:, m * SEQ + i * P:m * SEQ + L], identb[:, :], maskb[:, :], start=False, stop=False)
                    last = mm(out, q[0], k[0], start=False, stop=True)
            last.then_inc(s_ready.sem, 1)

        def groups(h, i, part):
            p = i // 2
            at = p * (p + 1) // 2

            def turn(g):
                n = at + g
                if n == 0:
                    qbc_used.wait(pe, h, 1)
                elif n == 1:
                    sexp_done.wait(pe, h, 0)
                elif n == 3:
                    w8_done.wait(pe, h, 0)
                elif n == 6:
                    osT_copied.wait(pe, h, 0)
                if n >= 2:
                    wt_lo.wait(pe, h, n - 2)
                for j in range(2):
                    for t in range(2):
                        last = tr(TB[n % 2][:, (2 * j + t) * P:(2 * j + t + 1) * P],
                                  Wt[:, t, (2 * g + j) * P:(2 * g + j + 1) * P], ident)
                last.then_inc(t_ready.sem, 1)

            def product(g):
                n = at + g
                wt_hi.wait(pe, h, n)
                wt_lo.wait(pe, h, n)
                if g == 0 and p > 0:
                    o_copied.wait(pe, h, p - 1)
                for j in range(2):
                    last = mm3(OB[:, 0:256], [v[:, 2 * g + j, :] for v in vhl], [w[:, j, :] for w in wt[n % 2]],
                               start=(g == 0 and j == 0), stop=(g == p and j == 1))
                last.then_inc(pv_done.sem, 1)

            if part == 0:
                comb.wait(pe, h, i)
                turn(0)
                if p:
                    turn(1)
            else:
                for g in range(p + 1):
                    if g >= 2:
                        turn(g)
                    if g >= 2 or g == 1:
                        product(g - 1)
                product(p)

        def step(h, nxt, first):
            qk_hi.wait(pe, h, 0)
            qk_lo.wait(pe, h, 0)
            if first:
                piece_copied.wait(pe, h, 14)
            else:
                ln_done.wait(pe, h, -1)
                piece_copied.wait(pe, h, 12)
            scores(h, 0)
            kt_copied.wait(pe, h, 4)
            bd_done.wait(pe, h, 0)
            for b in range(2):
                last = mm(TB[b][:, :], ones, Bd[:, 4 * b:4 * b + 4, :], start=True, stop=True)
            last.then_inc(qbc_ready.sem, 1)
            for i in range(8):
                if nxt:
                    proj(h + 1, i)
                if i == 7:
                    os_copied.wait(pe, h, 0)
                    apart(pe)
                    tr(TB[0][:, 0:NS], os32[0:NS, :], ident[0:NS, 0:NS]).then_inc(osT_ready.sem, 1)
                    if nxt:
                        proj(h + 1, 8)
                    groups(h, 7, 0)
                    if nxt:
                        exp_done.wait(pe, h, 7)
                        proj(h + 1, 9)
                if i == 2:
                    v_hi.wait(pe, h, 0)
                    v_lo.wait(pe, h, 0)
                    if not first:
                        o_copied.wait(pe, h, -1)
                if i % 2 == 0 and i:
                    groups(h, i - 1, 1)
                if i < 7:
                    exp_done.wait(pe, h, i)
                    scores(h, i + 1)
                    if i % 2:
                        groups(h, i, 0)
                if i == 2:
                    sT_done.wait(pe, h, 0)
                    for j in range(2):
                        tr(TB[1][0:16, j * P:(j + 1) * P], sT[:, j, :], ident)
                    mm(TB[1][0:16, PAST:PAST + 1], sE[:, :, :], ones[:, 0:1], start=True, stop=True).then_inc(sT_ready.sem, 1)
                if i == 4:
                    pn_done.wait(pe, h, 0)
                    wt_lo.wait(pe, h, 1)
                    apart(pe)
                    for j in range(2):
                        tr(TB[1][:, j * 16:j * 16 + 16], ps32[0:16, j * P:(j + 1) * P], ident[0:16, 0:16])
                    mm(TB[1][0:NS, 32:33], const("sel")[0:16, :], ps32[0:16, PAST:PAST + 1], start=True, stop=True)\
                        .then_inc(pnT_ready.sem, 1)
                if i == 6:
                    w8_done.wait(pe, h, 0)
                    wt_lo.wait(pe, h, 4)
                    pe.wait_ge(v_landed, (h + 1) * 256)
                    for n in range(16):
                        mm(TB[0][0:NS, 0:P], W8[:, n, :], KV[:, n, :], start=(n == 0), stop=False)
                    mm(TB[0][0:NS, 0:P], dgw[0:NS, :], vso[0:NS, :], start=False, stop=True).then_inc(os_ready.sem, 1)
            groups(h, 7, 1)
            if nxt:
                wt_lo.wait(pe, h, 9)
                kv_rows(h + 1, 0)
                kv_rows(h + 1, 1)
            exp_done.wait(pe, h, 7)
            sq_done.wait(pe, h, 0)
            for s in range(3):
                mm(Sb[s][:, 0:PIECE], ones, sq[:, s * PIECE:(s + 1) * PIECE], start=True, stop=True).then_inc(ms_ready.sem, 1)
            if nxt:
                proj(h + 1, 10)
                kv_rows(h + 1, 2)
                kv_rows(h + 1, 3)
                proj(h + 1, 11)
                kv_rows(h + 1, 4)
                for n in range(12, 15):
                    proj(h + 1, n)

        for n in range(15):
            proj(0, n, True)
            if n >= 9 and n < 14:
                kv_rows(0, n - 9)
        step(0, True, True)
        with pe.Fori(1, H - 1) as h:
            step(h, True, False)
        step(H - 1, False, False)
        stage_end(pe, 2)

        def project(n, b, rows, first=False):
            pe.wait_ge(m_hi, n + 1)
            pe.wait_ge(m_lo, n + 1)
            if not (isinstance(n, int) and n < 2):
                pe.wait_ge(wout_used, n - 1)
            for q in range(2):
                for k in range(KC):
                    if first and q == 0:
                        pe.wait_ge(wo_hi, k + 1)
                        pe.wait_ge(wo_lo, k + 1)
                    last = mm3(S[0:rows, 1024 * b + 512 * q:1024 * b + 512 * q + 512], [m[:, k, 0:rows] for m in mhl[b]],
                               [w[:, k, 512 * q:512 * q + 512] for w in wo], start=(k == 0), stop=(k == KC - 1))
            last.then_inc(wout_ready, 1)

        def turn_rows3(n, b, rows):
            pe.wait_ge(h2_done, n + 1)
            for k in range(KC):
                last = tr(TB[k // 4][:, (k % 4) * P:(k % 4) * P + rows], h2t[b][0:rows, k * P:(k + 1) * P], ident[0:rows, 0:rows])
            last.then_inc(h2T_ready, 1)

        def router(n, rows):
            pe.wait_ge(h2T_copied, n + 1)
            pe.wait_ge(rl_used, n + 1)
            for k in range(KC):
                last = mm(PB[0:rows, 0:20], h2T[:, k, 0:rows], wrgv[:, k, :], start=(k == 0), stop=(k == KC - 1))
            last.then_inc(rl_ready, 1)

        project(0, 0, P, True)
        project(1, 1, P)
        pe.wait_ge(tab_landed, 16 * 9)
        project(2, 0, P)
        turn_rows3(0, 0, P)
        project(3, 1, P)
        router(0, P)
        turn_rows3(1, 1, P)
        with pe.Fori(2, NT // 2) as i:
            for b in range(2):
                project(i * 2 + b, b, P)
                router(i * 2 + (b - 3), P)
                turn_rows3(i * 2 + (b - 2), b, P)
        project(NT, 0, NS)
        router(NT - 3, P)
        turn_rows3(NT - 2, 0, P)
        router(NT - 2, P)
        turn_rows3(NT - 1, 1, P)
        router(NT - 1, P)
        turn_rows3(NT, 0, NS)
        router(NT, NS)
        pe.wait_ge(m_mask, 1)
        mm(TB[0][:, 0:144], trib[:, :], Mb[:, :], start=True, stop=True)
        mm(TB[1][:, 0:144], onesb[:, :], Mb[:, :], start=True, stop=True).then_inc(pos_ready, 1)
        stage_end(pe, 3)

        def turn_rows(n, b, landed, later):
            pe.wait_ge(xg_landed[b], landed)
            if later:
                pe.wait_ge(hg_lo, 2 * n)
            for k in range(KC):
                last = tr(TB[k // 4][:, (k % 4) * P:(k % 4 + 1) * P], xg[b][:, k * P:(k + 1) * P], ident)
                if k == 3:
                    last.then_inc(xgT_ready, 1)
            last.then_inc(xgT_ready, 1)

        def gate_up(n, b, later):
            pe.wait_ge(hg_hi, n * 2 + 2)
            pe.wait_ge(hg_lo, n * 2 + 2)
            if later:
                pe.wait_ge(av_done, n - 1)
            for q in range(2):
                pe.wait_ge(g_hi, n * 4 + (2 * q + 2))
                pe.wait_ge(g_lo, n * 2 + (q + 1))
                pe.wait_ge(u_lo, n * 2 + (q + 1))
                for k in range(4 * q, 4 * q + 4):
                    last = mm3(Sb[b], [x[:, k, :] for x in hg[b]], [w[:, k, :] for w in gu[b]], start=(k == 0), stop=(k == KC - 1))
            last.then_inc(gu_used, 1)

        def turn_act(n, later):
            pe.wait_ge(av_done, n + 1)
            if later:
                pe.wait_ge(avT_lo, n)
            for c in range(2):
                last = tr(PB[:, c * P:(c + 1) * P], av[:, c * P:(c + 1) * P], ident)
            last.then_inc(avT_ready, 1)

        def down(n, b, later):
            pe.wait_ge(avT_hi, n + 1)
            pe.wait_ge(avT_lo, n + 1)
            pe.wait_ge(dn_hi, n * 2 + 2)
            pe.wait_ge(dn_lo, n * 2 + 2)
            if later:
                pe.wait_ge(y_copied, n)
            for q in range(2):
                for c in range(2):
                    last = mm3(Sb[2 + q], [a[:, c, :] for a in aT], [w[:, c, 512 * q:512 * q + 512] for w in dn[b]],
                               start=(c == 0), stop=(c == 1))
            last.then_inc(dn_used, 1)

        def tile4(n, b, landed, before, more=True):
            if more:
                turn_rows(n + 1, 1 - b, landed, True)
            if before >= 1:
                turn_act(n - 1, before >= 2)
            gate_up(n, b, before >= 2)
            if before >= 1:
                down(n - 1, 1 - b, before >= 2)

        turn_rows(0, 0, 16, False)
        tile4(0, 0, 16, 0)
        tile4(1, 1, 32, 1)
        with pe.Fori(1, SLOT_TILES // 2 - 1) as i:
            for b in range(2):
                tile4(i * 2 + b, b, i * 16 + 16 * (1 + b), 2)
        tile4(SLOT_TILES - 2, 0, 16 * (SLOT_TILES // 2), 2)
        tile4(SLOT_TILES - 1, 1, None, 2, more=False)
        turn_act(SLOT_TILES - 1, True)
        down(SLOT_TILES - 1, 1, True)
        stage_end(pe, 4)

    @block.scalar
    def _(act):
        A = Chain(act, a_chain)

        def sig(ins, event, h, k):
            ins.then_inc(event.sem, 1)
            event.wait(act, h, k)

        def act_(out, in_, func=ACT.Copy, **kw):
            return nc.scalar.activation(out, in_, func, **kw)

        act.wait_ge(ld_c, 48)
        act_(crow[0:9, :], crow[0:9, :], ACT.Silu).then_inc(silu_done, 1)

        def h_hi_part(m):
            act.wait_ge(h_full, m + 1)
            act_(hT[0][:, m // 2, 512 * (m % 2):512 * (m % 2) + 512], h32[m % 2]).then_inc(h_hi, 1)

        for n in range(NADA):
            act.wait_ge(ada_row, n + 1)
            act.dma_start(mod_d[:, n * AW:(n + 1) * AW], modrow[n % 3][0:9, 0:AW]).then_inc(ada_st[n % 3], 16)
            if n >= 9:
                h_hi_part(n - 9)
        h_hi_part(15)
        act.wait_ge(hs_ready, 1)
        act_(hT[0][:, :, SEQ:T], hs32).then_inc(h_hi, 1)
        act.wait_ge(lam_sum, 1)
        act_(lamt[:, 0:2], lamt[:, 2:4], ACT.Exp).then_inc(lam_exp, 1)
        act.wait_ge(h_hi, 17)
        for b in range(3):
            act.wait_ge(ada_st[b], 16 * NADA // 3)
        stage_end(act, 0)

        def w_split(g):
            act.wait_ge(w_landed[g % 2], 16 * (g // 2 + 1))
            if g >= 2:
                piece_ready.wait_first(act, 3 * (g - 2) + 2)
            act_(whl[g % 2][0], wraw[g % 2]).then_inc(w_hi.sem, 1)

        def pooling(g):
            act.wait_ge(uT_ready, g + 1)
            if g:
                act.wait_ge(u_st, 32 * g)
            act_(upo[0:BUF, :], OB[0:BUF, 0:P]).then_inc(uT_copied, 1)
            act_(uso[0:NS, :], OB[0:NS, P:2 * P]).then_inc(uT_copied, 1)
            act.wait_ge(uT_copied, 2 * g + 2)
            act.dma_start(O[4][0, 0, :, g * P:(g + 1) * P], upo[0:BUF, :]).then_inc(u_st, 16)
            act.dma_start(O[7][0, :, BUF - 1, g * P:(g + 1) * P], uso[0:NS, :]).then_inc(u_st, 16)
            act.wait_ge(wp_landed, 16)
            if g:
                act.wait_ge(pool_ready, 6 * g)
            act_(wpr[0], wp32[:, g, :]).then_inc(pl_hi, 1)
            act.wait_ge(pooled_done, g + 1)
            act_(plr[0], pooled).then_inc(pl_hi, 1)
            for c in range(2):
                ch = 2 * g + c
                if ch >= 2:
                    act.wait_ge(pool_st[c], 16 * g)
                for s in range(3):
                    n = 3 * ch + s
                    act.wait_ge(pool_ready, n + 1)
                    act_(poolo[c][:, s * PIECE:(s + 1) * PIECE], TB[n % 2][:, 0:PIECE], ACT.Copy, scale=pscale[:, ch:ch + 1])\
                        .then_inc(pool_out, 1)
                act.wait_ge(pool_out, 3 * ch + 3)
                act.dma_start(pool_d[ch], poolo[c]).then_inc(pool_st[c], 16)

        w_split(0)
        for g in range(4):
            if g < 3:
                w_split(g + 1)
            if g >= 2:
                act.wait_ge(pool_split, 2 * (g - 1))
                act.wait_ge(uT_ready, g - 1)
            for s in range(3):
                n = 3 * g + s
                piece_ready.wait_first(act, n)
                act_(ubuf[g % 2][:, 16 + s * PIECE:16 + (s + 1) * PIECE], Sb[n % 4][:, 0:PIECE]).then_inc(piece_copied.sem, 1)
            if g:
                pooling(g - 1)
        pooling(3)
        stage_end(act, 1)

        def split(h, c):
            act.wait_ge(w_landed[c % 2], landed_value(h, c))
            if c == 0:
                piece_ready.wait(act, h, -1)
            elif c == 1:
                piece_ready.wait(act, h, -4 if not isinstance(h, int) or h else -1)
            else:
                piece_ready.wait(act, h, 3 * (c - 2) + 2)
            sig(act_(whl[c % 2][0], wraw2[c % 2]), w_hi, h, c)

        def take(h, n, first=False):
            if not first:
                if n == 0:
                    qk_lo.wait(act, h, -1)
                if n == 3:
                    kt_ready.wait(act, h, -1)
            piece_ready.wait(act, h, n)
            bank = piece_bank(n, first)
            cols = slice((n % 3) * PIECE, (n % 3 + 1) * PIECE)
            if n < 6:
                dst = (q32, k32)[n // 3][:, cols]
                sig(act_(dst, bank[:, 0:PIECE]), piece_copied, h, n)
                if n:
                    piece_rope.wait(act, h, n - 1)
                for g, src in enumerate((1, 0, 3, 2)):
                    last = act_(swp[32 * g:32 * g + 32, :], dst[32 * src:32 * src + 32, :])
                sig(last, swap_done, h, n)
            elif n < 9:
                sig(act_(v32[:, cols], bank[:, 0:PIECE]), piece_copied, h, n)
            else:
                sig(act_(gate[(n - 9) // 3][:, cols], bank[:, 0:PIECE], ACT.Sigmoid), piece_copied, h, n)

        def rows(h, n, first=False):
            kt_ready.wait(act, h, n)
            if n == 0 and not first:
                act.wait_ge(kout_st, h * 16)
                act.wait_ge(vout_st, h * 16)
                act.wait_ge(kvs_st, h * 32)
            if n < 4:
                dst = (kout, vt32)[n // 2]
                sig(act_(dst[:, 4 * (n % 2):4 * (n % 2) + 4, :], TB[n % 2][:, :].rearrange("p (a b) -> p a b", a=4)), kt_copied, h, n)
            if n == 1:
                act.dma_start(nk_p[0, :, :, bass.ds(h, 1), :].rearrange("p t a d -> p t (a d)"), kout).then_inc(kout_st, 16)
            if n == 3:
                act.dma_start(nv_p[0, :, :, bass.ds(h, 1), :].rearrange("p t a d -> p t (a d)"), vt32).then_inc(vout_st, 16)
            if n == 4:
                A(act_(kso[0:NS, :], TB[0][0:NS, 0:P]))
                sig(act_(vso[0:NS, :], TB[0][0:NS, P:2 * P]), kt_copied, h, 4)
                act.dma_start(nk_s[0, :, bass.ds(h, 1), :].rearrange("b a d -> b (a d)"), kso[0:NS, :]).then_inc(kvs_st, 16)
                act.dma_start(nv_s[0, :, bass.ds(h, 1), :].rearrange("b a d -> b (a d)"), vso[0:NS, :]).then_inc(kvs_st, 16)

        def operands_qk(h, first):
            if not first:
                s_ready.wait(act, h, -1)
            piece_rope.wait(act, h, 5)
            A(act_(qhl[0][0:HD, 0, :], q32[0:HD, 0:SEQ]))
            A(act_(qhl[0][HD:P, 1, :], q32[HD:P, 0:SEQ]))
            sig(act_(khl[0], k32[:, 0:SEQ]), qk_hi, h, 0)

        def operands_v(h, first):
            if not first:
                pv_done.wait(act, h, -1)
            sig(act_(vhl[0], vt32), v_hi, h, 0)

        def exps(h, i):
            L = (i + 1) * P
            smax.wait(act, h, i)
            A(act_(Pr[:, 0, 0:L], S[:, 0:L], ACT.Exp, scale=SCALE, bias=nmax[:, 0:1], accum_out=esum[:, 0:1]))
            sig(act_(Pr[:, 1, 0:L], S[:, SEQ:SEQ + L], ACT.Exp, scale=SCALE, bias=nmax[:, 1:2], accum_out=esum[:, 1:2]), exp_done, h, i)

        def groups(h, i, part):
            p = i // 2
            at = p * (p + 1) // 2
            for g in (range(min(p + 1, 2)) if part == 0 else range(2, p + 1)):
                n = at + g
                t_ready.wait(act, h, n)
                if n >= 2:
                    pv_done.wait(act, h, n - 2)
                sig(act_(wt[n % 2][0], TB[n % 2][:, :].rearrange("p (a b) -> p a b", a=2)), wt_hi, h, n)
            if part == 0:
                return
            pv_done.wait(act, h, at + p)
            sig(act_(O32[:, 256 * p:256 * p + 256], OB[:, 0:256]), o_copied, h, p)

        def step(h, nxt, first):
            if nxt:
                split(h + 1, 0)
            exps(h, 0)
            for i in range(8):
                if nxt:
                    if i == 1:
                        split(h + 1, 1)
                    if i == 6:
                        split(h + 1, 3)
                    take(h + 1, i)
                if i == 7:
                    osT_ready.wait(act, h, 0)
                    sig(act_(O32[:, SEQ:T], TB[0][:, 0:NS]), osT_copied, h, 0)
                    if nxt:
                        take(h + 1, 8)
                    groups(h, 7, 0)
                if i == 2:
                    qbc_ready.wait(act, h, 0)
                if i % 2 == 0 and i:
                    groups(h, i - 1, 1)
                if i < 7:
                    if i % 2:
                        groups(h, i, 0)
                    exps(h, i + 1)
                if i == 2:
                    smx_done.wait(act, h, 0)
                    sT_ready.wait(act, h, 0)
                    sig(act_(ps32[0:16, 0:PAST + 1], TB[1][0:16, 0:PAST + 1], ACT.Exp, scale=SCALE, bias=snm[0:16, :], accum_out=sss[0:16, :]), sexp_done, h, 0)
                if i == 3 and nxt:
                    split(h + 1, 2)
                if i == 6:
                    os_ready.wait(act, h, 0)
                    sig(act_(os32[0:NS, :], TB[0][0:NS, 0:P]), os_copied, h, 0)
            groups(h, 7, 1)
            comb.wait(act, h, 7)
            sig(act_(sq, O32, ACT.Square), sq_done, h, 0)
            if nxt:
                rows(h + 1, 0)
                rows(h + 1, 1)
            for s in range(3):
                ms_ready.wait(act, h, s)
                t_ready.wait(act, h, 9)
                sig(act_(rst[:, s * PIECE:(s + 1) * PIECE], Sb[s][:, 0:PIECE], ACT.Ln, scale=1.0 / P, bias=const("eps")), ln_done, h, s)
            sig(act_(rst, rst, ACT.Exp, scale=-0.5), rst_done, h, 0)
            if nxt:
                merged.wait(act, h, 0)
                take(h + 1, 9)
                rows(h + 1, 2)
                rows(h + 1, 3)
                split(h + 1, 4)
                take(h + 1, 10)
                rows(h + 1, 4)
                operands_v(h + 1, False)
                take(h + 1, 11)
                operands_qk(h + 1, False)
            merged.wait(act, h, 1)
            act.dma_start(mg_d[bass.ds(h, 1), :, :].rearrange("a p n -> (a p) n"), poolc).then_inc(mg_st, 16)
            if nxt:
                for n in range(12, 15):
                    take(h + 1, n)

        split(0, 0)
        split(0, 1)
        for n in range(15):
            take(0, n, True)
            if n % 3 == 2 and n < 11:
                split(0, n // 3 + 2)
            if 9 <= n < 14:
                rows(0, n - 9, True)
        act.wait_ge(qzero, 4)
        operands_qk(0, True)
        operands_v(0, True)
        n_a = A.n
        step(0, True, True)
        with A.loop(1, H - 1, A.n - n_a) as h:
            step(h, True, False)
        step(H - 1, False, False)
        act.wait_ge(kout_st, 16 * H)
        act.wait_ge(vout_st, 16 * H)
        act.wait_ge(kvs_st, 32 * H)
        stage_end(act, 2)

        def tile3(n, b, rows, landed):
            act.wait_ge(m_landed[b], landed)
            if not (isinstance(n, int) and n < 2):
                act.wait_ge(wout_ready, n - 1)
            act_(mhl[b][0][:, :, 0:rows], mt32[b][:, :, 0:rows]).then_inc(m_hi, 1)

        def deviation(n, b, rows):
            act.wait_ge(var_done, n + 1)
            act_(rstd1[0:rows, :], mv[0:rows, 1:2], ACT.Sqrt, bias=const("eps")[0:rows, :]).then_inc(std_done, 1)
            act.wait_ge(x1_ready, n + 1)
            act.dma_start(x1_d[bass.ds(n * P, rows), :], x1t[b][0:rows, :]).then_inc(x1_st[b], 16)

        def columns(n, b, rows):
            act.wait_ge(h2_done, n + 1)
            act.dma_start(h2_d[bass.ds(n * P, rows), :], h2t[b][0:rows, :]).then_inc(h2_st[b], 16)
            act.wait_ge(h2T_ready, n + 1)
            if not (isinstance(n, int) and n == 0):
                act.wait_ge(rl_ready, n)
            A(act_(h2T[:, 0:4, 0:rows], TB[0][:, :].rearrange("p (a b) -> p a b", a=4)[:, :, 0:rows]))
            act_(h2T[:, 4:8, 0:rows], TB[1][:, :].rearrange("p (a b) -> p a b", a=4)[:, :, 0:rows]).then_inc(h2T_copied, 1)

        for k in range(KC):
            if k in (2, 4):
                tile3(k // 2 - 1, k // 2 - 1, P, 16)
            act.wait_ge(wo_landed[k % 4], WO[k % 4] + 16 * (k // 4 + 1))
            act_(wo[0][:, k, :], wo32[:, k % 4, :]).then_inc(wo_hi, 1)
        deviation(0, 0, P)
        tile3(2, 0, P, 32)
        deviation(1, 1, P)
        with A.loop(1, NT // 2 - 1, 2) as i:
            for b in range(2):
                tile3(i * 2 + (b + 1), 1 - b, P, i * 16 + 16 * (1 + b))
                columns(i * 2 + (b - 2), b, P)
                deviation(i * 2 + b, b, P)
        tile3(NT - 1, 1, P, 16 * 4)
        columns(NT - 4, 0, P)
        deviation(NT - 2, 0, P)
        tile3(NT, 0, NS, 16 * 5)
        columns(NT - 3, 1, P)
        deviation(NT - 1, 1, P)
        columns(NT - 2, 0, P)
        deviation(NT, 0, NS)
        columns(NT - 1, 1, P)
        columns(NT, 0, NS)
        act.wait_ge(route_exp, 1)
        act_(rt36[0], rt36[1], ACT.Exp).then_inc(route_exp_done, 1)
        act.wait_ge(route_exp, 2)
        act_(r9[2], r9[3], ACT.Exp).then_inc(route_exp_done, 1)
        act.wait_ge(route_exp_done, 2)
        act.wait_ge(h2T_copied, 9)
        stage_end(act, 3)

        def indices(b, i):
            act.dma_start(idx[b][:, :], tok_d[bass.ds((i + b * HALF) * P, P), :]).then_inc(idx_landed[b], 16)

        def gate_up_hi(n, b, landed):
            act.wait_ge(e_landed[b], landed)
            for q in range(2):
                k = slice(4 * q, 4 * q + 4)
                act_(gu[b][0][:, k, 0:FF], raw_g[b][:, k, :]).then_inc(g_hi, 1)
                act_(gu[b][0][:, k, FF:2 * FF], raw_u[b][:, k, :]).then_inc(g_hi, 1)

        def silu4(n, b, later):
            act.wait_ge(gu_used, n + 1)
            if later:
                act.wait_ge(av_done, n)
            act_(silu, Sb[b][:, 0:FF], ACT.Silu).then_inc(silu_ok, 1)

        def rows_out(n, b, i, st):
            act.wait_ge(dn_used, n + 1)
            if st is not None:
                act.wait_ge(y_st[b], st)
            act_(yv[b], S[:, 1024:2048]).then_inc(y_copied, 1)
            act.wait_ge(y_copied, n + 1)
            act.dma_start(y_d[bass.ds((i + b * HALF) * P, P), :], yv[b]).then_inc(y_st[b], 16)

        def act_hi(n, later):
            act.wait_ge(avT_ready, n + 1)
            if later:
                act.wait_ge(dn_used, n)
            act_(aT[0], PB[:, 0:FF].rearrange("p (a b) -> p a b", a=2)).then_inc(avT_hi, 1)

        def rows_hi(n, b):
            for q in range(2):
                act.wait_ge(xgT_ready, n * 2 + (q + 1))
                act_(hg[b][0][:, 4 * q:4 * q + 4, :], TB[q][:, :].rearrange("p (a b) -> p a b", a=4)).then_inc(hg_hi, 1)

        def down_hi(n, b, landed, later):
            act.wait_ge(d_landed[b], landed)
            if later:
                act.wait_ge(dn_used, n - 1)
            for c in range(2):
                act_(dn[b][0][:, c, :], raw_d[b][:, c, :]).then_inc(dn_hi, 1)

        def tile4(n, b, i, before, more=True, ahead=True):
            if more:
                rows_hi(n + 1, 1 - b)
            if ahead:
                indices(1 - b, i + (1 + b))
            if before >= 1:
                act_hi(n - 1, before >= 2)
            if before >= 2:
                rows_out(n - 2, b, i - 1, i * 16)
            if more:
                gate_up_hi(n + 1, 1 - b, i * 32 + 32 * (1 + b))
            silu4(n, b, before >= 1)
            down_hi(n, b, i * 16 + 16, before >= 2)

        for b in range(2):
            act.sem_inc(y_st[b], 16)
        gate_up_hi(0, 0, 32)
        act.wait_ge(tok_st, 16 * 2 * (NT + 1))
        indices(0, 0)
        indices(1, 0)
        rows_hi(0, 0)
        indices(0, 1)
        tile4(0, 0, 0, 0)
        tile4(1, 1, 0, 1)
        with act.Fori(1, HALF - 2) as i:
            for b in range(2):
                tile4(i * 2 + b, b, i, 2)
        tile4(SLOT_TILES - 4, 0, HALF - 2, 2)
        tile4(SLOT_TILES - 3, 1, HALF - 2, 2, ahead=False)
        tile4(SLOT_TILES - 2, 0, HALF - 1, 2, ahead=False)
        tile4(SLOT_TILES - 1, 1, HALF - 1, 2, more=False, ahead=False)
        act_hi(SLOT_TILES - 1, True)
        rows_out(SLOT_TILES - 2, 0, HALF - 1, 16 * HALF)
        rows_out(SLOT_TILES - 1, 1, HALF - 1, 16 * HALF)
        stage_end(act, 4)

        def store5(t):
            act.wait_ge(out_ready, t + 1)
            act.dma_start(y_p[t * P:(t + 1) * P, :] if t < NT else y_s, o5[t % 2][0:P if t < NT else NS, :]).then_inc(out_st[t % 2], 16)

        for t in range(NT + 1):
            rows = P if t < NT else NS
            act.wait_ge(y5_landed[t % 3], Y5[t % 3] + 32 * (t // 3 + 1))
            act_(ya[t % 3][0:rows, :], ya[t % 3][0:rows, :], ACT.Copy, scale=w1c[0:rows, t:t + 1]).then_inc(scaled5, 1)
            act.wait_ge(var_done, NT + 1 + t + 1)
            act_(rstd1[0:rows, :], mv[0:rows, 1:2], ACT.Sqrt, bias=const("eps")[0:rows, :]).then_inc(std_done, 1)
            if t:
                store5(t - 1)
        store5(NT)

    @block.vector
    def _(dve):
        V = Chain(dve, v_chain)
        TT, TS, STT = nc.vector.tensor_tensor, nc.vector.tensor_scalar, nc.vector.scalar_tensor_tensor

        def sig(ins, event, h, k):
            ins.then_inc(event.sem, 1)
            event.wait(dve, h, k)

        def mark(ins, semaphore, value):
            ins.then_inc(semaphore, 1)
            dve.wait_ge(semaphore, value)

        def rsum(out, in_):
            return nc.vector.tensor_reduce(out, in_, AX.X, ALU.add)

        def rmax(out, in_):
            return nc.vector.tensor_reduce(out, in_, AX.X, ALU.max)

        dve.wait_ge(ld_c, 48)
        V(nc.vector.tensor_copy(maskb[:, :], const("mask")))
        V(nc.vector.tensor_copy(identb[:, :], ident))
        V(nc.vector.tensor_copy(trib[:, :], const("tri")))
        V(nc.vector.tensor_copy(onesb[:, :], ones))
        dve.wait_ge(cT_done, 1)
        nc.vector.tensor_copy(sTc, TB[0][:, 0:72].rearrange("p (a b) -> p a b", a=8)).then_inc(cT_copied, 1)

        def h_part(m):
            dve.wait_ge(xT_done, m + 1)
            if m >= 2:
                dve.wait_ge(h_lo, m - 1)
            mark(TS(h32[m % 2], TB[m % 2][:, :], modT[:, 8 + m // 2, 0:1], modT[:, m // 2, 0:1], ALU.mult, ALU.add), h_full, m + 1)

        for n in range(NADA):
            dve.wait_ge(ada_done, n + 1)
            if n >= 3:
                dve.wait_ge(ada_st[n % 3], 16 * (n // 3))
            mark(TT(modrow[n % 3][0:9, 0:AW], Sb[n % 4][0:9, 0:AW], badab[n % 3][0:9, 0:AW], ALU.add), ada_row, n + 1)
            if 1 <= n <= 8:
                dve.wait_ge(modT_done, n)
                mark(nc.vector.tensor_copy(modT[:, 2 * n - 2:2 * n, :], OB[:, 0:18].rearrange("p (a b) -> p a b", a=2)),
                     modT_copied, n)
            if n == 8:
                mark(TS(modT[:, 8:16, :], modT[:, 8:16, :], 1.0, None, ALU.add), modT_copied, 9)
            if n >= 9:
                h_part(n - 9)
        h_part(15)
        dve.wait_ge(xT_done, 17)
        V(TT(hs32, OB[:, 0:64].rearrange("p (k b) -> p k b", k=8), modT[:, 8:16, 1:9], ALU.mult))
        mark(TT(hs32, hs32, modT[:, 0:8, 1:9], ALU.add), hs_ready, 1)
        dve.wait_ge(h_hi, 17)
        V(TT(hT[1][:, :, SEQ:T], hs32, hT[0][:, :, SEQ:T].bitcast(F32), ALU.subtract))
        dve.wait_ge(ld_small, 16 * 8)
        V(TT(lamv[:, 0, :], lamv[:, 0, :], lamv[:, 1, :], ALU.mult))
        V(TT(lamv[:, 1, :], lamv[:, 2, :], lamv[:, 3, :], ALU.mult))
        mark(rsum(lamt[:, 2:4], lamv[:, 0:2, :]), lam_sum, 1)
        dve.wait_ge(lam_exp, 1)
        V(TT(neglam, lamt[:, 1:2], lamt[:, 0:1], ALU.subtract))
        V(TS(neglam, neglam, LAM_INIT, None, ALU.subtract))
        V(TT(coef, const("coef_b"), neglam, ALU.mult))
        V(TT(coef, coef, const("coef_a"), ALU.add))
        V(TS(sublng, sublng, 1.0 - LAM_INIT, None, ALU.mult))
        stage_end(dve, 0)

        V(nc.vector.memset(ubuf[0][:, 0:16], 0.0))
        V(nc.vector.memset(ubuf[1][:, 0:16], 0.0))
        V(nc.vector.memset(sA[:, 0:16], 0.0))
        V(nc.vector.memset(sB[:, 0:16], 0.0))
        dve.wait_ge(stT_ready, 1)
        mark(nc.vector.tensor_copy(stall, TB[0][:, 0:480].rearrange("p (g n) -> p g n", g=4)), stT_copied, 1)
        for g, win in enumerate(WIN):
            ub = ubuf[g % 2]
            piece_copied.wait_first(dve, 3 * g + 2)
            cur = ub
            for l in range(g + 1):
                w, dst = 1 << l, (sA, sB)[l % 2]
                V(TT(dst[:, 16:16 + SEQ], cur[:, 16:16 + SEQ], cur[:, 16 - w:16 - w + SEQ], ALU.add))
                cur = dst
            V(TT(cur[:, 16:32], cur[:, 16:32], const("corr")[:, 16 * g:16 * g + 16], ALU.mult))
            V(STT(out=pooled[:, 0:SEQ], in0=cur[:, 16:16 + SEQ], scalar=1.0 / win, in1=ub[:, 16:16 + SEQ], op0=ALU.mult, op1=ALU.subtract))
            V(rsum(ssum, stall[:, g, :].rearrange("p (b r) -> p b r", b=NS)[:, :, 16 - win:BUF]))
            us = ub[:, 16 + SEQ:16 + T]
            V(TT(ssum, ssum, us, ALU.add))
            mark(STT(out=pooled[:, SEQ:T], in0=ssum, scalar=1.0 / win, in1=us, op0=ALU.mult, op1=ALU.subtract), pooled_done, g + 1)
            dve.wait_ge(pl_hi, 2 * g + 1)
            mark(TT(wpr[1], wp32[:, g, :], wpr[0].bitcast(F32), ALU.subtract), pool_split, 2 * g + 1)
            dve.wait_ge(pl_hi, 2 * g + 2)
            mark(TT(plr[1], pooled, plr[0].bitcast(F32), ALU.subtract), pool_split, 2 * g + 2)
        stage_end(dve, 1)

        def rope(h, n):
            cols = slice((n % 3) * PIECE, (n % 3 + 1) * PIECE)
            dst = (q32, k32)[n // 3][:, cols]
            swap_done.wait(dve, h, n)
            V(TT(dst, dst, cosT[:, cols], ALU.mult))
            V(TT(swp, swp, sinT[:, cols], ALU.mult))
            sig(TT(dst, dst, swp, ALU.add), piece_rope, h, n)

        def operands_qk(h):
            qk_hi.wait(dve, h, 0)
            V(TT(qhl[1][0:HD, 0, :], q32[0:HD, 0:SEQ], qhl[0][0:HD, 0, :].bitcast(F32), ALU.subtract))
            V(TT(qhl[1][HD:P, 1, :], q32[HD:P, 0:SEQ], qhl[0][HD:P, 1, :].bitcast(F32), ALU.subtract))
            sig(TT(khl[1], k32[:, 0:SEQ], khl[0].bitcast(F32), ALU.subtract), qk_lo, h, 0)

        def operands_v(h):
            v_hi.wait(dve, h, 0)
            sig(TT(vhl[1], vt32, vhl[0].bitcast(F32), ALU.subtract), v_lo, h, 0)

        def sample_queries(h):
            V(nc.vector.tensor_copy(qs, q32[:, SEQ:T]))
            V(nc.vector.tensor_copy(ks, k32[:, SEQ:T]))
            sig(TT(Bd, ident.rearrange("p (o f) -> p o f", o=1).to_broadcast([P, 8, P]),
                   qs.rearrange("p (b o) -> p b o", o=1).to_broadcast([P, 8, P]), ALU.mult), bd_done, h, 0)

        def maxima(h, i):
            L = (i + 1) * P
            s_ready.wait(dve, h, i)
            V(rmax(nmax, S[:, :].rearrange("p (m n) -> p m n", m=2)[:, :, 0:L]))
            sig(TS(nmax, nmax, -SCALE, None, ALU.mult), smax, h, i)

        def combine(h, i):
            L = (i + 1) * P
            exp_done.wait(dve, h, i)
            V(nc.vector.reciprocal(resum, esum))
            V(TT(resum[:, 1:2], resum[:, 1:2], neglam, ALU.mult))
            if i % 2 == 0:
                p = i // 2
                if p:
                    t_ready.wait(dve, h, p * (p + 1) // 2 - 1)
                V(nc.vector.memset(Wt[:, 0, L:L + P], 0.0))
            w = Wt[:, i % 2, 0:L]
            V(TS(w, Pr[:, 0, 0:L], resum[:, 0:1], None, ALU.mult))
            sig(STT(out=w, in0=Pr[:, 1, 0:L], scalar=resum[:, 1:2], in1=w, op0=ALU.mult, op1=ALU.add), comb, h, i)

        def groups(h, i, part):
            p = i // 2
            at = p * (p + 1) // 2
            for g in (range(min(p + 1, 2)) if part == 0 else range(2, p + 1)):
                n = at + g
                wt_hi.wait(dve, h, n)
                sig(TT(wt[n % 2][1], TB[n % 2][:, :].rearrange("p (a b) -> p a b", a=2), wt[n % 2][0].bitcast(F32), ALU.subtract), wt_lo, h, n)

        def page_products(h):
            qbc_ready.wait(dve, h, 0)
            dve.wait_ge(k_landed, (h + 1) * 256)
            for q in range(2):
                kv = KV[:, 8 * q:8 * q + 8, :].rearrange("p (b j) f -> p b j f", j=2)
                qb = TB[q][:, :].rearrange("p (b o f) -> p b o f", b=4, o=1).to_broadcast([P, 4, 2, P])
                sig(TT(kv, kv, qb, ALU.mult), qbc_used, h, q)

        def page_scores(h):
            for j in range(PAGES):
                V(rsum(sT[:, j, :].rearrange("p (b m) -> p b m", m=2),
                       KV.rearrange("p (b j) (m d) -> p b j m d", j=2, m=2)[:, :, j]))
            V(TT(qs, qs, ks, ALU.mult))
            sig(TT(sE, qs.rearrange("p (b o) -> p b o", o=1).to_broadcast([P, 8, 2]),
                   const("half").rearrange("p (o m) -> p o m", o=1).to_broadcast([P, 8, 2]), ALU.mult), sT_done, h, 0)

        def page_max(h):
            sT_ready.wait(dve, h, 0)
            V(rmax(snm[0:16, :], TB[1][0:16, 0:PAST + 1]))
            sig(TS(snm[0:16, :], snm[0:16, :], -SCALE, None, ALU.mult), smx_done, h, 0)

        def page_weights(h):
            sexp_done.wait(dve, h, 0)
            V(nc.vector.reciprocal(srs[0:16, :], sss[0:16, :]))
            V(TT(srs[0:16, :], srs[0:16, :], coef[0:16, :], ALU.mult))
            sig(TS(ps32[0:16, 0:PAST + 1], ps32[0:16, 0:PAST + 1], srs[0:16, :], None, ALU.mult), pn_done, h, 0)

        def page_columns(h):
            pnT_ready.wait(dve, h, 0)
            V(rsum(wsum.rearrange("p j b -> p (j b)"), TB[1][:, 0:32].rearrange("p (n m) -> p n m", m=2)))
            V(TT(W8.rearrange("p (b j) c -> p b j c", j=2),
                 const("delta").rearrange("p (b o c) -> p b o c", b=8, o=1).to_broadcast([P, 8, 2, 8]),
                 wsum.rearrange("p j (b o) -> p b j o", o=1).to_broadcast([P, 8, 2, 8]), ALU.mult))
            sig(TS(dgw[0:NS, :], ident[0:NS, 0:NS], TB[1][0:NS, 32:33], None, ALU.mult), w8_done, h, 0)

        def merge_gates(h):
            sq_done.wait(dve, h, 0)
            osT_copied.wait(dve, h, 0)
            piece_copied.wait(dve, h, 8)
            dve.wait_ge(poolc_landed, (h + 1) * 16)
            V(STT(out=O32, in0=O32, scalar=sublng, in1=gate[1], op0=ALU.mult, op1=ALU.mult))
            sig(TT(poolc, poolc, gate[0], ALU.mult), merged, h, 0)

        def merge(h):
            rst_done.wait(dve, h, 0)
            V(TT(O32, O32, rst, ALU.mult))
            sig(TT(poolc, poolc, O32, ALU.add), merged, h, 1)

        def step(h, nxt):
            maxima(h, 0)
            for i in range(8):
                if i % 2 == 0 and i:
                    groups(h, i - 1, 1)
                combine(h, i)
                if i == 7:
                    groups(h, 7, 0)
                if i < 6 and nxt:
                    rope(h + 1, i)
                if i < 7:
                    maxima(h, i + 1)
                    if i % 2:
                        groups(h, i, 0)
                if i == 0:
                    page_products(h)
                if i == 1:
                    page_scores(h)
                if i == 2:
                    page_max(h)
                if i == 3:
                    page_weights(h)
                if i == 4:
                    page_columns(h)
            groups(h, 7, 1)
            merge_gates(h)
            merge(h)
            if nxt:
                operands_v(h + 1)
                sample_queries(h + 1)
                operands_qk(h + 1)

        for q in range(2):
            nc.vector.memset(qhl[q][HD:P, 0, :].bitcast(F32), 0.0).then_inc(qzero, 1)
            nc.vector.memset(qhl[q][0:HD, 1, :].bitcast(F32), 0.0).then_inc(qzero, 1)
        dve.wait_ge(qzero, 4)
        for n in range(6):
            rope(0, n)
        operands_qk(0)
        operands_v(0)
        sample_queries(0)
        n_v = V.n
        step(0, True)
        with V.loop(1, H - 1, V.n - n_v) as h:
            step(h, True)
        step(H - 1, False)
        stage_end(dve, 2)

        for k in range(KC):
            dve.wait_ge(wo_hi, k + 1)
            mark(TT(wo[1][:, k, :], wo32[:, k % 4, :], wo[0][:, k, :].bitcast(F32), ALU.subtract), wo_lo, k + 1)
        dve.wait_ge(tab_landed, 16 * 9)
        V(TS(g1b, g1b, 1.0, None, ALU.add))
        V(TS(sc2b, sc2b, 1.0, None, ALU.add))
        V(nc.vector.memset(rlv, 0.0))
        dve.sem_inc(rl_used, 1)

        def normalise(y, rows, n, gain):
            for q in range(2):
                V(nc.vector.bn_stats(stat[0:rows, q, :], y[0:rows, 512 * q:512 * q + 512]))
            apart(dve)
            mark(nc.vector.bn_aggr(mv[0:rows, :], stat[0:rows, :, :].rearrange("p a b -> p (a b)")), var_done, n + 1)
            dve.wait_ge(std_done, n + 1)
            V(nc.vector.reciprocal(rstd1[0:rows, :], rstd1[0:rows, :]))
            V(TS(y[0:rows, :], y[0:rows, :], mv[0:rows, 0:1], rstd1[0:rows, :], ALU.subtract, ALU.mult))
            return TT(y[0:rows, :], y[0:rows, :], gain[0:rows, :], ALU.mult)

        def norm3(n, b, rows, before):
            dve.wait_ge(wout_ready, n + 1)
            mark(TT(y3[0:rows, :], S[0:rows, 1024 * b:1024 * b + 1024], g1b[0:rows, :], ALU.mult), wout_used, n + 1)
            dve.wait_ge(x3_landed[b], before * 16 + (X3 + 16))
            V(STT(out=y3[0:rows, :], in0=x3[b][0:rows, :], scalar=ALPHA, in1=y3[0:rows, :], op0=ALU.mult, op1=ALU.add))
            V(normalise(y3, rows, n, l1g))
            if not (isinstance(n, int) and n < 2):
                dve.wait_ge(x1_st[b], before * 16)
                dve.wait_ge(h2_done, n - 1)
            mark(TT(x1t[b][0:rows, :], y3[0:rows, :], l1b[0:rows, :], ALU.add), x1_ready, n + 1)

        def logits(n, rows):
            dve.wait_ge(rl_ready, n + 1)
            mark(TT(rlv[0:rows, bass.ds(n, 1), :].rearrange("p a n -> p (a n)"), PB[0:rows, 0:20], brg[0:rows, :], ALU.add), rl_used, n + 2)

        norm3(0, 0, P, 0)
        norm3(1, 1, P, 0)
        norm3(2, 0, P, 1)
        norm3(3, 1, P, 1)
        logits(0, P)
        with V.loop(2, NT // 2, 2 * 6) as i:
            for b in range(2):
                norm3(i * 2 + b, b, P, i)
                logits(i * 2 + (b - 3), P)
        dve.wait_ge(tab_landed, 16 * 12)
        V(TS(g1b[0:NS, :], g1b[0:NS, :], 1.0, None, ALU.add))
        V(TS(sc2b[0:NS, :], sc2b[0:NS, :], 1.0, None, ALU.add))
        norm3(NT, 0, NS, 4)
        for n in range(NT - 3, NT + 1):
            logits(n, P if n < NT else NS)

        def bc(a, n):
            return a.rearrange("p (t o) -> p t o", o=1).to_broadcast([P, 9, n])

        dec = const("dec").rearrange("p (o n) -> p o n", o=1).to_broadcast([P, 9, 4])

        def first_max(values, m, scratch, hot):
            V(rmax(m, values))
            V(TT(scratch, values, bc(m, 4), ALU.is_equal))
            V(TT(scratch, scratch, dec, ALU.mult))
            V(rmax(r9[1], scratch))
            V(TT(hot, scratch, bc(r9[1], 4), ALU.is_equal))

        gl = rlv[:, :, 0:4]
        first_max(gl, r9[0], rt36[0], oh_g)
        mark(TT(rt36[1], gl, bc(r9[0], 4), ALU.subtract), route_exp, 1)
        hg44 = oh_g.rearrange("p t (g o) -> p t g o", o=1).to_broadcast([P, 9, 4, 4])
        M14 = M1.rearrange("p t (g e) -> p t g e", g=4)
        M24 = M2.rearrange("p t (g e) -> p t g e", g=4)
        V(TT(M14, rlv[:, :, 4:20].rearrange("p t (g e) -> p t g e", g=4), hg44, ALU.mult))
        V(rsum(esel, M1.rearrange("p t (g e) -> p t e g", g=4)))
        first_max(esel, r9[2], oh2, oh1)
        V(STT(out=esel, in0=oh1, scalar=-BIG, in1=esel, op0=ALU.mult, op1=ALU.add))
        first_max(esel, r9[3], slotf[:, :, 0:4], oh2)
        mark(TT(r9[3], r9[3], r9[2], ALU.subtract), route_exp, 2)
        for M, oh in ((M14, oh1), (M24, oh2)):
            V(TT(M, hg44, oh.rearrange("p t (o e) -> p t o e", o=1).to_broadcast([P, 9, 4, 4]), ALU.mult))
        V(TT(M12, M1, M2, ALU.add))
        mark(TT(Mb[:, :].rearrange("p (t e) -> p t e", t=9), M12, bc(const("valid"), 16), ALU.mult), m_mask, 1)
        dve.wait_ge(route_exp_done, 2)
        V(rsum(r9[0], rt36[0]))
        V(TS(r9[3], r9[2], 1.0, None, ALU.add))
        V(TT(r9[0], r9[0], r9[3], ALU.mult))
        V(nc.vector.reciprocal(w1c[:, :], r9[0]))
        V(TT(w2c[:, :], w1c[:, :], r9[2], ALU.mult))
        V(nc.vector.memset(pref[:, 0, :], 0.0))
        V(nc.vector.memset(base[:, 0:1], 0.0))
        dve.wait_ge(pos_ready, 1)
        for t in range(9):
            V(TT(pref[:, t + 1, :], pref[:, t, :], TB[1][:, 16 * t:16 * t + 16], ALU.add))
        V(TS(cnti[:, :], pref[:, 9, :], float(P - 1), None, ALU.add))
        V(TS(cnti[:, :], cnti[:, :], 7, 7, ALU.arith_shift_right, ALU.logical_shift_left))
        sums = [cnt, tef[:, 0, :]]
        V(nc.vector.tensor_copy(sums[0], cnti[:, :]))
        for l in range(4):
            w, a, o = 1 << l, sums[l % 2], sums[(l + 1) % 2] if l < 3 else base[:, 1:NE + 1]
            V(nc.vector.tensor_copy(o[:, 0:w], a[:, 0:w]))
            V(TT(o[:, w:NE], a[:, w:NE], a[:, 0:NE - w], ALU.add))
        V(TT(slotf, TB[0][:, 0:144].rearrange("p (t e) -> p t e", t=9), pref[:, 0:9, :], ALU.add))
        V(TT(slotf, slotf, base[:, 0:16].rearrange("p (o e) -> p o e", o=1).to_broadcast([P, 9, 16]), ALU.add))
        V(TT(M1, M1, slotf, ALU.mult))
        V(TT(M2, M2, slotf, ALU.mult))
        V(rsum(r9[0], M1))
        V(rsum(r9[1], M2))
        V(nc.vector.tensor_copy(slot[0][:, :], r9[0]))
        V(nc.vector.tensor_copy(slot[1][:, :], r9[1]))
        mark(nc.vector.tensor_copy(toku[:, :], const("tok")), slots_done, 1)
        V(TT(tef, base[:, 1:17].rearrange("p (o e) -> p o e", o=1).to_broadcast([P, 32, 16]),
             const("start").rearrange("p (j o) -> p j o", o=1).to_broadcast([P, 32, 16]), ALU.is_le))
        V(rsum(te32, tef))
        V(TS(te[:, :], te32[0:1, :], float(NE - 1), None, ALU.min))
        stage_end(dve, 3)

        def gate_lo(n, b):
            for q in range(2):
                k = slice(4 * q, 4 * q + 4)
                dve.wait_ge(g_hi, n * 4 + (2 * q + 1))
                TT(gu[b][1][:, k, 0:FF], raw_g[b][:, k, :], gu[b][0][:, k, 0:FF].bitcast(F32), ALU.subtract).then_inc(g_lo, 1)

        def gated(n, b, later):
            dve.wait_ge(silu_ok, n + 1)
            if later:
                dve.wait_ge(avT_ready, n)
            TT(av, silu, Sb[b][:, FF:2 * FF], ALU.mult).then_inc(av_done, 1)

        def act_lo(n):
            dve.wait_ge(avT_hi, n + 1)
            TT(aT[1], PB[:, 0:FF].rearrange("p (a b) -> p a b", a=2), aT[0].bitcast(F32), ALU.subtract).then_inc(avT_lo, 1)

        def rows_lo(n, b):
            for q in range(2):
                dve.wait_ge(hg_hi, n * 2 + (q + 1))
                TT(hg[b][1][:, 4 * q:4 * q + 4, :], TB[q][:, :].rearrange("p (a b) -> p a b", a=4),
                   hg[b][0][:, 4 * q:4 * q + 4, :].bitcast(F32), ALU.subtract).then_inc(hg_lo, 1)

        def down_lo(n, b):
            for c in range(2):
                dve.wait_ge(dn_hi, n * 2 + (c + 1))
                TT(dn[b][1][:, c, :], raw_d[b][:, c, :], dn[b][0][:, c, :].bitcast(F32), ALU.subtract).then_inc(dn_lo, 1)

        def tile4(n, b, before, more=True):
            if more:
                rows_lo(n + 1, 1 - b)
            if before >= 1:
                act_lo(n - 1)
            if more:
                gate_lo(n + 1, 1 - b)
            gated(n, b, before >= 1)
            down_lo(n, b)

        gate_lo(0, 0)
        rows_lo(0, 0)
        tile4(0, 0, 0)
        tile4(1, 1, 1)
        with dve.Fori(1, SLOT_TILES // 2 - 1) as i:
            for b in range(2):
                tile4(i * 2 + b, b, 2)
        tile4(SLOT_TILES - 2, 0, 2)
        tile4(SLOT_TILES - 1, 1, 2, more=False)
        act_lo(SLOT_TILES - 1)
        stage_end(dve, 4)

        dve.wait_ge(tab5, 48)
        V(TS(g2b, g2b, 1.0, None, ALU.add))
        for t in range(NT + 1):
            b, rows = t % 2, P if t < NT else NS
            if t == NT:
                dve.wait_ge(tab5, 64)
                V(TS(g2b[0:NS, :], g2b[0:NS, :], 1.0, None, ALU.add))
            dve.wait_ge(y5_landed[t % 3], Y5[t % 3] + 32 * (t // 3 + 1))
            dve.wait_ge(scaled5, SC5 + t + 1)
            if t >= 2:
                dve.wait_ge(out_ready, t - 1)
            m = m5[b]
            V(STT(out=m[0:rows, :], in0=yb[t % 3][0:rows, :], scalar=w2c[0:rows, t:t + 1], in1=ya[t % 3][0:rows, :], op0=ALU.mult, op1=ALU.add))
            V(TT(m[0:rows, :], m[0:rows, :], g2b[0:rows, :], ALU.mult))
            dve.wait_ge(x5_landed[b], LD5 + 16 * (t // 2 + 1))
            mark(STT(out=m[0:rows, :], in0=x5[b][0:rows, :], scalar=ALPHA, in1=m[0:rows, :], op0=ALU.mult, op1=ALU.add), m5_used, t + 1)
            mark(normalise(m, rows, NT + 1 + t, l2g), gained5, GA5 + t + 1)

    @block.gpsimd
    def _(pool):
        for m in range(16):
            cols = slice(512 * (m % 2), 512 * (m % 2) + 512)
            pool.wait_ge(h_hi, m + 1)
            nc.gpsimd.tensor_tensor(hT[1][:, m // 2, cols], h32[m % 2], hT[0][:, m // 2, cols].bitcast(F32), ALU.subtract).then_inc(h_lo, 1)
        pool.wait_ge(h_lo, 16)
        stage_end(pool, 0)

        for g in range(4):
            pool.wait_ge(w_landed[g % 2], 16 * (g // 2 + 1))
            w_hi.wait_first(pool, g)
            nc.gpsimd.tensor_tensor(whl[g % 2][1], wraw[g % 2], whl[g % 2][0].bitcast(F32), ALU.subtract).then_inc(w_lo.sem, 1)
        w_lo.wait_first(pool, 3)
        stage_end(pool, 1)

        def split(h, c):
            pool.wait_ge(w_landed[c % 2], landed_value(h, c))
            w_hi.wait(pool, h, c)
            nc.gpsimd.tensor_tensor(whl[c % 2][1], wraw2[c % 2], whl[c % 2][0].bitcast(F32), ALU.subtract).then_inc(w_lo.sem, 1)

        for c in range(5):
            split(0, c)
        for c in range(5):
            split(1, c)
        with pool.Fori(1, H - 1) as h:
            for c in range(5):
                split(h + 1, c)
        stage_end(pool, 2)

        G = Chain(pool, p_chain)

        def m_rest(n, b, rows):
            pool.wait_ge(m_hi, n + 1)
            nc.gpsimd.tensor_tensor(mhl[b][1][:, :, 0:rows], mt32[b][:, :, 0:rows], mhl[b][0][:, :, 0:rows].bitcast(F32), ALU.subtract)\
                .then_inc(m_lo, 1)

        def second_input(n, b, rows, before):
            pool.wait_ge(x1_ready, n + 1)
            if not (isinstance(n, int) and n < 2):
                pool.wait_ge(h2_st[b], before * 16)
                pool.wait_ge(h2T_ready, n - 1)
            G(nc.gpsimd.tensor_tensor(h2t[b][0:rows, :], x1t[b][0:rows, :], sc2b[0:rows, :], ALU.mult))
            nc.gpsimd.tensor_tensor(h2t[b][0:rows, :], h2t[b][0:rows, :], sh2b[0:rows, :], ALU.add).then_inc(h2_done, 1)

        m_rest(0, 0, P)
        m_rest(1, 1, P)
        second_input(0, 0, P, 0)
        m_rest(2, 0, P)
        second_input(1, 1, P, 0)
        with G.loop(1, NT // 2 - 1, 2) as i:
            for b in range(2):
                m_rest(i * 2 + (b + 1), 1 - b, P)
                second_input(i * 2 + b, b, P, i)
        m_rest(NT - 1, 1, P)
        second_input(NT - 2, 0, P, 3)
        m_rest(NT, 0, NS)
        second_input(NT - 1, 1, P, 3)
        second_input(NT, 0, NS, 4)
        pool.wait_ge(wo_lo, KC)
        pool.wait_ge(h2T_ready, NT + 1)
        G(nc.gpsimd.memset(tokz, 0.0))
        pool.dma_start(tok_d.rearrange("(p n) o -> p (n o)", p=P), tokz.bitcast(U32)).then_inc(zero_st, 16)
        pool.wait_ge(zero_st, 16)
        pool.wait_ge(slots_done, 1)
        stage_end(pool, 3)
        for t in range(NT + 1):
            rows = P if t < NT else NS
            for c in range(2):
                nc.gpsimd.indirect_dma_start(
                    out=tok_d, out_offset=bass.IndirectOffsetOnAxis(ap=slot[c][0:rows, t:t + 1], axis=0),
                    in_=toku[0:rows, t:t + 1], in_offset=None).then_inc(tok_st, 16)

        def gather(n, b, landed, later):
            pool.wait_ge(idx_landed[b], landed)
            if later:
                pool.wait_ge(xgT_ready, n * 2 - 2)
                apart(pool)
            nc.gpsimd.indirect_dma_start(
                out=xg[b], out_offset=None, in_=h2_d,
                in_offset=bass.IndirectOffsetOnAxis(ap=idx[b][:, 0:1], axis=0)).then_inc(xg_landed[b], 16)

        def up_lo(n, b):
            for q in range(2):
                k = slice(4 * q, 4 * q + 4)
                pool.wait_ge(g_hi, n * 4 + (2 * q + 2))
                nc.gpsimd.tensor_tensor(gu[b][1][:, k, FF:2 * FF], raw_u[b][:, k, :], gu[b][0][:, k, FF:2 * FF].bitcast(F32), ALU.subtract)\
                    .then_inc(u_lo, 1)

        gather(0, 0, 16, False)
        gather(1, 1, 16, False)
        gather(2, 0, 32, True)
        up_lo(0, 0)
        gather(3, 1, 32, True)
        up_lo(1, 1)
        with pool.Fori(1, HALF - 1) as i:
            for b in range(2):
                gather(i * 2 + (b + 2), b, i * 16 + 32, True)
                up_lo(i * 2 + b, b)
        up_lo(SLOT_TILES - 2, 0)
        up_lo(SLOT_TILES - 1, 1)
        stage_end(pool, 4)

        def gather5(t):
            if t >= 3:
                pool.wait_ge(m5_used, t - 2)
            for c, dst in enumerate((ya, yb)):
                nc.gpsimd.indirect_dma_start(
                    out=dst[t % 3][0:P if t < NT else NS, :], out_offset=None, in_=y_d,
                    in_offset=bass.IndirectOffsetOnAxis(ap=slot[c][0:P if t < NT else NS, t:t + 1], axis=0)).then_inc(y5_landed[t % 3], 16)

        gather5(0)
        gather5(1)
        for t in range(NT + 1):
            b, rows = t % 2, P if t < NT else NS
            if t + 2 <= NT:
                gather5(t + 2)
            pool.wait_ge(gained5, GA5 + t + 1)
            if t >= 2:
                pool.wait_ge(out_st[b], ST5 + 16 * (t // 2))
            nc.gpsimd.tensor_tensor(o5[b][0:rows, :], m5[b][0:rows, :], l2b[0:rows, :], ALU.add).then_inc(out_ready, 1)


INS = ["x_prompt", "x_sample", "cache_k", "cache_v", "state_pool", "page_table", "c_prompt", "c_sample",
       "w_ada", "b_ada", "w_in", "lambda_q1", "lambda_k1", "lambda_q2", "lambda_k2", "subln_g",
       "w_pool", "pool_scale", "w_out", "ln1_g", "ln1_b",
       "w_group", "b_group", "w_router", "b_router", "w_e_gate", "w_e_up", "w_e_down", "ln2_g", "ln2_b"]
OUTS = [(1, SEQ, D), (NS, 1, D), (1, 1, SEQ, H, 2, HD), (1, 1, SEQ, H, P), (1, 1, BUF, 512),
        (1, NS, 1, H, 2, HD), (1, NS, 1, H, P), (1, NS, BUF, 512)]


def kernel(**inputs):
    import concourse.bacc as bacc
    from concourse.bass_utils import run_bass_kernel_spmd as run

    nc = bacc.Bacc("TRN2", target_bir_lowering=False, num_devices=1)
    arrays, ins = {}, {}
    cst, rope = constants()
    for name in INS + ["cst", "rope"]:
        a = np.ascontiguousarray(cst if name == "cst" else rope if name == "rope" else inputs[name])
        arrays[f"in_{name}"] = a
        ins[name] = nc.dram_tensor(f"in_{name}", a.shape, mybir.dt.from_np(a.dtype), kind="ExternalInput").ap()
    outs = [nc.dram_tensor(f"out_{i}", shape, F32, kind="ExternalOutput").ap() for i, shape in enumerate(OUTS)]
    build(nc, ins, outs)
    r = run(nc, [arrays], core_ids=[0])
    return tuple(r.results[0][f"out_{i}"] for i in range(len(OUTS)))
```
